# Optimizing a Trainium2 kernel written in Bass

```python
import math
import jax
import jax.numpy as jnp
from jax import lax
import numpy as np

D_MODEL = 1024
BATCH = 1
SEQ = 512
DEPTH = 2
DEC_BATCH = 8
DEC_SEQ = 4
PAST_LEN = 2048
PAGE_SIZE = 128

N_EVEN = (DEPTH + 1) // 2
N_ODD = DEPTH // 2
WINDOW = 128
ATTN_HEADS = 8
KV_HEADS = 2
HEAD_DIM = 64
ATTN_WIDTH = ATTN_HEADS * HEAD_DIM
KV_WIDTH = KV_HEADS * HEAD_DIM
ROT_DIM = HEAD_DIM // 4
ROPE_THETA = 500000.0
S5_GROUP = 16
S5_WIDTH = D_MODEL // 2
S5_GROUPS = S5_WIDTH // S5_GROUP
S5_STATE = 64
EVEN_IN = ATTN_WIDTH + 2 * KV_WIDTH + S5_WIDTH
EVEN_MIX = ATTN_WIDTH + S5_WIDTH
ML_HEADS = 8
ML_DV = D_MODEL // ML_HEADS
ML_DK = ML_DV // 2
ML_CHUNK = 64
ML_QK = ML_HEADS * ML_DK
ML_WIDTH = ML_HEADS * ML_DV
ODD_IN = 2 * ML_QK + 2 * ML_WIDTH + 2 * ML_HEADS
D_FF = -(-8 * D_MODEL // (3 * 256)) * 256
EPS = 1e-6

kernel_name = 'hybrid_swa_s5_mlstm_step'

def rmsnorm(x, g):
    xf = x.astype(jnp.float32)
    y = xf * lax.rsqrt(jnp.mean(xf * xf, axis=-1, keepdims=True) + EPS)
    return (y * g.astype(jnp.float32)).astype(x.dtype)

def rope_partial(x, pos):
    half = ROT_DIM // 2
    inv = jnp.power(jnp.float32(ROPE_THETA), -jnp.arange(half, dtype=jnp.float32) / half)
    ang = pos.astype(jnp.float32)[:, None] * inv[None, :]
    cos = jnp.cos(ang)[:, None, :]
    sin = jnp.sin(ang)[:, None, :]
    xr = x[..., :ROT_DIM].astype(jnp.float32)
    x1, x2 = xr[..., :half], xr[..., half:]
    rot = jnp.concatenate([x1 * cos - x2 * sin, x2 * cos + x1 * sin], axis=-1)
    return jnp.concatenate([rot.astype(x.dtype), x[..., ROT_DIM:]], axis=-1)

def sink_attention(q, k, v, mask, sinks):
    *lead, lq, n_heads, hd = q.shape
    grp = n_heads // KV_HEADS
    qg = q.reshape(*lead, lq, KV_HEADS, grp, hd)
    s = jnp.einsum('...qhgd,...khd->...hgqk', qg, k).astype(jnp.float32) * (hd ** -0.5)
    s = jnp.where(mask, s, -jnp.inf)
    sink = sinks.astype(jnp.float32).reshape(KV_HEADS, grp, 1)
    m = jnp.maximum(jnp.max(s, axis=-1), sink)
    p = jnp.exp(s - m[..., None])
    p = p / (jnp.sum(p, axis=-1) + jnp.exp(sink - m))[..., None]
    o = jnp.einsum('...hgqk,...khd->...qhgd', p.astype(v.dtype), v)
    return o.reshape(*lead, lq, n_heads * hd)

def banded_attention(q, k, v, sinks):
    bsz, L = q.shape[:2]
    nb = L // WINDOW
    qb = q.reshape(bsz, nb, WINDOW, ATTN_HEADS, HEAD_DIM)

    def band(t):
        tb = t.reshape(bsz, nb, WINDOW, KV_HEADS, HEAD_DIM)
        prev = jnp.concatenate([jnp.zeros_like(tb[:, :1]), tb[:, :-1]], axis=1)
        return jnp.concatenate([prev, tb], axis=2)

    kb, vb = band(k), band(v)
    rel = (jnp.arange(WINDOW)[:, None] + WINDOW) - jnp.arange(2 * WINDOW)[None, :]
    in_band = (rel >= 0) & (rel <= WINDOW)
    valid = (jnp.arange(nb)[:, None] > 0) | (jnp.arange(2 * WINDOW)[None, :] >= WINDOW)
    mask = (in_band[None] & valid[:, None, :])[:, None, None]
    o = sink_attention(qb, kb, vb, mask, sinks)
    return o.reshape(bsz, L, ATTN_WIDTH)

def s5_mixer(u, a_re, a_im, log_dt, b_re, b_im, c_re, c_im, d_skip, w_glu, b_glu, h0):
    bsz, L, _ = u.shape
    uf = u.astype(jnp.float32).reshape(bsz, L, S5_GROUPS, S5_GROUP)
    dt = jnp.exp(log_dt.astype(jnp.float32))
    ar, ai = a_re.astype(jnp.float32), a_im.astype(jnp.float32)
    mag = jnp.exp(ar * dt)
    lr, li = mag * jnp.cos(ai * dt), mag * jnp.sin(ai * dt)
    den = ar * ar + ai * ai
    cr = ((lr - 1.0) * ar + li * ai) / den
    ci = (li * ar - (lr - 1.0) * ai) / den
    br, bi = b_re.astype(jnp.float32), b_im.astype(jnp.float32)
    bbr = cr[..., None] * br - ci[..., None] * bi
    bbi = cr[..., None] * bi + ci[..., None] * br
    xr = jnp.einsum('blgh,gph->blgp', uf, bbr)
    xi = jnp.einsum('blgh,gph->blgp', uf, bbi)
    if h0 is not None:
        h0r, h0i = h0[0].astype(jnp.float32), h0[1].astype(jnp.float32)
        xr = xr.at[:, 0].add(lr * h0r - li * h0i)
        xi = xi.at[:, 0].add(lr * h0i + li * h0r)

    def combine(e1, e2):
        a1r, a1i, b1r, b1i = e1
        a2r, a2i, b2r, b2i = e2
        return (a1r * a2r - a1i * a2i, a1r * a2i + a1i * a2r,
                a2r * b1r - a2i * b1i + b2r, a2r * b1i + a2i * b1r + b2i)

    _, _, sr, si = lax.associative_scan(
        combine, (jnp.broadcast_to(lr, xr.shape), jnp.broadcast_to(li, xr.shape), xr, xi), axis=1)
    y = (jnp.einsum('blgp,ghp->blgh', sr, c_re.astype(jnp.float32))
         - jnp.einsum('blgp,ghp->blgh', si, c_im.astype(jnp.float32))
         + d_skip.astype(jnp.float32) * uf).reshape(bsz, L, S5_WIDTH)
    g = jax.nn.gelu(y, approximate=False)
    out = g * jax.nn.sigmoid(g @ w_glu.astype(jnp.float32) + b_glu.astype(jnp.float32))
    return out.astype(u.dtype), sr[:, -1], si[:, -1]

def even_mixer(h, pos, kv_window, ssm0, w_in, g_q, g_k, sinks, a_re, a_im, log_dt, b_re, b_im,
               c_re, c_im, d_skip, w_glu, b_glu, w_out):
    bsz, L, _ = h.shape
    proj = h @ w_in
    q, k, v, u = jnp.split(proj, [ATTN_WIDTH, ATTN_WIDTH + KV_WIDTH, ATTN_WIDTH + 2 * KV_WIDTH], axis=-1)
    q = rope_partial(rmsnorm(q.reshape(bsz, L, ATTN_HEADS, HEAD_DIM), g_q), pos)
    k = rope_partial(rmsnorm(k.reshape(bsz, L, KV_HEADS, HEAD_DIM), g_k), pos)
    v = v.reshape(bsz, L, KV_HEADS, HEAD_DIM)
    if kv_window is None:
        attn = banded_attention(q, k, v, sinks)
        k_all, v_all = k, v
    else:
        k_all = jnp.concatenate([kv_window[0].astype(k.dtype), k], axis=1)
        v_all = jnp.concatenate([kv_window[1].astype(v.dtype), v], axis=1)
        k_pos = pos[0] - WINDOW + jnp.arange(WINDOW + L)
        rel = pos[:, None] - k_pos[None, :]
        mask = (rel >= 0) & (rel <= WINDOW)
        attn = sink_attention(q, k_all, v_all, mask, sinks)
    ssm_out, sr, si = s5_mixer(u, a_re, a_im, log_dt, b_re, b_im, c_re, c_im, d_skip, w_glu, b_glu, ssm0)
    mixed = jnp.concatenate([attn, ssm_out.astype(attn.dtype)], axis=-1)
    return mixed @ w_out, k_all[:, -WINDOW:], v_all[:, -WINDOW:], sr, si

def mlstm_chunk(carry, inp):
    c, n, m = carry
    q, k, v, ig, lf = inp
    T = q.shape[-2]
    b = lax.cumsum(lf, axis=2)
    causal = jnp.tril(jnp.ones((T, T), dtype=bool))
    dmat = jnp.where(causal, b[..., :, None] - b[..., None, :] + ig[..., None, :], -jnp.inf)
    inter = b + m[..., None]
    m_row = jnp.maximum(inter, jnp.max(dmat, axis=-1))
    w_intra = jnp.exp(dmat - m_row[..., None])
    w_inter = jnp.exp(inter - m_row)
    qk = jnp.einsum('bhtd,bhsd->bhts', q, k) * w_intra
    num = w_inter[..., None] * jnp.einsum('bhtd,bhdv->bhtv', q, c) + jnp.einsum('bhts,bhsv->bhtv', qk, v)
    den = w_inter * jnp.einsum('bhtd,bhd->bht', q, n) + jnp.sum(qk, axis=-1)
    h = num / jnp.maximum(jnp.abs(den), jnp.exp(-m_row))[..., None]
    m_new = m_row[..., -1]
    wk = w_intra[..., -1, :]
    decay = w_inter[..., -1]
    c_new = decay[..., None, None] * c + jnp.einsum('bhs,bhsd,bhsv->bhdv', wk, k, v)
    n_new = decay[..., None] * n + jnp.einsum('bhs,bhsd->bhd', wk, k)
    return (c_new, n_new, m_new), h

def mlstm(q, k, v, ig, lf, c0, n0, m0):
    bsz, L = q.shape[:2]
    lc = ML_CHUNK if L % ML_CHUNK == 0 else L
    nc = L // lc

    def to_chunks(t):
        t = t.reshape(bsz, nc, lc, *t.shape[2:])
        return jnp.swapaxes(jnp.moveaxis(t, 1, 0), 2, 3)

    (c, n, m), h = lax.scan(mlstm_chunk, (c0, n0, m0),
                            (to_chunks(q), to_chunks(k), to_chunks(v), to_chunks(ig), to_chunks(lf)))
    h = jnp.moveaxis(jnp.swapaxes(h, 2, 3), 0, 1).reshape(bsz, L, ML_HEADS, ML_DV)
    return h, c, n, m

def odd_mixer(h, state0, w_in, b_i, b_f, g_out, w_out):
    bsz, L, _ = h.shape
    proj = (h @ w_in).astype(jnp.float32)
    q, k, v, o, ig, fg = jnp.split(
        proj, [ML_QK, 2 * ML_QK, 2 * ML_QK + ML_WIDTH, 2 * ML_QK + 2 * ML_WIDTH,
               2 * ML_QK + 2 * ML_WIDTH + ML_HEADS], axis=-1)
    q = q.reshape(bsz, L, ML_HEADS, ML_DK)
    k = k.reshape(bsz, L, ML_HEADS, ML_DK) * (ML_DK ** -0.5)
    v = v.reshape(bsz, L, ML_HEADS, ML_DV)
    ig = ig + b_i.astype(jnp.float32)
    lf = jax.nn.log_sigmoid(fg + b_f.astype(jnp.float32))
    if state0 is None:
        c0 = jnp.zeros((bsz, ML_HEADS, ML_DK, ML_DV), jnp.float32)
        n0 = jnp.zeros((bsz, ML_HEADS, ML_DK), jnp.float32)
        m0 = jnp.zeros((bsz, ML_HEADS), jnp.float32)
    else:
        c0, n0, m0 = (s.astype(jnp.float32) for s in state0)
    hh, c, n, m = mlstm(q, k, v, ig, lf, c0, n0, m0)
    hh = rmsnorm(hh, g_out.reshape(ML_HEADS, ML_DV))
    out = (hh.reshape(bsz, L, ML_WIDTH) * jax.nn.sigmoid(o)).astype(h.dtype)
    return out @ w_out, c, n, m

def swiglu(h, wg, wu, wd):
    return (jax.nn.silu(h @ wg) * (h @ wu)) @ wd

def setup_inputs(seed: int = 0) -> dict:
    key = jax.random.key(seed)
    ks = iter(jax.random.split(key, 48))

    def nrm(shape, scale=1.0):
        return jax.random.normal(next(ks), shape, jnp.float32) * scale

    a_im_base = jnp.pi * jnp.arange(S5_STATE, dtype=jnp.float32)
    return {
        'x_prompt': nrm((BATCH, SEQ, D_MODEL)),
        'x_sample': nrm((DEC_BATCH, DEC_SEQ, D_MODEL)),
        'cache_k': nrm((N_EVEN, DEC_BATCH, WINDOW, KV_HEADS, HEAD_DIM)),
        'cache_v': nrm((N_EVEN, DEC_BATCH, WINDOW, KV_HEADS, HEAD_DIM)),
        'state_ssm_re': nrm((N_EVEN, DEC_BATCH, S5_GROUPS, S5_STATE), 0.1),
        'state_ssm_im': nrm((N_EVEN, DEC_BATCH, S5_GROUPS, S5_STATE), 0.1),
        'state_mlstm_c': nrm((N_ODD, DEC_BATCH, ML_HEADS, ML_DK, ML_DV), 0.1),
        'state_mlstm_n': nrm((N_ODD, DEC_BATCH, ML_HEADS, ML_DK), 0.1),
        'state_mlstm_m': nrm((N_ODD, DEC_BATCH, ML_HEADS)),
        'norm_mix': 1.0 + nrm((DEPTH, D_MODEL), 0.01),
        'norm_ffn': 1.0 + nrm((DEPTH, D_MODEL), 0.01),
        'w_in_even': nrm((N_EVEN, D_MODEL, EVEN_IN), D_MODEL ** -0.5),
        'q_norm': 1.0 + nrm((N_EVEN, HEAD_DIM), 0.01),
        'k_norm': 1.0 + nrm((N_EVEN, HEAD_DIM), 0.01),
        'attn_sinks': nrm((N_EVEN, ATTN_HEADS), 0.5),
        's5_a_re': -0.5 + nrm((N_EVEN, S5_GROUPS, S5_STATE), 0.01),
        's5_a_im': a_im_base + nrm((N_EVEN, S5_GROUPS, S5_STATE), 0.01),
        's5_log_dt': jax.random.uniform(next(ks), (N_EVEN, S5_GROUPS, S5_STATE), jnp.float32,
                                        math.log(0.001), math.log(0.1)),
        's5_b_re': nrm((N_EVEN, S5_GROUPS, S5_STATE, S5_GROUP), (2 * S5_GROUP) ** -0.5),
        's5_b_im': nrm((N_EVEN, S5_GROUPS, S5_STATE, S5_GROUP), (2 * S5_GROUP) ** -0.5),
        's5_c_re': nrm((N_EVEN, S5_GROUPS, S5_GROUP, S5_STATE), S5_STATE ** -0.5),
        's5_c_im': nrm((N_EVEN, S5_GROUPS, S5_GROUP, S5_STATE), S5_STATE ** -0.5),
        's5_d': nrm((N_EVEN, S5_GROUPS, S5_GROUP), 0.5),
        's5_w_glu': nrm((N_EVEN, S5_WIDTH, S5_WIDTH), S5_WIDTH ** -0.5),
        's5_b_glu': nrm((N_EVEN, S5_WIDTH), 0.01),
        'w_out_even': nrm((N_EVEN, EVEN_MIX, D_MODEL), EVEN_MIX ** -0.5),
        'w_in_odd': nrm((N_ODD, D_MODEL, ODD_IN), D_MODEL ** -0.5),
        'ml_b_i': nrm((N_ODD, ML_HEADS), 0.1),
        'ml_b_f': jnp.linspace(3.0, 6.0, ML_HEADS, dtype=jnp.float32)[None] + nrm((N_ODD, ML_HEADS), 0.1),
        'ml_out_norm': 1.0 + nrm((N_ODD, ML_WIDTH), 0.01),
        'w_out_odd': nrm((N_ODD, ML_WIDTH, D_MODEL), ML_WIDTH ** -0.5),
        'w_gate': nrm((DEPTH, D_MODEL, D_FF), D_MODEL ** -0.5),
        'w_up': nrm((DEPTH, D_MODEL, D_FF), D_MODEL ** -0.5),
        'w_down': nrm((DEPTH, D_FF, D_MODEL), D_FF ** -0.5),
    }

def reference(x_prompt, x_sample, cache_k, cache_v, state_ssm_re, state_ssm_im, state_mlstm_c,
              state_mlstm_n, state_mlstm_m, norm_mix, norm_ffn, w_in_even, q_norm, k_norm, attn_sinks,
              s5_a_re, s5_a_im, s5_log_dt, s5_b_re, s5_b_im, s5_c_re, s5_c_im, s5_d, s5_w_glu, s5_b_glu,
              w_out_even, w_in_odd, ml_b_i, ml_b_f, ml_out_norm, w_out_odd, w_gate, w_up, w_down):
    pos_p = jnp.arange(x_prompt.shape[1])
    pos_s = PAST_LEN + jnp.arange(x_sample.shape[1])
    yp, ys = x_prompt, x_sample
    pk, pv, psr, psi, pc, pn, pm = [], [], [], [], [], [], []
    sk, sv, ssr, ssi, sc, sn, sm = [], [], [], [], [], [], []
    for layer in range(DEPTH):
        if layer % 2 == 0:
            e = layer // 2
            w = (w_in_even[e], q_norm[e], k_norm[e], attn_sinks[e], s5_a_re[e], s5_a_im[e], s5_log_dt[e],
                 s5_b_re[e], s5_b_im[e], s5_c_re[e], s5_c_im[e], s5_d[e], s5_w_glu[e], s5_b_glu[e],
                 w_out_even[e])
            out, k_new, v_new, sr, si = even_mixer(rmsnorm(yp, norm_mix[layer]), pos_p, None, None, *w)
            yp = yp + out
            pk.append(k_new); pv.append(v_new); psr.append(sr); psi.append(si)
            out, k_new, v_new, sr, si = even_mixer(rmsnorm(ys, norm_mix[layer]), pos_s,
                                                   (cache_k[e], cache_v[e]),
                                                   (state_ssm_re[e], state_ssm_im[e]), *w)
            ys = ys + out
            sk.append(k_new); sv.append(v_new); ssr.append(sr); ssi.append(si)
        else:
            o = layer // 2
            w = (w_in_odd[o], ml_b_i[o], ml_b_f[o], ml_out_norm[o], w_out_odd[o])
            out, c, n, m = odd_mixer(rmsnorm(yp, norm_mix[layer]), None, *w)
            yp = yp + out
            pc.append(c); pn.append(n); pm.append(m)
            out, c, n, m = odd_mixer(rmsnorm(ys, norm_mix[layer]),
                                     (state_mlstm_c[o], state_mlstm_n[o], state_mlstm_m[o]), *w)
            ys = ys + out
            sc.append(c); sn.append(n); sm.append(m)
        yp = yp + swiglu(rmsnorm(yp, norm_ffn[layer]), w_gate[layer], w_up[layer], w_down[layer])
        ys = ys + swiglu(rmsnorm(ys, norm_ffn[layer]), w_gate[layer], w_up[layer], w_down[layer])
    return (yp, ys,
            jnp.stack(pk), jnp.stack(pv), jnp.stack(psr), jnp.stack(psi),
            jnp.stack(pc), jnp.stack(pn), jnp.stack(pm),
            jnp.stack(sk), jnp.stack(sv), jnp.stack(ssr), jnp.stack(ssi),
            jnp.stack(sc), jnp.stack(sn), jnp.stack(sm))


_drawn_inputs = setup_inputs


def setup_inputs(seed=0):
    import zlib

    import numpy as np

    out = dict(_drawn_inputs(seed))
    spreads = {}
    factors = {'norm_mix': 2.813,
     'norm_ffn': 4.292,
     'q_norm': 8.0,
     'k_norm': 5.617,
     'attn_sinks': 4.733,
     's5_a_re': 3.866,
     's5_b_glu': 8.0,
     'ml_out_norm': 8.0}
    for name, (base, spread) in spreads.items():
        noise = np.random.default_rng([zlib.crc32(name.encode()), seed]).standard_normal(out[name].shape)
        drawn = base * np.exp(spread * noise) if base else spread * noise
        out[name] = jnp.asarray(drawn.astype(out[name].dtype))
    for name, factor in factors.items():
        out[name] = (out[name] * factor).astype(out[name].dtype)
    return out
```

```python
from contextlib import ExitStack

import numpy as np
import concourse.bass as bass
from concourse import mybir
from concourse.alu_op_type import AluOpType as ALU

F32 = mybir.dt.float32
F32R = mybir.dt.float32r
ACT = mybir.ActivationFunctionType
AX = mybir.AxisListType

P = 128
D = 1024
DC = D // P
LP = 512
NB, NT = 8, 4
LS = NB * NT
T = LP + LS
HT = T // 2
WIN = 128
PAST = 2048
HD = 64
QH, KVH = 8, 2
QG = QH // KVH
EVEN_IN = 1280
S5G, S5H, S5P = 32, 16, 64
NPAIR = S5G // 2
SUB = 8
NSUB = LP // SUB
MH, DK, DV = 8, 64, 128
ODD_IN = 3088
FF = 2816
FC = FF // P
FH = FC // 2
EPS = 1e-6
NEG = -1e30
TINY = 1e-37
TWO_PI = 2 * np.pi
ROUND = float(1.5 * 2 ** 23)


def constant_tables():
    f = np.float32
    t = {}
    t["ident"] = np.eye(P, dtype=f)
    blk = np.zeros((P, P), f)
    blk[:HD, :HD] = 1
    blk[HD:, HD:] = 1
    t["head_ones"] = blk
    half = HD // 8
    swap = np.zeros((P, P), f)
    for h in range(2):
        for d in range(half):
            swap[h * HD + half + d, h * HD + d] = -1
            swap[h * HD + d, h * HD + half + d] = 1
    t["rope_swap"] = swap
    inv = np.power(f(500000.0), -np.arange(half, dtype=f) / f(half)).astype(f)
    pos = np.concatenate([np.arange(LP), np.tile(PAST + np.arange(NT), NB)]).astype(f)
    ang = (pos[:, None] * inv[None, :]).astype(f)
    c = np.ones((P, T), f)
    s = np.zeros((P, T), f)
    for h in range(2):
        for part in range(2):
            at = h * HD + part * half
            c[at:at + half] = np.cos(ang).T
            s[at:at + half] = np.sin(ang).T
    t["rope_cos"], t["rope_sin"] = c, s
    q = np.arange(P)[:, None]
    j = np.arange(2 * P)[None, :]
    t["band"] = np.where((j >= q) & (j <= q + WIN), 0, NEG).astype(f)
    qb = (np.arange(P) % LS // NT)[:, None]
    qt = (np.arange(P) % NT)[:, None]
    old = np.arange(NB * WIN)[None, :]
    new = np.arange(LS)[None, :]
    m_old = (old // WIN == qb) & (old % WIN >= qt)
    m_new = (new // NT == qb) & (new % NT <= qt)
    t["sample_band"] = np.where(np.concatenate([m_old, m_new], 1), 0, NEG).astype(f)
    tt = np.arange(P)
    t["causal"] = np.where(tt[:, None] <= tt[None, :], 0, NEG).astype(f)
    st = np.arange(LS)
    same = st[:, None] // NT == st[None, :] // NT
    cs = np.full((P, LS), NEG, f)
    cs[:LS] = np.where(same & (st[:, None] <= st[None, :]), 0, NEG)
    t["sample_causal"] = cs
    last = np.zeros((P, LS), f)
    last[:LS] = same & (st[None, :] % NT == NT - 1)
    t["sample_last"] = last
    inb = np.zeros((P, NB), f)
    inb[:LS] = st[:, None] // NT == np.arange(NB)[None, :]
    t["in_batch"] = inb
    sel = np.zeros((P, MH * P), f)
    for h in range(MH):
        sel[h, h * P:(h + 1) * P] = 1
    t["head_sel"] = sel
    keep = np.ones((P, T), f)
    keep[:, 0:LP:P] = 0
    keep[:, LP::NT] = 0
    t["keep"] = keep
    return t


def table_places():
    at, out = 0, {}
    for name, a in constant_tables().items():
        out[name] = (at, at + a.shape[1])
        at += a.shape[1]
    return out, at


class Steps:

    def __init__(self, eng):
        self.eng, self.count, self.open = eng, {}, {}

    def __call__(self, ins, sem):
        ins.then_inc(sem, 1)
        self.count[sem.name] = self.count.get(sem.name, 0) + 1
        self.open[sem.name] = sem
        return ins

    def sync(self):
        for name, sem in self.open.items():
            self.eng.wait_ge(sem, self.count[name])
        self.open = {}


class Region:

    def __init__(self, nc, at):
        self.nc, self.at = nc, at

    def __call__(self, name, shape, dt=F32):
        n = int(np.prod(shape[1:])) * 4
        t = self.nc.alloc_sbuf_tensor_at(name, list(shape), dt, offset=self.at)
        self.at += -(-n // 64) * 64
        return t


class Core:

    def __init__(self, nc, ins, outs):
        self.nc, self.I, self.O, self.sems = nc, ins, outs, {}
        self.places, _ = table_places()
        self.ps = nc.alloc_psum_tensor("ps", [P, 8, 512], F32)
        r = Region(nc, 16512)
        self.cst = r("cst", [P, self.places["band"][0]])
        self.gains = r("gains", [P, 4, DC])
        self.rstd = r("rstd", [P, T])
        self.ssum = r("ssum", [P, T])
        self.sq = r("sq", [P, T])
        self.ones = r("ones", [P, P])
        self.resid = r("resid", [P, DC, T])
        self.xh = r("xh", [P, DC, T], F32R)
        self.xl = r("xl", [P, DC, T], F32R)
        self.panels_at = r.at
        self.wraw = [r(f"wraw{s}", [P, FH, P]) for s in range(2)]
        self.whi = [r(f"whi{s}", [P, FH, P], F32R) for s in range(2)]
        self.wlo = [r(f"wlo{s}", [P, FH, P], F32R) for s in range(2)]
        self.scratch_at = r.at
        self.n, self.raw = [0, 0], [0, 0]
        self.ident = self.table("ident")
        self.raw_ready = [self.sem(f"raw_ready{s}") for s in range(2)]
        self.hi_ready = [self.sem(f"hi_ready{s}") for s in range(2)]
        self.lo_ready = [self.sem(f"lo_ready{s}") for s in range(2)]
        self.panel_done = [self.sem(f"panel_done{s}") for s in range(2)]
        self.acc_free = [self.sem(f"acc_free{s}") for s in range(2)]
        self.acc = [self.ps[:, 2 * s:2 * s + 2, 0:HT] for s in range(2)]

    def sem(self, name):
        if name not in self.sems:
            self.sems[name] = self.nc.alloc_semaphore(name)
        return self.sems[name]

    def clear_sems(self, prefixes):
        done = [s for n, s in self.sems.items() if n.startswith(prefixes)]
        self.sems = {n: s for n, s in self.sems.items() if not n.startswith(prefixes)}
        with self.nc.Block() as block:
            @block.gpsimd
            def _(pool):
                self.nc.clear_and_free_semaphores(done)

    def table(self, name):
        a, b = self.places[name]
        return self.cst[:, a:b]

    def table_dram(self, name, rows=P):
        a, b = self.places[name]
        return self.I["tables"][0:rows, a:b]

    def product(self, pairs, kc, nd, slots=(0, 1)):
        g = Product()
        g.n, g.raw, g.pairs, g.kc, g.nd, g.slots = list(self.n), list(self.raw), pairs, kc, nd, slots
        for s in slots:
            self.n[s] += pairs
            self.raw[s] += 16 * nd * pairs
        return g


class Product:
    pass


def chunk(t, m, cols=slice(None)):
    if isinstance(m, int):
        return t[:, m, cols]
    return t[:, bass.ds(m, 1), cols].rearrange("p a t -> p (a t)")


def halves(ap):
    return ap.rearrange("p (a t) -> p a t", a=2)


def loop(eng, start, end, body):
    if end == start + 1:
        body(start)
    elif end > start:
        with eng.Fori(start, end) as i:
            body(i)


def load_panels(K, sp, g, dmas, start=0, end=None):
    def body(i):
        for s in g.slots:
            if not (isinstance(i, int) and g.n[s] + i == 0):
                sp.wait_ge(K.lo_ready[s], g.n[s] + i)
            for dst, src in dmas(s, i):
                sp.dma_start(dst, src).then_inc(K.raw_ready[s], 16)
    if g.n[0] == 0 and start == 0:
        body(0)
        start = 1
    loop(sp, start, g.pairs if end is None else end, body)


def split_hi(K, act, g, s, i):
    act.wait_ge(K.raw_ready[s], g.raw[s] + (i + 1) * (16 * g.nd))
    if not (isinstance(i, int) and g.n[s] + i == 0):
        act.wait_ge(K.panel_done[s], g.n[s] + i)
    act.copy(K.whi[s][:, 0:g.kc, :], K.wraw[s][:, 0:g.kc, :]).then_inc(K.hi_ready[s], 1)


def split_lo(K, dve, g, s, i):
    dve.wait_ge(K.hi_ready[s], g.n[s] + i + 1)
    dve.tensor_tensor(K.wlo[s][:, 0:g.kc, :], K.wraw[s][:, 0:g.kc, :], K.whi[s][:, 0:g.kc, :].bitcast(F32),
                      ALU.subtract).then_inc(K.lo_ready[s], 1)


def split_and_take(K, eng, g, split, evac=None):
    for s in g.slots:
        split(K, eng, g, s, 0)

    def body(i):
        for s in g.slots:
            if evac is not None:
                evac(s, i)
            split(K, eng, g, s, i + 1)
    loop(eng, 0, g.pairs - 1, body)
    for s in g.slots:
        if evac is not None:
            evac(s, g.pairs - 1)


def multiply_panels(K, pe, g, ah, al, before_chunk=None):
    def body(i):
        for s in g.slots:
            pe.wait_ge(K.lo_ready[s], g.n[s] + i + 1)
            if not (isinstance(i, int) and g.n[s] + i == 0):
                pe.wait_ge(K.acc_free[s], g.n[s] + i)
            for k in range(g.kc):
                if before_chunk is not None and s == 0 and isinstance(i, int) and i == 0:
                    before_chunk(k)
                for w, a, start, stop in ((K.whi, ah, k == 0, False), (K.whi, al, False, False),
                                          (K.wlo, ah, False, k == g.kc - 1)):
                    for h in range(2):
                        ins = pe.matmul(K.ps[:, 2 * s + h, 0:HT], w[s][:, k, :],
                                        a[:, k, h * HT:(h + 1) * HT], start=start, stop=stop)
            ins.then_inc(K.panel_done[s], 1)
    first = 1 if g.n[0] == 0 or before_chunk is not None else 0
    if first:
        body(0)
    loop(pe, first, g.pairs, body)


def take(K, eng, g, s, i):
    eng.wait_ge(K.panel_done[s], g.n[s] + i + 1)


def plain_dmas(K, w, kc, m_of=lambda s, i: i * 2 + s):
    v = w.rearrange("(k p) (m c) -> m p k c", p=P, c=P)
    cut = kc // 2

    def dmas(s, i):
        m = m_of(s, i)
        src = v[m] if isinstance(m, int) else v[bass.ds(m, 1)].rearrange("a p k c -> p (a k) c")
        return [(K.wraw[s][:, 0:cut, :], src[:, 0:cut, :]), (K.wraw[s][:, cut:kc, :], src[:, cut:kc, :])]
    return dmas


def square_chunk(K, pool, m, before):
    if not (isinstance(before, int) and before == 0):
        pool.wait_ge(K.sem("summed"), before)
    pool.tensor_tensor(K.sq[:], chunk(K.resid, m), chunk(K.resid, m), ALU.mult).then_inc(K.sem("squared"), 1)
    pool.wait_ge(K.sem("squared"), before + 1)
    pool.tensor_tensor(K.ssum[:], K.ssum[:], K.sq[:], ALU.add).then_inc(K.sem("summed"), 1)


def clear_squares(K, pool, norm):
    if norm:
        pool.wait_ge(K.sem("rms_sum"), norm)
    pool.memset(K.ssum[:], 0.0).then_inc(K.sem("squares_cleared"), 1)
    pool.wait_ge(K.sem("squares_cleared"), norm + 1)


def rms_pe(K, pe, norm):
    pe.wait_ge(K.sem("summed"), DC * (norm + 1))
    for h in range(2):
        ins = pe.matmul(K.ps[:, 6 + h, 0:HT], K.ones[:], K.ssum[:, h * HT:(h + 1) * HT], start=True, stop=True)
    ins.then_inc(K.sem("rms_sum"), 1)


def rms_dve(K, dve, norm):
    dve.wait_ge(K.sem("rms_sum"), norm + 1)
    dve.tensor_scalar(halves(K.rstd[:]), K.ps[:, 6:8, 0:HT], 1.0 / D, EPS, ALU.mult, ALU.add)\
        .then_inc(K.sem("rms_taken"), 1)
    dve.wait_ge(K.sem("rms_taken"), norm + 1)
    dve.reciprocal(K.rstd[:], K.rstd[:]).then_inc(K.sem("rms_inverse"), 1)


def rms_act(K, act, norm):
    act.wait_ge(K.sem("rms_inverse"), norm + 1)
    act.activation(K.rstd[:], K.rstd[:], ACT.Sqrt).then_inc(K.sem("rms_ready"), 1)


def split_x_hi(K, act, norm):
    for m in range(DC):
        act.activation(K.xh[:, m, :], K.resid[:, m, :], ACT.Copy, scale=K.gains[:, norm, m:m + 1])\
            .then_inc(K.sem("x_hi"), 1)


def split_x_lo(K, dve, norm):
    for m in range(DC):
        dve.wait_ge(K.sem("x_hi"), DC * norm + m + 1)
        dve.scalar_tensor_tensor(K.xl[:, m, :], K.resid[:, m, :], K.gains[:, norm, m:m + 1],
                                 K.xh[:, m, :].bitcast(F32), ALU.mult, ALU.subtract).then_inc(K.sem("x_lo"), 1)


def wait_x(K, pe, norm):
    return lambda k: pe.wait_ge(K.sem("x_lo"), DC * norm + k + 1)


def phase_load(K):
    nc, I = K.nc, K.I
    sem = K.sem
    xs = Region(nc, K.scratch_at)("xs", [P, 5, D])
    x_in, consts_in, x_t = sem("x_in"), sem("consts_in"), sem("x_transposed")
    res_act, res_dve = sem("resid_prompt"), sem("resid_sample")

    with nc.Block() as block:
        @block.sync
        def _(sp):
            sp.dma_start(xs[:, 0:4, :], I["x_prompt"][0].rearrange("(n p) d -> p n d", p=P)).then_inc(x_in, 16)
            sp.dma_start(xs[0:LS, 4, :], I["x_sample"].rearrange("b t d -> (b t) d")).then_inc(x_in, 16)

        @block.scalar
        def _(act):
            act.dma_start(K.cst[:], I["tables"][:, 0:K.places["band"][0]]).then_inc(consts_in, 16)
            for n, g in enumerate(("norm_mix", "norm_ffn")):
                for l in range(2):
                    act.dma_start(K.gains[:, 2 * l + n, :], I[g][l].rearrange("(c p) -> p c", p=P),
                                  allow_slow_non_contiguous=True).then_inc(consts_in, 16)
            act.wait_ge(consts_in, 80)
            for m in range(DC):
                act.wait_ge(x_t, m + 1)
                act.copy(K.resid[:, m, 0:LP], K.ps[:, 2 * (m % 2), :]).then_inc(res_act, 1)

        @block.vector
        def _(dve):
            dve.memset(K.ones[:], 1.0).then_inc(sem("ones_ready"), 1)
            dve.wait_ge(consts_in, 80)
            for m in range(DC):
                dve.wait_ge(x_t, m + 1)
                dve.tensor_copy(K.resid[:, m, LP:T], K.ps[:, 2 * (m % 2) + 1, 0:LS]).then_inc(res_dve, 1)

        @block.gpsimd
        def _(pool):
            clear_squares(K, pool, 0)
            for m in range(DC):
                pool.wait_ge(res_act, m + 1)
                pool.wait_ge(res_dve, m + 1)
                square_chunk(K, pool, m, m)

        @block.tensor
        def _(pe):
            pe.wait_ge(consts_in, 80)
            pe.wait_ge(x_in, 32)
            for m in range(DC):
                if m >= 2:
                    pe.wait_ge(res_act, m - 1)
                    pe.wait_ge(res_dve, m - 1)
                for n in range(4):
                    pe.transpose(K.ps[:, 2 * (m % 2), n * P:(n + 1) * P], xs[:, n, m * P:(m + 1) * P], K.ident)
                pe.transpose(K.ps[:, 2 * (m % 2) + 1, 0:LS], xs[0:LS, 4, m * P:(m + 1) * P],
                             K.cst[0:LS, 0:LS]).then_inc(x_t, 1)


def phase_out_ffn(K, dmas_out, layer):
    nc, I, sem = K.nc, K.I, K.sem
    r = Region(nc, K.scratch_at)
    hh, hl = r(f"hh{layer}", [P, FH, T], F32R), r(f"hl{layer}", [P, FH, T], F32R)
    gate, up, act_gate = (r(f"{x}{layer}", [P, T]) for x in ("gate", "up", "act_gate"))
    norm = 2 * layer + 1
    squares = DC * norm
    w_gate, w_up, w_down = I["w_gate"][layer], I["w_up"][layer], I["w_down"][layer]
    g_out = K.product(DC // 2, DC, dmas_out[1])
    g_up, g_down = [], []
    for half in range(2):
        g_up.append(K.product(FH, DC, 2))
        g_down.append(K.product(DC // 2, FH, 2))
    gate_ready, gated, hid, hid_hi, hid_lo = (sem(x) for x in ("gate_ready", "gated", "hidden", "hidden_hi", "hidden_lo"))
    up_ready = sem("up_ready")
    turns = [FH * (2 * layer + half) for half in range(2)]

    def two_loads(half):
        vs = [w.rearrange("(k p) (m c) -> m p k c", p=P, c=P) for w in (w_gate, w_up)]

        def dmas(s, i):
            m = i + FH * half
            src = vs[s][m] if isinstance(m, int) else vs[s][bass.ds(m, 1)].rearrange("a p k c -> p (a k) c")
            return [(K.wraw[s][:, 0:4, :], src[:, 0:4, :]), (K.wraw[s][:, 4:8, :], src[:, 4:8, :])]
        return dmas

    def add_resid(dve, g):
        def evac(s, i):
            take(K, dve, g, s, i)
            m = i * 2 + s
            x = chunk(K.resid, m)
            dve.tensor_tensor(halves(x), K.acc[s], halves(x), ALU.add).then_inc(K.acc_free[s], 1)
        return evac

    with nc.Block() as block:
        @block.sync
        def _(sp):
            load_panels(K, sp, g_out, dmas_out[0])
            for half in range(2):
                load_panels(K, sp, g_up[half], two_loads(half))
                load_panels(K, sp, g_down[half], plain_dmas(K, w_down[half * FH * P:(half + 1) * FH * P], FH))

        @block.tensor
        def _(pe):
            multiply_panels(K, pe, g_out, K.xh, K.xl)
            for half in range(2):
                if half == 0:
                    multiply_first = wait_x(K, pe, norm)
                    rms_pe(K, pe, norm)
                    multiply_panels(K, pe, g_up[0], K.xh, K.xl, multiply_first)
                else:
                    multiply_panels(K, pe, g_up[1], K.xh, K.xl)
                multiply_panels(K, pe, g_down[half], hh, hl,
                                lambda k: pe.wait_ge(hid_lo, turns[half] + k + 1))

        @block.vector
        def _(dve):
            split_and_take(K, dve, g_out, split_lo, add_resid(dve, g_out))
            split_x_lo(K, dve, norm)
            rms_dve(K, dve, norm)
            for half in range(2):
                n = turns[half]

                def evac(s, i):
                    take(K, dve, g_up[half], s, i)
                    if s == 0:
                        if half == 0 and isinstance(i, int):
                            dve.wait_ge(sem("rms_ready"), norm + 1)
                        if not (isinstance(i, int) and n + i == 0):
                            dve.wait_ge(gated, n + i)
                        dve.tensor_tensor(halves(gate[:]), K.acc[0], halves(K.rstd[:]), ALU.mult)\
                            .then_inc(K.acc_free[0], 1)
                    else:
                        if not (isinstance(i, int) and n + i == 0):
                            dve.wait_ge(hid_lo, n + i)
                        dve.tensor_tensor(halves(up[:]), K.acc[1], halves(K.rstd[:]), ALU.mult)\
                            .then_inc(K.acc_free[1], 1)
                        dve.wait_ge(K.acc_free[1], g_up[half].n[1] + i + 1)
                        dve.wait_ge(gated, n + i + 1)
                        dve.tensor_tensor(up[:], up[:], act_gate[:], ALU.mult).then_inc(hid, 1)
                        dve.wait_ge(hid_hi, n + i + 1)
                        dve.tensor_tensor(chunk(hl, i), up[:], chunk(hh, i).bitcast(F32), ALU.subtract)\
                            .then_inc(hid_lo, 1)
                if half == 0:
                    dve.wait_ge(sem("rms_ready"), norm + 1)
                split_and_take(K, dve, g_up[half], split_lo, evac)
                split_and_take(K, dve, g_down[half], split_lo, add_resid(dve, g_down[half]))

        @block.scalar
        def _(act):
            split_and_take(K, act, g_out, split_hi)
            act.wait_ge(K.acc_free[0], g_out.n[0] + g_out.pairs)
            act.wait_ge(K.acc_free[1], g_out.n[1] + g_out.pairs)
            split_x_hi(K, act, norm)
            rms_act(K, act, norm)
            for half in range(2):
                n = turns[half]

                def evac(s, i):
                    if s == 0:
                        act.wait_ge(K.acc_free[0], g_up[half].n[0] + i + 1)
                        if not (isinstance(i, int) and n + i == 0):
                            act.wait_ge(hid, n + i)
                        act.activation(act_gate[:], gate[:], ACT.Silu).then_inc(gated, 1)
                    else:
                        act.wait_ge(hid, n + i + 1)
                        act.copy(chunk(hh, i), up[:]).then_inc(hid_hi, 1)
                split_and_take(K, act, g_up[half], split_hi, evac)
                split_and_take(K, act, g_down[half], split_hi)

        @block.gpsimd
        def _(pool):
            def squares_of(g, at):
                def body(i):
                    for s in (0, 1):
                        pool.wait_ge(K.acc_free[s], g.n[s] + i + 1)
                        square_chunk(K, pool, i * 2 + s, i * 2 + (s + at))
                loop(pool, 0, g.pairs, body)
            clear_squares(K, pool, norm)
            squares_of(g_out, squares)
            if layer == 0:
                clear_squares(K, pool, norm + 1)
                squares_of(g_down[1], squares + DC)


def phase_store(K):
    nc, sem = K.nc, K.sem
    ys = Region(nc, K.scratch_at)("ys", [P, 5, D])
    y_t, y_a, y_d, y_out = sem("y_transposed"), sem("y_taken_act"), sem("y_taken_dve"), sem("y_out")
    with nc.Block() as block:
        @block.tensor
        def _(pe):
            for n in range(5):
                rows = P if n < 4 else LS
                for q in range(2):
                    j = 2 * n + q
                    if j >= 4:
                        pe.wait_ge(y_a, j // 2 - 1)
                        pe.wait_ge(y_d, j // 2 - 1)
                    for m in range(4):
                        ins = pe.transpose(K.ps[0:rows, j % 4, m * P:(m + 1) * P],
                                           K.resid[:, 4 * q + m, n * P:n * P + rows], K.ident)
                    ins.then_inc(y_t, 1)

        @block.scalar
        def _(act):
            for n in range(5):
                rows = P if n < 4 else LS
                act.wait_ge(y_t, 2 * n + 1)
                act.copy(ys[0:rows, n, 0:512], K.ps[0:rows, (2 * n) % 4, :]).then_inc(y_a, 1)

        @block.vector
        def _(dve):
            for n in range(5):
                rows = P if n < 4 else LS
                dve.wait_ge(y_t, 2 * n + 2)
                dve.tensor_copy(ys[0:rows, n, 512:D], K.ps[0:rows, (2 * n + 1) % 4, :]).then_inc(y_d, 1)

        @block.sync
        def _(sp):
            for n in range(5):
                sp.wait_ge(y_a, n + 1)
                sp.wait_ge(y_d, n + 1)
                if n < 4:
                    sp.dma_start(K.O[0][0, n * P:(n + 1) * P, :], ys[:, n, :]).then_inc(y_out, 16)
                else:
                    sp.dma_start(K.O[1].rearrange("b t d -> (b t) d"), ys[0:LS, 4, :]).then_inc(y_out, 16)
            sp.wait_ge(y_out, 80)


def cmul(st, eng, s, out_r, out_i, ar, ai, br, bi, tmp):
    st(eng.tensor_tensor(out_r, ar, br, ALU.mult), s)
    st(eng.tensor_tensor(tmp, ai, bi, ALU.mult), s)
    st(eng.tensor_tensor(out_i, ar, bi, ALU.mult), s)
    st.sync()
    st(eng.tensor_tensor(out_r, out_r, tmp, ALU.subtract), s)
    st.sync()
    st(eng.tensor_tensor(tmp, ai, br, ALU.mult), s)
    st.sync()
    st(eng.tensor_tensor(out_i, out_i, tmp, ALU.add), s)
    st.sync()


def phase_even_in(K):
    nc, I, sem = K.nc, K.I, K.sem
    r = Region(nc, K.scratch_at)
    proj = K.proj = r("proj", [P, EVEN_IN // P, T])
    E = K.s5_e = [r(f"s5_e_{x}", [P, NPAIR, P]) for x in "ri"]
    F = K.s5_f = [r(f"s5_f_{x}", [P, NPAIR, SUB + 1, S5H]) for x in "ri"]
    G = K.s5_g = r("s5_g", [P, S5G, P])
    rot = K.s5_rot = [r(f"s5_rot_{x}", [P, NPAIR, NSUB]) for x in "ri"]
    decay = K.s5_decay = r("s5_decay", [P, NPAIR, NSUB])
    pw = K.s5_pw = [r(f"s5_pw_{x}", [P, NPAIR, SUB + 1]) for x in "ri"]
    K.even_scratch = r.at
    par = r("s5_par", [P, 3 * NPAIR])
    par_in = r("s5_par_in", [P, P])
    b_in = [r(f"s5_b_{x}", [P, NPAIR, S5H]) for x in "ri"]
    bb = [r(f"s5_bb_{x}", [P, NPAIR, S5H]) for x in "ri"]
    c_in = [r(f"s5_c_{x}", [P, 4, 2, S5P]) for x in "ri"]
    ct = [r(f"s5_ct_{x}", [P, NPAIR, S5H]) for x in "ri"]
    d_in = r("s5_d_in", [S5H, S5G])
    small = r("s5_small", [P, 18, NPAIR])
    tmp = r("s5_tmp", [P, NPAIR, SUB, S5H])
    assert r.at <= 229368, r.at
    kt = Region(nc, 16512 + (K.panels_at - 16512) - 2 * DC * T * 4)("s5_kt", [S5H, S5G, P])
    eb = [G[:, 0:NPAIR, :], G[:, NPAIR:2 * NPAIR, :]]
    g = K.product(5, DC, 2)
    s5_in, s5_small, s5_act = sem("s5_in"), sem("s5_small"), sem("s5_act")
    par_t, c_t, c_taken = sem("s5_par_t"), sem("s5_c_t"), sem("s5_c_taken")
    s5_pool, s5_mats = sem("s5_pool"), sem("s5_mats")
    e_t, e_act, e_dve, kt_t, kt_taken, g_in = (sem(x) for x in ("s5_e_t", "s5_e_act", "s5_e_dve", "s5_kt_t", "s5_kt_taken", "s5_g_in"))
    ROW = {n: k for k, n in enumerate("dt ard aid mag k r carg wi wr lr li den lm cr ci t1 t2 m8".split())}

    def sm(name):
        return small[:, ROW[name], :]
    coef_ready, zeroed = sem("s5_coef"), sem("s5_zeroed")
    w_in = I["w_in_even"][0]
    vq = w_in[:, 0:512].rearrange("(k p) (two h d) -> h two p k d", p=P, two=2, d=HD)

    def q_dmas(s, i):
        return [(K.wraw[s][:, 0:DC, two * HD:(two + 1) * HD], vq[2 * i + s][two]) for two in range(2)]

    with nc.Block() as block:
        @block.sync
        def _(sp):
            load_panels(K, sp, g, q_dmas, 0, 1)
            load_panels(K, sp, g, q_dmas, 1, 2)
            load_panels(K, sp, g, plain_dmas(K, w_in, DC), 2)
            sp.wait_ge(kt_taken, 10)
            sp.wait_ge(zeroed, 1)
            for row in range(SUB):
                s = SUB - 1 - row
                sp.dma_start(G[row * S5H:(row + 1) * S5H, :, s * S5H:P], kt[:, :, 0:P - s * S5H]).then_inc(g_in, 16)
            sp.wait_ge(g_in, 16 * SUB)

        @block.tensor
        def _(pe):
            pe.wait_ge(s5_in, 160)
            pe.transpose(K.ps[:, 6, 0:48], par_in[0:48, :], K.cst[0:48, 0:48]).then_inc(par_t, 1)
            for x in range(2):
                for m in range(4):
                    ins = pe.transpose(K.ps[:, 4 + x, m * P:(m + 1) * P],
                                       c_in[x][:, m, :, :].rearrange("p a b -> p (a b)"), K.ident)
            ins.then_inc(c_t, 1)
            pe.wait_ge(s5_small, 1)
            rms_pe(K, pe, 0)
            multiply_panels(K, pe, g, K.xh, K.xl, wait_x(K, pe, 0))
            pe.wait_ge(s5_mats, 1)
            pe.wait_ge(c_taken, 4)
            for x in range(2):
                for b in range(4):
                    k = 4 * x + b
                    if k >= 4:
                        pe.wait_ge(e_act if k % 2 == 0 else e_dve, (k - 4) // 2 + 1)
                    if k == 2:
                        pe.wait_ge(sem("rms_taken"), 1)
                    for m in range(4):
                        ins = pe.transpose(K.ps[:, 4 + k % 4, m * P:(m + 1) * P], eb[x][:, 4 * b + m, :], K.ident)
                    ins.then_inc(e_t, 1)
            for q in range(4):
                for two in range(2):
                    k = 2 * q + two
                    bank = 4 + k % 4
                    if k < 4:
                        pe.wait_ge(e_act if k % 2 == 0 else e_dve, (4 + k) // 2 + 1)
                    else:
                        pe.wait_ge(kt_taken, k - 3)
                    hp = slice(two * S5P, (two + 1) * S5P)
                    for jj in range(4):
                        j = 4 * q + jj
                        for x in range(2):
                            ins = pe.matmul(K.ps[0:S5H, bank, jj * P:(jj + 1) * P], bb[x][hp, j, :],
                                            F[x][hp, j, 0:SUB, :].rearrange("p a b -> p (a b)"), start=x == 0, stop=x == 1)
                    ins.then_inc(kt_t, 1)

        @block.scalar
        def _(act):
            for n, x in enumerate(("s5_a_re", "s5_a_im", "s5_log_dt")):
                act.dma_start(par_in[16 * n:16 * n + 16, :], I[x][0].rearrange("(j two) p -> j (two p)", two=2))\
                    .then_inc(s5_in, 16)
            for x, nm in enumerate(("re", "im")):
                act.dma_start(b_in[x][:], I["s5_b_" + nm][0].rearrange("(j two) p h -> (two p) j h", two=2)).then_inc(s5_in, 16)
                cv = I["s5_c_" + nm][0].rearrange("g h p -> (g h) p").rearrange("(m q) p -> q m p", q=P)
                for two in range(2):
                    act.dma_start(c_in[x][:, :, two, :], cv).then_inc(s5_in, 16)
            act.dma_start(d_in[:], I["s5_d"][0].rearrange("g h -> h g"), allow_slow_non_contiguous=True).then_inc(s5_in, 16)
            split_x_hi(K, act, 0)
            act.wait_ge(s5_small, 1)
            act.activation(sm("dt"), par[:, 32:48], ACT.Exp).then_inc(s5_act, 1)
            act.wait_ge(c_t, 1)
            for x in range(2):
                cp = K.ps[:, 4 + x, :].rearrange("p (j two h) -> p j two h", two=2, h=S5H)
                for two in range(2):
                    hp = slice(two * S5P, (two + 1) * S5P)
                    ins = act.copy(ct[x][hp, :, :], cp[hp, :, two, :])
                    ins.then_inc(c_taken, 1)
            act.wait_ge(s5_small, 3)
            act.activation(sm("mag"), sm("ard"), ACT.Exp).then_inc(s5_act, 1)
            rms_act(K, act, 0)
            act.wait_ge(s5_small, 12)
            act.activation(sm("wi"), sm("r"), ACT.Sin).then_inc(s5_act, 1)
            act.activation(sm("wr"), sm("carg"), ACT.Sin).then_inc(s5_act, 1)
            split_and_take(K, act, g, split_hi)
            for k in range(0, 8, 2):
                act.wait_ge(e_t, k + 1)
                act.copy(E[k // 4][:, 4 * (k % 4):4 * (k % 4) + 4, :].rearrange("p a b -> p (a b)"),
                         K.ps[:, 4 + k % 4, :]).then_inc(e_act, 1)

        @block.vector
        def _(dve):
            st = Steps(dve)
            s = s5_small
            split_x_lo(K, dve, 0)
            dve.wait_ge(par_t, 1)
            st(dve.tensor_copy(par[:], K.ps[:, 6, 0:48]), s)
            ar, ai = par[:, 0:16], par[:, 16:32]
            st.sync()
            dve.wait_ge(s5_act, 1)
            st(dve.tensor_tensor(sm("aid"), ai, sm("dt"), ALU.mult), s)
            st(dve.tensor_tensor(sm("ard"), ar, sm("dt"), ALU.mult), s)
            st.sync()
            st(dve.tensor_scalar(sm("k"), sm("aid"), 1 / TWO_PI, ROUND, ALU.mult, ALU.add), s)
            st.sync()
            st(dve.tensor_scalar(sm("k"), sm("k"), ROUND, None, ALU.subtract), s)
            st.sync()
            c1 = 6.28125
            c2 = round((TWO_PI - c1) * 2 ** 20) / 2 ** 20
            c3 = TWO_PI - c1 - c2
            src = "aid"
            for c in (c1, c2, c3):
                st(dve.scalar_tensor_tensor(sm("r"), sm("k"), -c, sm(src), ALU.mult, ALU.add), s)
                st.sync()
                src = "r"
            st(dve.tensor_scalar(sm("r"), sm("r"), 3.1415925, -3.1415925, ALU.min, ALU.max), s)
            st.sync()
            st(dve.tensor_scalar(sm("carg"), sm("r"), -1.0, None, ALU.mult), s)
            st.sync()
            st(dve.tensor_tensor(sm("carg"), sm("carg"), sm("r"), ALU.min), s)
            st.sync()
            st(dve.tensor_scalar(sm("carg"), sm("carg"), np.pi / 2, None, ALU.add), s)
            rms_dve(K, dve, 0)
            dve.wait_ge(s5_act, 4)
            st(dve.tensor_tensor(sm("lr"), sm("mag"), sm("wr"), ALU.mult), s)
            st(dve.tensor_tensor(sm("li"), sm("mag"), sm("wi"), ALU.mult), s)
            st(dve.tensor_tensor(sm("den"), ar, ar, ALU.mult), s)
            st(dve.tensor_tensor(sm("t1"), ai, ai, ALU.mult), s)
            st(dve.tensor_tensor(sm("m8"), sm("mag"), sm("mag"), ALU.mult), s)
            st.sync()
            st(dve.tensor_tensor(sm("den"), sm("den"), sm("t1"), ALU.add), s)
            st(dve.tensor_scalar(sm("lm"), sm("lr"), -1.0, None, ALU.add), s)
            st(dve.tensor_tensor(sm("t2"), sm("m8"), sm("m8"), ALU.mult), s)
            st.sync()
            st(dve.reciprocal(sm("den"), sm("den")), s)
            st(dve.tensor_tensor(sm("m8"), sm("t2"), sm("t2"), ALU.mult), s)
            st.sync()
            st(dve.tensor_tensor(sm("cr"), sm("lm"), ar, ALU.mult), s)
            st(dve.tensor_tensor(sm("t1"), sm("li"), ai, ALU.mult), s)
            st(dve.tensor_tensor(sm("ci"), sm("li"), ar, ALU.mult), s)
            st(dve.tensor_tensor(sm("t2"), sm("lm"), ai, ALU.mult), s)
            st.sync()
            st(dve.tensor_tensor(sm("cr"), sm("cr"), sm("t1"), ALU.add), s)
            st(dve.tensor_tensor(sm("ci"), sm("ci"), sm("t2"), ALU.subtract), s)
            st.sync()
            st(dve.tensor_tensor(sm("cr"), sm("cr"), sm("den"), ALU.mult), s)
            st(dve.tensor_tensor(sm("ci"), sm("ci"), sm("den"), ALU.mult), s)
            st.sync()
            dve.memset(decay[:, :, 0:1], 0.0).then_inc(coef_ready, 1)
            dve.wait_ge(sem("rms_ready"), 1)

            def evac(slot, i):
                take(K, dve, g, slot, i)
                dve.tensor_tensor(halves(chunk(proj, i * 2 + slot)), K.acc[slot], halves(K.rstd[:]), ALU.mult)\
                    .then_inc(K.acc_free[slot], 1)
            split_and_take(K, dve, g, split_lo, evac)
            for k in range(1, 8, 2):
                dve.wait_ge(e_t, k + 1)
                dve.tensor_copy(E[k // 4][:, 4 * (k % 4):4 * (k % 4) + 4, :].rearrange("p a b -> p (a b)"),
                                K.ps[:, 4 + k % 4, :]).then_inc(e_dve, 1)
            dve.wait_ge(e_act, 4)
            dve.memset(G[:], 0.0).then_inc(zeroed, 1)
            for q in range(4):
                for two in range(2):
                    k = 2 * q + two
                    dve.wait_ge(kt_t, k + 1)
                    v = kt[:, :, :].rearrange("h (j two) x -> h j two x", two=2)[:, 4 * q:4 * q + 4, two, :]
                    dve.tensor_copy(v, K.ps[0:S5H, 4 + k % 4, :].rearrange("h (j x) -> h j x", x=P)).then_inc(kt_taken, 1)
            dve.wait_ge(kt_taken, 8)
            dd = K.sq[0:S5H, 0:S5G * S5H].rearrange("p (g x) -> p g x", x=S5H)
            dve.tensor_tensor(dd, K.ident[0:S5H, 0:S5H].unsqueeze(1).broadcast_to([S5H, S5G, S5H]),
                              d_in[:].unsqueeze(2).broadcast_to([S5H, S5G, S5H]), ALU.mult).then_inc(kt_taken, 1)
            dve.wait_ge(kt_taken, 9)
            dve.tensor_tensor(kt[:, :, 0:S5H], kt[:, :, 0:S5H], dd, ALU.add).then_inc(kt_taken, 1)

        @block.gpsimd
        def _(pool):
            st = Steps(pool)
            s = s5_pool
            pool.wait_ge(coef_ready, 1)

            def b3(name):
                return sm(name).unsqueeze(2).broadcast_to([P, NPAIR, S5H])
            t3 = tmp[:, :, 0, :]
            cmul(st, pool, s, bb[0][:], bb[1][:], b3("cr"), b3("ci"), b_in[0][:], b_in[1][:], t3)
            st(pool.memset(pw[0][:, :, 0:1], 1.0), s)
            st(pool.memset(pw[1][:, :, 0:1], 0.0), s)
            st(pool.tensor_copy(pw[0][:, :, 1:2], sm("lr").unsqueeze(2)), s)
            st(pool.tensor_copy(pw[1][:, :, 1:2], sm("li").unsqueeze(2)), s)
            st.sync()
            for n in (1, 2, 4):
                a = [pw[x][:, :, 1:n + 1] for x in range(2)]
                w = [pw[x][:, :, n:n + 1].broadcast_to([P, NPAIR, n]) for x in range(2)]
                cmul(st, pool, s, pw[0][:, :, n + 1:2 * n + 1], pw[1][:, :, n + 1:2 * n + 1], *a, *w, t3[:, :, 0:n])
            pool.wait_ge(c_taken, 4)
            for lo, hi in ((0, SUB), (SUB, SUB + 1)):
                n = hi - lo
                sh = [P, NPAIR, n, S5H]
                cb = [ct[x][:].unsqueeze(2).broadcast_to(sh) for x in range(2)]
                pb = [pw[x][:, :, lo:hi].unsqueeze(3).broadcast_to(sh) for x in range(2)]
                cmul(st, pool, s, F[0][:, :, lo:hi, :], F[1][:, :, lo:hi, :], *cb, *pb, tmp[:, :, 0:n, :])
                st(pool.tensor_scalar(F[1][:, :, lo:hi, :], F[1][:, :, lo:hi, :], -1.0, None, ALU.mult), s)
                st.sync()
            sh = [P, NPAIR, SUB, S5H]
            ev = [eb[x].rearrange("p j (s h) -> p j s h", h=S5H) for x in range(2)]
            cmul(st, pool, s, ev[0], ev[1], *[pw[x][:, :, 0:SUB].unsqueeze(3).broadcast_to(sh) for x in range(2)],
                 *[bb[x][:].unsqueeze(2).broadcast_to(sh) for x in range(2)], tmp[:])
            pool.memset(sm("t1"), 0.0).then_inc(s5_mats, 1)
            w = [tmp[:, :, 0, x:x + 1] for x in range(2)]
            v = [tmp[:, :, 1, x:x + 1] for x in range(2)]
            tq = tmp[:, :, 2, 0:1]
            st(pool.tensor_copy(w[0], sm("wr").unsqueeze(2)), s)
            st(pool.tensor_copy(w[1], sm("wi").unsqueeze(2)), s)
            st.sync()
            for k in range(3):
                cmul(st, pool, s, *v, *w, *w, tq)
                w, v = v, w
            st(pool.memset(rot[0][:, :, 0:1], 1.0), s)
            st(pool.memset(rot[1][:, :, 0:1], 0.0), s)
            st(pool.tensor_copy(rot[0][:, :, 1:2], w[0]), s)
            st(pool.tensor_copy(rot[1][:, :, 1:2], w[1]), s)
            st.sync()
            n = 1
            while n < NSUB - 1:
                k = min(n, NSUB - 1 - n)
                a = [rot[x][:, :, 1:k + 1] for x in range(2)]
                wb = [rot[x][:, :, n:n + 1].broadcast_to([P, NPAIR, k]) for x in range(2)]
                tt = tmp[:].rearrange("p j a b -> p j (a b)")[:, :, 0:k]
                cmul(st, pool, s, rot[0][:, :, n + 1:n + 1 + k], rot[1][:, :, n + 1:n + 1 + k], *a, *wb, tt)
                n += k
            st(pool.tensor_copy(decay[:, :, 1:NSUB], sm("m8").unsqueeze(2).broadcast_to([P, NPAIR, NSUB - 1])), s)
            st.sync()


def phase_s5(K):
    nc, I, O, sem = K.nc, K.I, K.O, K.sem
    proj, E, F, G, rot, decay, pw = K.proj, K.s5_e, K.s5_f, K.s5_g, K.s5_rot, K.s5_decay, K.s5_pw
    a = Region(nc, K.panels_at)
    U = a("s5_u", [P, S5G, NSUB])
    US = a("s5_us", [P, S5G, NB])
    X = [a(f"s5_x_{x}", [P, NPAIR, NSUB]) for x in "ri"]
    R = [a(f"s5_r_{x}", [P, NPAIR, NSUB]) for x in "ri"]
    tp = a("s5_tp", [P, NPAIR * NSUB])
    h_nat = [a(f"s5_h_nat_{x}", [P, P]) for x in "ri"]
    assert a.at <= K.scratch_at
    b = Region(nc, K.even_scratch)
    H = [b(f"s5_h_{x}", [P, NPAIR, NSUB + 1]) for x in "ri"]
    up = b("s5_up", [P, 4, T])
    h0 = [b(f"s5_h0_{x}", [P, NPAIR, NB]) for x in "ri"]
    fin_s = [b(f"s5_fin_s_{x}", [P, NB, NPAIR]) for x in "ri"]
    fin_p = b("s5_fin_p", [P, 2, NPAIR])
    b_glu = b("s5_b_glu_t", [P, 4])
    YS = b("s5_ys", [P, S5G, NB])
    t8 = b("s5_t8", [P, NPAIR, NB])
    assert b.at <= 229368, b.at
    fin_pt = t8[0:32].rearrange("p j b -> p (j b)")
    Y = U
    yT = proj[:, 6:10, :]
    wg = Region(nc, K.panels_at + 8192 + 1024)("s5_wg", [P, 4, 512])
    o_glu = [Region(nc, K.panels_at + 9216 + 8192 + 2176 * x)(f"s5_o{x}", [P, T]) for x in range(2)]
    sg = [Region(nc, K.panels_at + 9216 + 8192 + 4352 + 2176 * x)(f"s5_sg{x}", [P, T]) for x in range(2)]
    u_d = nc.dram_tensor("u_scratch", [512, T], F32, kind="Internal").ap()
    y_d = nc.dram_tensor("y_scratch", [512, T], F32, kind="Internal").ap()
    ud_v, yd_v = (x.rearrange("(g h) x -> h g x", h=S5H) for x in (u_d, y_d))
    S = {n: sem("s5a_" + n) for n in ("up", "ud", "u", "h_in", "h_t", "h0", "inc", "x_pe", "x_sb", "rot_r", "rot_i",
                                      "scan", "h", "y_pe", "y_sb", "ys_sb", "yd", "yt", "gelu", "glu", "sig", "o", "mh",
                                      "fin", "fin_t", "fin_sb", "st", "z_in", "small", "dve", "pool", "ml", "xfree")}

    def perm(ap, outer, inner):
        return ap.rearrange("p (c t) -> p t c", c=inner, t=outer)

    def natural(ap, lo, hi, outer, inner):
        return ap[:, lo:hi].rearrange("p (t c) -> p t c", t=outer, c=inner)

    with nc.Block() as block:
        @block.sync
        def _(sp):
            for x, nm in enumerate(("re", "im")):
                sp.dma_start(h_nat[x][:], I["state_ssm_" + nm][0].rearrange("b (j two) p -> (b j) (two p)", two=2))\
                    .then_inc(S["h_in"], 16)
            sp.dma_start(b_glu[:], I["s5_b_glu"][0].rearrange("(m p) -> p m", p=P), allow_slow_non_contiguous=True)\
                .then_inc(S["z_in"], 16)
            sp.wait_ge(S["up"], 8)
            sp.dma_start(u_d.rearrange("(m q) x -> q m x", q=P), up[:]).then_inc(S["ud"], 16)
            sp.wait_ge(S["ud"], 16)
            for row in range(0, SUB):
                t = SUB - 1 - row
                sp.dma_start(U[row * S5H:(row + 1) * S5H, :, :], ud_v[:, :, t * NSUB:(t + 1) * NSUB]).then_inc(S["u"], 16)
            sp.wait_ge(S["xfree"], 1)
            sp.dma_start(wg[:], I["s5_w_glu"][0].rearrange("(k p) n -> p k n", p=P)).then_inc(S["z_in"], 16)
            for m in range(4):
                sp.wait_ge(S["y_sb"], m + 1)
            sp.wait_ge(S["ys_sb"], 2)
            for t in range(SUB):
                sp.dma_start(yd_v[:, :, t * NSUB:(t + 1) * NSUB], Y[t * S5H:(t + 1) * S5H, :, :]).then_inc(S["yd"], 16)
            for t in range(NT):
                sp.dma_start(yd_v[:, :, LP + t * NB:LP + (t + 1) * NB], YS[t * S5H:(t + 1) * S5H, :, :]).then_inc(S["yd"], 16)
            sp.wait_ge(S["yd"], 16 * (SUB + NT))
            sp.dma_start(yT, y_d.rearrange("(m q) x -> q m x", q=P)).then_inc(S["yt"], 16)
            sp.wait_ge(S["fin_sb"], 3)
            for x in range(2):
                sp.dma_start(O[4 + x][0, 0].rearrange("(j two) p -> j (two p)", two=2), fin_pt[16 * x:16 * x + 16, :])\
                    .then_inc(S["st"], 16)
                sp.dma_start(O[11 + x][0].rearrange("b (j two) p -> (b j) (two p)", two=2),
                             h_nat[x][:]).then_inc(S["st"], 16)
            sp.wait_ge(S["st"], 64)

        @block.scalar
        def _(act):
            for m in range(4):
                act.copy(natural(up[:, m, :], 0, LP, SUB, NSUB), perm(proj[:, 6 + m, 0:LP], SUB, NSUB)).then_inc(S["up"], 1)
                act.copy(natural(up[:, m, :], LP, T, NT, NB), perm(proj[:, 6 + m, LP:T], NT, NB)).then_inc(S["up"], 1)
            act.wait_ge(S["ud"], 16)
            for t in range(NT):
                for row in (SUB - 1 - t, NT - 1 - t):
                    act.dma_start(US[row * S5H:(row + 1) * S5H, :, :], ud_v[:, :, LP + t * NB:LP + (t + 1) * NB])\
                        .then_inc(S["u"], 16)
            for x in range(2):
                act.wait_ge(S["h_t"], 1)
                act.copy(h0[x][:].rearrange("p j b -> p b j"),
                         K.ps[:, 7, x * P:(x + 1) * P].rearrange("p (b j) -> p b j", b=NB)).then_inc(S["h0"], 1)
            for x in range(2):
                act.wait_ge(S["x_pe"], x + 1)
                act.copy(X[x][:].rearrange("p j c -> p (j c)").rearrange("p (a q) -> p a q", a=2),
                         K.ps[:, 2 * x:2 * x + 2, :]).then_inc(S["x_sb"], 1)
            for m in range(4):
                act.wait_ge(S["y_pe"], m + 1)
                at = 8 * (m // 2)
                act.copy(Y[:].rearrange("p (j two) c -> p j two c", two=2)[:, at:at + 8, m % 2, :],
                         K.ps[:, m, :].rearrange("p (j c) -> p j c", c=NSUB)).then_inc(S["y_sb"], 1)
            act.wait_ge(S["yt"], 16)
            for m in range(4):
                act.activation(up[:, m, :], yT[:, m, :], ACT.Gelu).then_inc(S["gelu"], 1)
            act.wait_ge(S["z_in"], 32)
            for m in range(4):
                act.wait_ge(S["glu"], m + 1)
                if m >= 2:
                    act.wait_ge(S["o"], m - 1)
                act.activation(halves(sg[m % 2][:]), K.ps[:, 2 * (m % 2):2 * (m % 2) + 2, 0:HT], ACT.Sigmoid,
                               bias=b_glu[:, m:m + 1]).then_inc(S["sig"], 1)
                act.wait_ge(S["o"], m + 1)
                act.copy(perm(K.xh[:, 4 + m, 0:LP], SUB, NSUB), natural(o_glu[m % 2], 0, LP, SUB, NSUB))
                act.copy(perm(K.xh[:, 4 + m, LP:T], NT, NB), natural(o_glu[m % 2], LP, T, NT, NB)).then_inc(S["mh"], 1)

        @block.tensor
        def _(pe):
            pe.wait_ge(S["h_in"], 32)
            for x in range(2):
                ins = pe.transpose(K.ps[:, 7, x * P:(x + 1) * P], h_nat[x][:], K.ident)
            ins.then_inc(S["h_t"], 1)
            pe.wait_ge(S["u"], 16 * (SUB + 2 * NT))
            for x in range(2):
                for j in range(NPAIR):
                    for two in range(2):
                        hp = slice(two * S5P, (two + 1) * S5P)
                        c = x * P + j * NB
                        ins = pe.matmul(K.ps[hp, 4, c:c + NB], E[x][0:64, j, hp], US[0:64, 2 * j + two, :], start=True, stop=True)
            ins.then_inc(S["inc"], 1)
            for x in range(2):
                for j in range(NPAIR):
                    for two in range(2):
                        hp = slice(two * S5P, (two + 1) * S5P)
                        c = (j % 8) * NSUB
                        ins = pe.matmul(K.ps[hp, 2 * x + j // 8, c:c + NSUB], E[x][:, j, hp], U[:, 2 * j + two, :],
                                        start=True, stop=True)
                ins.then_inc(S["x_pe"], 1)
            pe.wait_ge(S["h0"], 2)
            for gg in [*range(0, S5G, 2), *range(1, S5G, 2)]:
                j, two = gg // 2, gg % 2
                hp = slice(two * S5P, (two + 1) * S5P)
                out = K.ps[0:64, 5 + two, j * NB:(j + 1) * NB]
                pe.matmul(out, G[:, gg, 0:64], US[:, gg, :], start=True, stop=False)
                for x in range(2):
                    ins = pe.matmul(out, F[x][hp, j, 1:5, :].rearrange("p a b -> p (a b)"), h0[x][hp, j, :],
                                    start=False, stop=x == 1)
            ins.then_inc(S["small"], 1)
            pe.wait_ge(S["x_sb"], 2)
            pe.wait_ge(S["h"], 2)
            for m in range(4):
                two, at = m % 2, 8 * (m // 2)
                hp = slice(two * S5P, (two + 1) * S5P)
                for k in range(8):
                    j = at + k
                    gg = 2 * j + two
                    out = K.ps[:, m, k * NSUB:(k + 1) * NSUB]
                    pe.matmul(out, G[:, gg, :], U[:, gg, :], start=True, stop=False)
                    for x in range(2):
                        ins = pe.matmul(out, F[x][hp, j, 1:SUB + 1, :].rearrange("p a b -> p (a b)"),
                                        H[x][hp, j, 0:NSUB], start=False, stop=x == 1)
                ins.then_inc(S["y_pe"], 1)
            pe.wait_ge(S["fin"], 3)
            pe.wait_ge(S["ys_sb"], 2)
            pe.transpose(K.ps[0:32, 6, 0:P], fin_p[:].rearrange("p x j -> p (x j)"), K.ident).then_inc(S["fin_t"], 1)
            for x in range(2):
                ins = pe.transpose(K.ps[:, 7, x * P:(x + 1) * P], fin_s[x][:].rearrange("p b j -> p (b j)"), K.ident)
            ins.then_inc(S["fin_t"], 1)
            pe.wait_ge(S["z_in"], 32)
            pe.wait_ge(S["gelu"], 4)
            pe.wait_ge(S["y_sb"], 4)
            for m in range(4):
                if m >= 2:
                    pe.wait_ge(S["sig"], m - 1)
                for k in range(4):
                    for h in range(2):
                        ins = pe.matmul(K.ps[:, 2 * (m % 2) + h, 0:HT], wg[:, k, m * P:(m + 1) * P],
                                        up[:, k, h * HT:(h + 1) * HT], start=k == 0, stop=k == 3)
                ins.then_inc(S["glu"], 1)

        @block.vector
        def _(dve):
            st = Steps(dve)
            s = S["dve"]
            st(dve.memset(H[0][:, :, 0:1], 0.0), s)
            st(dve.memset(H[1][:, :, 0:1], 0.0), s)
            dve.wait_ge(S["inc"], 1)
            dve.wait_ge(S["h0"], 2)
            l4 = [pw[x][:, :, 4:5].broadcast_to([P, NPAIR, NB]) for x in range(2)]
            f = [fin_s[x][:].rearrange("p b j -> p j b") for x in range(2)]
            cmul(st, dve, s, *f, *l4, h0[0][:], h0[1][:], t8[:])
            for x in range(2):
                dve.tensor_tensor(f[x], K.ps[:, 4, x * P:(x + 1) * P].rearrange("p (j b) -> p j b", b=NB), f[x], ALU.add)\
                    .then_inc(S["fin"], 1)
            dve.wait_ge(S["small"], 1)
            for two in range(2):
                dve.tensor_copy(YS[0:64].rearrange("p (j two) b -> p j two b", two=2)[:, :, two, :],
                                K.ps[0:64, 5 + two, 0:NPAIR * NB].rearrange("p (j b) -> p j b", b=NB)).then_inc(S["ys_sb"], 1)
            dve.wait_ge(S["x_sb"], 2)
            st(dve.tensor_tensor(R[0][:], X[0][:], rot[0][:], ALU.mult), s)
            t = H[1][:, :, 1:NSUB + 1]
            st(dve.tensor_tensor(t, X[1][:], rot[1][:], ALU.mult), s)
            st.sync()
            st(dve.tensor_tensor(R[0][:], R[0][:], t, ALU.add), s)
            st.sync()
            dve.wait_ge(S["rot_i"], 1)
            fl = lambda ap: ap.rearrange("p j c -> p (j c)")
            st(dve.tensor_tensor_scan(fl(X[0][:]), fl(decay[:]), fl(R[0][:]), 0.0, ALU.mult, ALU.add), s)
            st(dve.tensor_tensor_scan(fl(X[1][:]), fl(decay[:]), fl(R[1][:]), 0.0, ALU.mult, ALU.add), S["scan"])
            st.sync()
            h = H[0][:, :, 1:NSUB + 1]
            st(dve.tensor_tensor(h, X[0][:], rot[0][:], ALU.mult), s)
            st(dve.tensor_tensor(R[0][:], X[1][:], rot[1][:], ALU.mult), s)
            st.sync()
            st(dve.tensor_tensor(h, h, R[0][:], ALU.subtract), S["h"])
            st.sync()
            dve.wait_ge(S["h"], 2)
            st(dve.tensor_copy(fin_p[:, 0, :].unsqueeze(2), H[0][:, :, NSUB:NSUB + 1]), s)
            st.sync()
            dve.tensor_copy(fin_p[:, 1, :].unsqueeze(2), H[1][:, :, NSUB:NSUB + 1]).then_inc(S["fin"], 1)
            dve.wait_ge(S["fin"], 3)
            dve.memset(t8[:, 0:1, 0:1], 0.0).then_inc(S["xfree"], 1)
            dve.wait_ge(S["fin_t"], 1)
            dve.wait_ge(S["xfree"], 1)
            dve.tensor_copy(fin_pt, K.ps[0:32, 6, 0:P]).then_inc(S["fin_sb"], 1)
            dve.wait_ge(S["fin_t"], 2)
            for x in range(2):
                dve.tensor_copy(h_nat[x][:], K.ps[:, 7, x * P:(x + 1) * P]).then_inc(S["fin_sb"], 1)
            for m in range(4):
                dve.wait_ge(S["sig"], m + 1)
                if m >= 2:
                    dve.wait_ge(S["mh"], m - 1)
                    dve.wait_ge(S["ml"], m - 1)
                dve.tensor_tensor(o_glu[m % 2][:], up[:, m, :], sg[m % 2][:], ALU.mult).then_inc(S["o"], 1)
                dve.wait_ge(S["mh"], m + 1)
                dve.tensor_tensor(perm(K.xl[:, 4 + m, 0:LP], SUB, NSUB), natural(o_glu[m % 2], 0, LP, SUB, NSUB),
                                  perm(K.xh[:, 4 + m, 0:LP].bitcast(F32), SUB, NSUB), ALU.subtract)
                dve.tensor_tensor(perm(K.xl[:, 4 + m, LP:T], NT, NB), natural(o_glu[m % 2], LP, T, NT, NB),
                                  perm(K.xh[:, 4 + m, LP:T].bitcast(F32), NT, NB), ALU.subtract).then_inc(S["ml"], 1)

        @block.gpsimd
        def _(pool):
            st = Steps(pool)
            s = S["pool"]
            tv = tp[:].rearrange("p (j c) -> p j c", c=NSUB)
            pool.wait_ge(S["x_sb"], 2)
            st(pool.tensor_tensor(R[1][:], X[1][:], rot[0][:], ALU.mult), s)
            st(pool.tensor_tensor(tv, X[0][:], rot[1][:], ALU.mult), s)
            st.sync()
            st(pool.tensor_tensor(R[1][:], R[1][:], tv, ALU.subtract), S["rot_i"])
            pool.wait_ge(S["scan"], 1)
            h = H[1][:, :, 1:NSUB + 1]
            st.sync()
            st(pool.tensor_tensor(h, X[1][:], rot[0][:], ALU.mult), s)
            st(pool.tensor_tensor(tv, X[0][:], rot[1][:], ALU.mult), s)
            st.sync()
            pool.tensor_tensor(h, h, tv, ALU.add).then_inc(S["h"], 1)


def even_out_dmas(K):
    w = K.I["w_out_even"][0]
    va = w[0:512].rearrange("(two c d) (m x) -> m two d c x", two=2, d=HD, x=P)
    vs = w[512:D].rearrange("(k p) (m x) -> m p k x", p=P, x=P)

    def dmas(s, i):
        m = i * 2 + s
        out = []
        for two in range(2):
            src = va[m, two] if isinstance(m, int) else va[bass.ds(m, 1), two].rearrange("a d c x -> d (a c) x")
            out.append((K.wraw[s][two * HD:(two + 1) * HD, 0:4, :], src))
        src = vs[m] if isinstance(m, int) else vs[bass.ds(m, 1)].rearrange("a p k x -> p (a k) x")
        return out + [(K.wraw[s][:, 4:8, :], src)]
    return dmas


def phase_attention(K):
    nc, I, O, sem, ps = K.nc, K.I, K.O, K.sem, K.ps
    proj = K.proj
    a = Region(nc, K.panels_at)
    kc_in = a("kc_in", [P, NB, P])
    vc = a("vc", [P, NB, P])
    kc = a("kc", [P, NB, P])
    band = a("band", [P, 2 * P])
    sband = a("sband", [P, NB * WIN + LS])
    v_nat = a("v_nat", [P, 5, P])
    k_nat = a("k_nat", [P, 2, P])
    r = Region(nc, K.scratch_at + 10 * T * 4)
    assert a.at <= K.scratch_at
    sqb = [r(f"at_sq{x}", [P, T]) for x in range(2)]
    inv = [r(f"at_inv{x}", [P, T]) for x in range(2)]
    qn = [r(f"at_qn{x}", [P, T]) for x in range(2)]
    qc = [r(f"at_qc{x}", [P, T]) for x in range(2)]
    rs = [r(f"at_rs{x}", [P, T]) for x in range(2)]
    g_qk = r("g_qk", [P, 2])
    qs = r("qs", [P, QG, LS])
    nsink = r("nsink", [P, QH])
    nsink_s = r("nsink_s", [P, KVH])
    pm = [r(f"at_p{x}", [P, QG, 2 * P]) for x in range(2)]
    pt = [r(f"at_pt{x}", [P, 2, QG * P]) for x in range(2)]
    pms = [r(f"at_ps{x}", [P, NB * WIN + LS]) for x in range(2)]
    pts = [r(f"at_pts{x}", [P, NB, P]) for x in range(2)]
    ptn = [r(f"at_ptn{x}", [LS, P]) for x in range(2)]
    UN = 10
    mx, nm, dk, es, den = (r("at_" + n, [P, UN, QG]) for n in ("mx", "nm", "dk", "es", "den"))
    assert r.at <= 229368
    S = {n: sem("att_" + n) for n in ("in", "cache", "sq", "ssq", "var", "inv", "rt", "qn", "swap", "qc", "rs", "rope",
                                      "kt", "kc", "ktake", "s_pe", "mask", "mx", "nm", "dk", "exp", "es", "den", "rd", "p",
                                      "t_pe", "pt_a", "pt_d", "pv", "oh", "ol", "out", "sink", "qs")}
    ones64, swap, cos, sin = (K.table(x) for x in ("head_ones", "rope_swap", "rope_cos", "rope_sin"))

    units = [(i, kv) for i in range(4) for kv in range(KVH)]

    def rows(kv):
        return slice(kv * HD, (kv + 1) * HD)

    with nc.Block() as block:
        @block.sync
        def _(sp):
            for x, n in enumerate(("q_norm", "k_norm")):
                for two in range(2):
                    sp.dma_start(g_qk[rows(two), x:x + 1], I[n].rearrange("a d -> d a")).then_inc(S["in"], 16)
            sp.dma_start(nsink[:], I["attn_sinks"][0].partition_broadcast(P)).then_inc(S["in"], 16)
            sv = I["attn_sinks"].rearrange("a (kv c) -> a c kv", c=QG)
            for c in range(QG):
                sp.dma_start(nsink_s[c * LS:(c + 1) * LS, :], sv[0, c].partition_broadcast(LS),
                             allow_slow_non_contiguous=True).then_inc(S["in"], 16)
            sp.dma_start(band[:], K.table_dram("band")).then_inc(S["in"], 16)
            sp.dma_start(kc_in[:], I["cache_k"][0].rearrange("b w h d -> w b (h d)")).then_inc(S["cache"], 16)
            sp.dma_start(vc[:], I["cache_v"][0].rearrange("b w h d -> w b (h d)")).then_inc(S["cache"], 16)
            sp.dma_start(sband[:], K.table_dram("sample_band")).then_inc(S["cache"], 16)
            for o, x in ((9, "cache_k"), (10, "cache_v")):
                sp.dma_start(O[o][0, :, 0:WIN - NT], I[x][0, :, NT:WIN]).then_inc(S["out"], 16)
            sp.wait_ge(S["ktake"], 3)
            sp.dma_start(O[2][0, 0].rearrange("w h d -> w (h d)"), k_nat[:, 0, :]).then_inc(S["out"], 16)
            sp.dma_start(O[3][0, 0].rearrange("w h d -> w (h d)"), v_nat[:, 3, :]).then_inc(S["out"], 16)
            for b in range(NB):
                for o, t in ((9, k_nat[b * NT:(b + 1) * NT, 1, :]), (10, v_nat[b * NT:(b + 1) * NT, 4, :])):
                    sp.dma_start(O[o][0, b, WIN - NT:WIN].rearrange("w h d -> w (h d)"), t).then_inc(S["out"], 16)
            sp.wait_ge(S["out"], 16 * 20)

        @block.tensor
        def _(pe):
            for c in range(5):
                pe.wait_ge(S["sq"], c + 1)
                if c:
                    pe.wait_ge(S["var"], c)
                for h in range(2):
                    ins = pe.matmul(ps[:, h, 0:HT], ones64, sqb[c % 2][:, h * HT:(h + 1) * HT], start=True, stop=True)
                ins.then_inc(S["ssq"], 1)
                if c == 0:
                    for n in range(5):
                        w = P if n < 4 else LS
                        bank = 4 + n // 4
                        ins = pe.transpose(ps[0:w, bank, (n % 4) * P:(n % 4 + 1) * P], proj[:, 5, n * P:n * P + w], K.ident)
                    ins.then_inc(S["kt"], 1)
                    pe.wait_ge(S["cache"], 48)
                    for b in range(NB):
                        ins = pe.transpose(ps[:, 6 + b // 4, (b % 4) * P:(b % 4 + 1) * P], kc_in[:, b, :], K.ident)
                    ins.then_inc(S["kc"], 1)
                pe.wait_ge(S["qn"], c + 1)
                if c:
                    pe.wait_ge(S["rs"], c)
                for h in range(2):
                    ins = pe.matmul(ps[:, 2 + h, 0:HT], swap, qn[c % 2][:, h * HT:(h + 1) * HT], start=True, stop=True)
                ins.then_inc(S["swap"], 1)
            pe.wait_ge(S["rope"], 5)
            pe.wait_ge(S["ktake"], 2)
            for n in range(2):
                w, at = (P, 3 * P) if n == 0 else (LS, LP)
                ins = pe.transpose(ps[0:w, 4, n * P:(n + 1) * P], proj[:, 4, at:at + w], K.ident)
            ins.then_inc(S["kt"], 1)

            def scores(u):
                i, kv = units[u]
                if u >= 2:
                    pe.wait_ge(S["mask"], u - 1)
                lo = (i - 1) * P if i else 0
                at = 0 if i else P
                for c in range(QG):
                    ins = pe.matmul(ps[:, 2 * kv + c // 2, (c % 2) * 2 * P + at:(c % 2 + 1) * 2 * P],
                                    proj[rows(kv), c, i * P:(i + 1) * P], proj[rows(kv), 4, lo:(i + 1) * P],
                                    start=True, stop=True)
                ins.then_inc(S["s_pe"], 1)

            def finish(u):
                i, kv = units[u]
                pe.wait_ge(S["p"], u + 1)
                if u:
                    pe.wait_ge(S["pt_a"], u)
                    pe.wait_ge(S["pt_d"], u)
                else:
                    pe.wait_ge(S["ktake"], 3)
                for kb in ((0, 1) if i else (1,)):
                    for c in range(QG):
                        ins = pe.transpose(ps[:, 4 + kb, c * P:(c + 1) * P], pm[kv][:, c, kb * P:(kb + 1) * P], K.ident)
                ins.then_inc(S["t_pe"], 1)
                pe.wait_ge(S["pt_a"], u + 1)
                pe.wait_ge(S["pt_d"], u + 1)
                if u >= 2:
                    pe.wait_ge(S["ol"], u - 1)
                for kb in ((0, 1) if i else (1,)):
                    ins = pe.matmul(ps[rows(kv), 6 + kv, :], v_nat[:, i - 1 + kb, rows(kv)], pt[kv][:, kb, :],
                                    start=kb == 1 and not i or kb == 0, stop=kb == 1)
                ins.then_inc(S["pv"], 1)
            def sample_scores(kv):
                pe.wait_ge(S["mask"], 8)
                pe.wait_ge(S["ol"], 7 + kv)
                q = qs[rows(kv), :, :].rearrange("p c t -> p (c t)")
                for half in range(2):
                    pe.matmul(ps[:, 2 * kv + half, :], q, kc[rows(kv), 4 * half:4 * half + 4, :].rearrange("p b w -> p (b w)"),
                              start=True, stop=True)
                pe.matmul(ps[:, 6 + kv, 0:LS], q, proj[rows(kv), 4, LP:T], start=True, stop=True).then_inc(S["s_pe"], 1)
            pe.wait_ge(S["rs"], 5)
            scores(0)
            for u in range(8):
                if u + 1 < 8:
                    scores(u + 1)
                else:
                    pe.wait_ge(S["qs"], 1)
                    sample_scores(0)
                finish(u)
            sample_scores(1)
            for kv in range(KVH):
                u = 8 + kv
                pe.wait_ge(S["p"], u + 1)
                pe.wait_ge(S["pt_a"], u)
                pe.wait_ge(S["pt_d"], u)
                for b in range(NB):
                    pe.transpose(ps[:, 4 + b // 4, (b % 4) * P:(b % 4 + 1) * P], pms[kv][:, b * P:(b + 1) * P], K.ident)
                pe.transpose(ps[0:LS, 2 * kv, 0:P], pms[kv][:, NB * P:], K.ident).then_inc(S["t_pe"], 1)
                pe.wait_ge(S["pt_a"], u + 1)
                pe.wait_ge(S["pt_d"], u + 1)
                out = ps[rows(kv), 6 + kv, P:2 * P]
                for b in range(NB):
                    pe.matmul(out, vc[:, b, rows(kv)], pts[kv][:, b, :], start=b == 0, stop=False)
                pe.matmul(out, v_nat[0:LS, 4, rows(kv)], ptn[kv][:], start=False, stop=True).then_inc(S["pv"], 1)

        @block.scalar
        def _(act):
            def square(c):
                if c >= 2:
                    act.wait_ge(S["ssq"], c - 1)
                act.activation(sqb[c % 2][:], proj[:, c, :], ACT.Square).then_inc(S["sq"], 1)
            square(0)
            square(1)
            for c in range(5):
                act.wait_ge(S["inv"], c + 1)
                act.activation(inv[c % 2][:], inv[c % 2][:], ACT.Sqrt).then_inc(S["rt"], 1)
                if c + 2 < 5:
                    square(c + 2)
                if c == 0:
                    act.wait_ge(S["kt"], 1)
                    act.copy(v_nat[:, 0:4, :].rearrange("p n x -> p (n x)"), ps[:, 4, :])
                    act.copy(v_nat[0:LS, 4, :], ps[0:LS, 5, 0:P]).then_inc(S["ktake"], 1)
                    act.wait_ge(S["kc"], 1)
                    act.copy(kc[:].rearrange("p (a b) w -> p a (b w)", a=2), ps[:, 6:8, :]).then_inc(S["ktake"], 1)

            def exps(u):
                act.wait_ge(S["nm"], u + 1)
                if u < 8:
                    i, kv = units[u]
                    ks = slice(0, 2 * P) if i else slice(P, 2 * P)
                    for c in range(QG):
                        ins = act.activation(pm[kv][:, c, ks], pm[kv][:, c, ks], ACT.Exp, bias=nm[:, u, c:c + 1],
                                             accum_out=den[:, u, c:c + 1])
                else:
                    ins = act.activation(pms[u - 8][:], pms[u - 8][:], ACT.Exp, bias=nm[:, u, 0:1],
                                         accum_out=den[:, u, 0:1])
                ins.then_inc(S["exp"], 1)
                n = QG if u < 8 else 1
                act.wait_ge(S["dk"], u + 1)
                act.activation(es[:, u, 0:n], dk[:, u, 0:n], ACT.Exp).then_inc(S["es"], 1)

            def take_out(u):
                act.wait_ge(S["t_pe"], u + 1)
                if u >= 8:
                    kv = u - 8
                    act.copy(pts[kv][:, 0:4, :].rearrange("p b w -> p (b w)"), ps[:, 4, :])
                    act.copy(ptn[kv][:], ps[0:LS, 2 * kv, 0:P]).then_inc(S["pt_a"], 1)
                    act.wait_ge(S["pv"], u + 1)
                    act.copy(K.xh[rows(kv), 0:QG, LP:T],
                             ps[rows(kv), 6 + kv, P:2 * P].rearrange("p (c t) -> p c t", c=QG)).then_inc(S["oh"], 1)
                    return
                i, kv = units[u]
                if i:
                    ins = act.copy(pt[kv][:, 0, :], ps[:, 4, :])
                else:
                    ins = act.copy(es[:, u, :], es[:, u, :])
                ins.then_inc(S["pt_a"], 1)
                act.wait_ge(S["pv"], u + 1)
                act.copy(K.xh[rows(kv), 0:QG, i * P:(i + 1) * P],
                         ps[rows(kv), 6 + kv, :].rearrange("p (c t) -> p c t", c=QG)).then_inc(S["oh"], 1)
            exps(0)
            for u in range(UN):
                if u + 1 < UN:
                    exps(u + 1)
                take_out(u)

        @block.vector
        def _(dve):
            dve.wait_ge(S["in"], 16 * 10)
            dve.tensor_scalar(nsink[:], nsink[:], -1.0, None, ALU.mult).then_inc(S["sink"], 1)
            dve.tensor_scalar(nsink_s[:], nsink_s[:], -1.0, None, ALU.mult).then_inc(S["sink"], 1)
            for c in range(5):
                dve.wait_ge(S["ssq"], c + 1)
                t = inv[c % 2]
                dve.tensor_scalar(halves(t[:]), ps[:, 0:2, 0:HT], 1.0 / HD, EPS, ALU.mult, ALU.add).then_inc(S["var"], 1)
                dve.wait_ge(S["var"], c + 1)
                dve.reciprocal(t[:], t[:]).then_inc(S["inv"], 1)
                dve.wait_ge(S["rt"], c + 1)
                if c >= 2:
                    dve.wait_ge(S["swap"], c - 1)
                    dve.wait_ge(S["qc"], c - 1)
                g = g_qk[:, 0:1] if c < 4 else g_qk[:, 1:2]
                dve.scalar_tensor_tensor(qn[c % 2][:], proj[:, c, :], g, t[:], ALU.mult, ALU.mult).then_inc(S["qn"], 1)
                dve.wait_ge(S["swap"], c + 1)
                if c >= 2:
                    dve.wait_ge(S["rope"], c - 1)
                dve.tensor_tensor(halves(rs[c % 2][:]), ps[:, 2:4, 0:HT], halves(sin), ALU.mult).then_inc(S["rs"], 1)
                dve.wait_ge(S["rs"], c + 1)
                dve.wait_ge(S["qc"], c + 1)
                dve.wait_ge(S["qn"], c + 1)
                dve.tensor_tensor(proj[:, c, :], qc[c % 2][:], rs[c % 2][:], ALU.add).then_inc(S["rope"], 1)
            dve.wait_ge(S["kt"], 2)
            dve.tensor_copy(k_nat[:, 0, :], ps[:, 4, 0:P])
            dve.tensor_copy(k_nat[0:LS, 1, :], ps[0:LS, 4, P:2 * P]).then_inc(S["ktake"], 1)
            dve.wait_ge(S["sink"], 2)

            def masked(u):
                dve.wait_ge(S["s_pe"], u + 1)
                if u >= 2:
                    dve.wait_ge(S["t_pe"], u - 1)
                if u < 8:
                    i, kv = units[u]
                    ks = slice(0, 2 * P) if i else slice(P, 2 * P)
                    for h in range(2):
                        sc = ps[:, 2 * kv + h, :].rearrange("p (c k) -> p c k", c=2)[:, :, ks]
                        ins = dve.scalar_tensor_tensor(pm[kv][:, 2 * h:2 * h + 2, ks], sc, HD ** -0.5,
                                                       band[:, ks].unsqueeze(1).broadcast_to([P, 2, ks.stop - ks.start]),
                                                       ALU.mult, ALU.add)
                    ins.then_inc(S["mask"], 1)
                    src, n, ns = pm[kv][:, :, ks], QG, nsink[:, kv * QG:(kv + 1) * QG]
                else:
                    kv = u - 8
                    for h in range(2):
                        dve.scalar_tensor_tensor(pms[kv][:, h * 512:(h + 1) * 512], ps[:, 2 * kv + h, :], HD ** -0.5,
                                                 sband[:, h * 512:(h + 1) * 512], ALU.mult, ALU.add)
                    dve.scalar_tensor_tensor(pms[kv][:, 1024:], ps[:, 6 + kv, 0:LS], HD ** -0.5,
                                             sband[:, 1024:], ALU.mult, ALU.add).then_inc(S["mask"], 1)
                    src, n, ns = pms[kv][:], 1, nsink_s[:, kv:kv + 1]
                dve.wait_ge(S["mask"], u + 1)
                dve.tensor_reduce(mx[:, u, 0:n], src, AX.X, ALU.max).then_inc(S["mx"], 1)
                dve.wait_ge(S["mx"], u + 1)
                dve.scalar_tensor_tensor(nm[:, u, 0:n], mx[:, u, 0:n], -1.0, ns, ALU.mult, ALU.min).then_inc(S["nm"], 1)
                dve.wait_ge(S["nm"], u + 1)
                dve.tensor_tensor(dk[:, u, 0:n], nm[:, u, 0:n], ns, ALU.subtract).then_inc(S["dk"], 1)

            def normed(u):
                dve.wait_ge(S["exp"], u + 1)
                dve.wait_ge(S["es"], u + 1)
                n = QG if u < 8 else 1
                dve.tensor_tensor(den[:, u, 0:n], den[:, u, 0:n], es[:, u, 0:n], ALU.add).then_inc(S["den"], 1)
                dve.wait_ge(S["den"], u + 1)
                dve.reciprocal(den[:, u, 0:n], den[:, u, 0:n]).then_inc(S["rd"], 1)
                dve.wait_ge(S["rd"], u + 1)
                if u < 8:
                    i, kv = units[u]
                    ks = slice(0, 2 * P) if i else slice(P, 2 * P)
                    v = pm[kv][:, :, ks]
                    dve.tensor_tensor(v, v, den[:, u, :].unsqueeze(2).broadcast_to([P, QG, ks.stop - ks.start]), ALU.mult)\
                        .then_inc(S["p"], 1)
                else:
                    v = pms[u - 8][:]
                    dve.tensor_scalar(v, v, den[:, u, 0:1], None, ALU.mult).then_inc(S["p"], 1)

            def take_out(u):
                dve.wait_ge(S["t_pe"], u + 1)
                if u < 8:
                    i, kv = units[u]
                    dve.tensor_copy(pt[kv][:, 1, :], ps[:, 5, :]).then_inc(S["pt_d"], 1)
                    cols, src = slice(i * P, (i + 1) * P), ps[rows(kv), 6 + kv, :]
                else:
                    kv = u - 8
                    dve.tensor_copy(pts[kv][:, 4:8, :].rearrange("p b w -> p (b w)"), ps[:, 5, :]).then_inc(S["pt_d"], 1)
                    cols, src = slice(LP, T), ps[rows(kv), 6 + kv, P:2 * P]
                dve.wait_ge(S["oh"], u + 1)
                dve.tensor_tensor(K.xl[rows(kv), 0:QG, cols], src.rearrange("p (c t) -> p c t", c=QG),
                                  K.xh[rows(kv), 0:QG, cols].bitcast(F32), ALU.subtract).then_inc(S["ol"], 1)
            masked(0)
            for u in range(UN):
                if u + 1 < UN:
                    masked(u + 1)
                normed(u)
                take_out(u)

        @block.gpsimd
        def _(pool):
            for c in range(5):
                pool.wait_ge(S["qn"], c + 1)
                if c >= 2:
                    pool.wait_ge(S["rope"], c - 1)
                pool.tensor_tensor(qc[c % 2][:], qn[c % 2][:], cos, ALU.mult).then_inc(S["qc"], 1)
            pool.wait_ge(S["rope"], 5)
            pool.tensor_copy(qs[:], proj[:, 0:QG, LP:T]).then_inc(S["qs"], 1)


def phase_odd_in(K):
    nc, I, sem = K.nc, K.I, K.sem
    K.clear_sems(("s5", "att_"))
    r = Region(nc, K.scratch_at)
    proj = K.projo = r("projo", [P, 24, T])
    gates = K.gates = r("gates", [MH, 2, T])
    K.odd_scratch = r.at
    w_in = I["w_in_odd"][0]
    g = K.product(12, DC, 2)
    g_gate = K.product(1, DC, 2, slots=(0,))
    w_gate = w_in[:, 3072:ODD_IN].rearrange("(k p) (two c) -> two p k c", p=P, two=2)
    k_scaled = sem("k_scaled")

    def gate_dmas(s, i):
        return [(K.wraw[0][:, 0:DC, 32 * two:32 * two + MH], w_gate[two]) for two in range(2)]

    with nc.Block() as block:
        @block.sync
        def _(sp):
            load_panels(K, sp, g, plain_dmas(K, w_in[:, 0:3072], DC))
            load_panels(K, sp, g_gate, gate_dmas)

        @block.tensor
        def _(pe):
            rms_pe(K, pe, 2)
            multiply_panels(K, pe, g, K.xh, K.xl, wait_x(K, pe, 2))
            multiply_panels(K, pe, g_gate, K.xh, K.xl)

        @block.vector
        def _(dve):
            split_x_lo(K, dve, 2)
            rms_dve(K, dve, 2)
            dve.wait_ge(sem("rms_ready"), 3)

            def evac(s, i):
                take(K, dve, g, s, i)
                dve.tensor_tensor(halves(chunk(proj, i * 2 + s)), K.acc[s], halves(K.rstd[:]), ALU.mult)\
                    .then_inc(K.acc_free[s], 1)
            split_and_take(K, dve, g, split_lo, evac)

            def evac_gates(s, i):
                take(K, dve, g_gate, s, i)
                dve.tensor_tensor(halves(gates[:, 0, :]), K.ps[0:MH, 0:2, 0:HT], halves(K.rstd[0:MH, :]), ALU.mult)
                dve.tensor_tensor(halves(gates[:, 1, :]), K.ps[32:32 + MH, 0:2, 0:HT], halves(K.rstd[32:32 + MH, :]),
                                  ALU.mult).then_inc(K.acc_free[0], 1)
            split_and_take(K, dve, g_gate, split_lo, evac_gates)

        @block.scalar
        def _(act):
            split_x_hi(K, act, 2)
            rms_act(K, act, 2)
            split_and_take(K, act, g, split_hi)
            split_and_take(K, act, g_gate, split_hi)

        @block.gpsimd
        def _(pool):
            for s in range(2):
                pool.wait_ge(K.acc_free[s], g.n[s] + 4)
            pool.tensor_scalar(proj[:, 4:8, :], proj[:, 4:8, :], DK ** -0.5, None, ALU.mult).then_inc(k_scaled, 1)


def phase_mlstm(K):
    nc, I, O, sem, ps, proj, gates = K.nc, K.I, K.O, K.sem, K.ps, K.projo, K.gates
    a = Region(nc, K.panels_at)
    b = Region(nc, K.odd_scratch)
    NC = LP // P
    causal = b("ml_causal", [P, P])
    s_causal, s_last = b("ml_s_causal", [LS, LS]), b("ml_s_last", [LS, LS])
    in_batch = b("ml_in_batch", [LS, NB])
    sel = b("ml_sel", [MH, MH * P])
    keep = b("ml_keep", [MH, T])
    bias = b("ml_bias", [MH, 2])
    m0 = b("ml_m0", [MH, NB])
    gain = b("ml_gain", [P, MH])
    n0_nat = b("ml_n0_nat", [LS, P])
    c0 = b("ml_c0", [P, NB * 4, DV])
    e, lf, cum, m, rr, cc, wi = (b(f"ml_g_{x}", [MH, T]) for x in "elbmrcw")
    mp = b("ml_mp", [MH, NC + NB])
    ct = b("ml_ct", [P, NC + 1, MH])
    cfin = b("ml_cfin", [P, 4, 2 * P])
    dec = b("ml_dec", [P, 4, NC])
    wt = [a(f"ml_wt{x}", [P, LP]) for x in range(2)]
    at = [a(f"ml_at{x}", [P, LP]) for x in range(2)]
    v_nat = [a(f"ml_v_nat{x}", [P, NC, P]) for x in range(2)]
    k_nat = [a(f"ml_k_nat{x}", [P, NC, P]) for x in range(2)]
    ksc = [a(f"ml_ksc{x}", [P, NC, DK]) for x in range(2)]
    mo = [a(f"ml_mo{x}", [P, LP]) for x in range(2)]
    sqn = [a(f"ml_sqn{x}", [P, LP]) for x in range(2)]
    assert a.at <= K.scratch_at, (a.at, K.scratch_at)
    qw = [b(f"ml_qw{x}", [P, LP]) for x in range(2)]
    cn = b("ml_cn", [P, NC - 1, 2 * P])
    em = a("ml_em", [P, LP])
    sqd = a("ml_sqd", [P, LP])
    ln_eps = b("ml_ln_eps", [P, 1])
    og = a("ml_og", [P, LP])
    assert b.at <= 229368, b.at
    S = {n: sem("ml_" + n) for n in ("in", "c_in", "gd", "ga", "gates", "ct_pe", "ct", "sig", "win", "qw", "kt", "knat", "wpre",
                                     "w", "s", "at", "vt", "vnat", "ksc", "dc", "cn", "nd", "mb", "em", "sqn",
                                     "d", "d2", "msq", "var", "inv", "rs", "og", "out", "hi", "lo", "out_c")}

    def rows(h):
        return slice((h % 2) * DK, (h % 2 + 1) * DK)

    def sel_of(h, n=P):
        return sel[:, h * P:h * P + n]

    with nc.Block() as block:
        @block.sync
        def _(sp):
            for t, nm in ((causal, "causal"), (s_causal, "sample_causal"), (s_last, "sample_last"),
                          (in_batch, "in_batch"), (sel, "head_sel"), (keep, "keep")):
                sp.dma_start(t[:], K.table_dram(nm, t.shape[0])).then_inc(S["in"], 16)
            for n, nm in enumerate(("ml_b_i", "ml_b_f")):
                sp.dma_start(bias[:, n:n + 1], I[nm][0].unsqueeze(1)).then_inc(S["in"], 16)
            sp.dma_start(m0[:], I["state_mlstm_m"][0].rearrange("b h -> h b"), allow_slow_non_contiguous=True)\
                .then_inc(S["in"], 16)
            sp.dma_start(gain[:], I["ml_out_norm"][0].rearrange("(h p) -> p h", p=P), allow_slow_non_contiguous=True)\
                .then_inc(S["in"], 16)
            sp.dma_start(n0_nat[:], I["state_mlstm_n"][0].rearrange("b (j two) d -> (b j) (two d)", two=2))\
                .then_inc(S["c_in"], 16)
            sp.dma_start(c0[:], I["state_mlstm_c"][0].rearrange("b (j two) d v -> (two d) (b j) v", two=2))\
                .then_inc(S["c_in"], 16)
            for h in range(MH):
                sp.wait_ge(S["cn"], NC * (h + 1))
                sp.dma_start(O[6][0, 0, h], cfin[rows(h), h // 2, 0:P]).then_inc(S["out_c"], 16)
            sp.wait_ge(S["gates"], 1)
            sp.dma_start(O[8][0, 0].unsqueeze(1), m[:, LP - 1:LP]).then_inc(S["out_c"], 16)
            sp.dma_start(O[15][0].rearrange("b h -> h b"), m[:, LP + NT - 1:T:NT], allow_slow_non_contiguous=True)\
                .then_inc(S["out_c"], 16)
            sp.wait_ge(S["out_c"], 16 * (MH + 2))
            sp.wait_ge(S["c_in"], 32)

        @block.tensor
        def _(pe):
            pe.wait_ge(S["in"], 161)
            pe.wait_ge(S["gates"], 1)
            for i in range(NC + 1):
                w = P if i < NC else LS
                ins = pe.transpose(ps[0:w, 2, i * MH:(i + 1) * MH], cc[:, i * P:i * P + w], K.ident[0:MH, 0:MH])
            ins.then_inc(S["ct_pe"], 1)
            pe.wait_ge(S["gates"], 2)

            def first(h):
                j, two = h // 2, h % 2
                if two == 0:
                    if h:
                        pe.wait_ge(S["em"], h - 1)
                        pe.wait_ge(S["cn"], NC * h)
                    pe.matmul(ps[:, 7, :], sel[:, h * P + DK:h * P + DK + P], wi[:, 0:LP], start=True, stop=True)\
                        .then_inc(S["win"], 1)
                    for i in range(NC):
                        ins = pe.transpose(ps[:, 3, i * P:(i + 1) * P], proj[:, 4 + j, i * P:(i + 1) * P], K.ident)
                    ins.then_inc(S["kt"], 1)
                if h:
                    pe.wait_ge(S["w"], h)
                    pe.wait_ge(S["at"], h)
                    pe.wait_ge(S["vnat"], h)
                else:
                    pe.wait_ge(S["ct"], 1)
                out = ps[:, 0, :].rearrange("p (i t) -> p i t", i=NC)
                pe.matmul(ps[:, 0, :], sel_of(h), rr[:, 0:LP], start=True, stop=False)
                pe.matmul(out, K.ident, causal[:].unsqueeze(1).broadcast_to([P, NC, P]), start=False, stop=True)\
                    .then_inc(S["wpre"], 1)
                for i in range(NC):
                    ts = slice(i * P, (i + 1) * P)
                    ins = pe.matmul(ps[:, 1, ts], proj[rows(h), 4 + j, ts], proj[rows(h), j, ts], start=True, stop=True)
                ins.then_inc(S["s"], 1)
                for i in range(NC):
                    ins = pe.transpose(ps[:, 2, i * P:(i + 1) * P], proj[:, 8 + h, i * P:(i + 1) * P], K.ident)
                ins.then_inc(S["vt"], 1)
                pe.wait_ge(S["ksc"], h + 1)
                pe.wait_ge(S["vnat"], h + 1)
                if h:
                    pe.wait_ge(S["cn"], NC * h)
                for i in range(NC):
                    c = (i % 2) * 2 * P
                    pe.matmul(ps[rows(h), 3 + i // 2, c:c + P], ksc[two][:, i, :], v_nat[two][:, i, :], start=True, stop=True)
                    ins = pe.matmul(ps[rows(h), 3 + i // 2, c + P:c + 2 * P], ksc[two][:, i, :], K.ones[:], start=True, stop=True)
                ins.then_inc(S["dc"], 1)

            def second(h):
                j, two = h // 2, h % 2
                pe.wait_ge(S["at"], h + 1)
                pe.wait_ge(S["cn"], NC * h + NC - 1)
                pe.wait_ge(S["qw"], 2 * min(4, (h + 1) // 2 + 1))
                if h:
                    pe.wait_ge(S["em"], h)
                    pe.wait_ge(S["var"], h)
                pe.matmul(ps[:, 7, :], sel_of(h), m[:, 0:LP], start=True, stop=True).then_inc(S["mb"], 1)
                pe.matmul(ps[:, 6, :], K.ones[:], at[two][:], start=True, stop=False)
                for i in range(1, NC):
                    ts = slice(i * P, (i + 1) * P)
                    ins = pe.matmul(ps[:, 6, ts], cn[rows(h), i - 1, P:2 * P], qw[j % 2][rows(h), ts], start=False, stop=i == NC - 1)
                ins.then_inc(S["nd"], 1)
                if h:
                    pe.wait_ge(S["out"], h)
                    pe.wait_ge(S["sqn"], h)
                for i in range(NC):
                    ts = slice(i * P, (i + 1) * P)
                    ins = pe.matmul(ps[:, 5, ts], v_nat[two][:, i, :], at[two][:, ts], start=True, stop=i == 0)
                    if i:
                        ins = pe.matmul(ps[:, 5, ts], cn[rows(h), i - 1, 0:P], qw[j % 2][rows(h), ts], start=False, stop=True)
                ins.then_inc(S["nd"], 1)
                pe.wait_ge(S["sqn"], h + 1)
                pe.wait_ge(S["d2"], h + 1)
                pe.matmul(ps[:, 6, :], K.ones[:], sqn[two][:], start=True, stop=True).then_inc(S["msq"], 1)
            first(0)
            for h in range(MH):
                if h + 1 < MH:
                    first(h + 1)
                second(h)

        @block.scalar
        def _(act):
            act.wait_ge(S["in"], 161)
            act.wait_ge(S["gd"], 2)
            act.activation(e[:], e[:], ACT.Exp).then_inc(S["ga"], 1)
            act.wait_ge(S["ga"], 1)
            act.activation(e[:], e[:], ACT.Ln, bias=K.ones[0:MH, 0:1]).then_inc(S["ga"], 1)
            act.wait_ge(S["gates"], 1)
            act.activation(wi[:], wi[:], ACT.Exp).then_inc(S["gates"], 1)
            for h in range(MH):
                act.activation(proj[:, 16 + h, :], proj[:, 16 + h, :], ACT.Sigmoid).then_inc(S["sig"], 1)

            def first(h):
                j, two = h // 2, h % 2
                if two == 0:
                    act.wait_ge(S["kt"], j + 1)
                    if j >= 2:
                        act.wait_ge(S["ksc"], h - 2)
                    act.copy(k_nat[j % 2][:].rearrange("p i x -> p (i x)"), ps[:, 3, :]).then_inc(S["knat"], 1)
                act.wait_ge(S["wpre"], h + 1)
                if h >= 2:
                    act.wait_ge(S["at"], h - 1)
                    act.wait_ge(S["ksc"], h - 1)
                else:
                    act.wait_ge(S["ct"], 1)
                for i in range(NC):
                    ts = slice(i * P, (i + 1) * P)
                    ins = act.activation(wt[two][:, ts], ps[:, 0, ts], ACT.Exp, bias=ct[:, i, h:h + 1])
                ins.then_inc(S["w"], 1)
                act.wait_ge(S["vt"], h + 1)
                if h >= 2:
                    act.wait_ge(S["nd"], 2 * (h - 1))
                act.copy(v_nat[two][:].rearrange("p i x -> p (i x)"), ps[:, 2, :]).then_inc(S["vnat"], 1)

            def high(h):
                act.wait_ge(S["out"], h + 1)
                act.copy(K.xh[:, h, 0:LP], mo[h % 2][:]).then_inc(S["hi"], 1)

            def second(h):
                act.wait_ge(S["mb"], h + 1)
                if h:
                    act.wait_ge(S["d"], h)
                    act.wait_ge(S["rs"], h)
                act.activation(em[:], ps[:, 7, :], ACT.Exp, scale=-2.0, bias=ln_eps[:]).then_inc(S["em"], 1)
                act.wait_ge(S["nd"], 2 * h + 1)
                act.activation(sqd[:], ps[:, 6, :], ACT.Square, scale=EPS ** 0.5).then_inc(S["d2"], 1)
                act.wait_ge(S["nd"], 2 * h + 2)
                if h >= 2:
                    act.wait_ge(S["msq"], h - 1)
                act.activation(sqn[h % 2][:], ps[:, 5, :], ACT.Square).then_inc(S["sqn"], 1)
                act.wait_ge(S["inv"], h + 1)
                act.activation(og[:], em[:], ACT.Sqrt).then_inc(S["rs"], 1)
            first(0)
            for h in range(MH):
                if h + 1 < MH:
                    first(h + 1)
                if h:
                    high(h - 1)
                second(h)
            high(MH - 1)

        @block.vector
        def _(dve):
            s = S["gd"]
            st = Steps(dve)
            dve.memset(ln_eps[:], float(np.log(EPS))).then_inc(S["in"], 1)
            dve.wait_ge(S["in"], 161)
            ig, f = gates[:, 0, :], gates[:, 1, :]
            st(dve.tensor_scalar(f, f, bias[:, 1:2], None, ALU.add), s)
            st.sync()
            st(dve.scalar_tensor_tensor(e[:], f, -1.0, f, ALU.mult, ALU.min), s)
            st(dve.tensor_scalar(ig, ig, bias[:, 0:1], None, ALU.add), s)
            dve.wait_ge(S["ga"], 2)
            st.sync()
            st(dve.scalar_tensor_tensor(lf[:], f, 0.0, e[:], ALU.min, ALU.subtract), s)
            st.sync()
            st(dve.tensor_tensor_scan(cum[:], keep[:], lf[:], 0.0, ALU.mult, ALU.add), s)
            st(dve.tensor_tensor_scan(m[:, 0:LP], lf[:, 0:LP], ig[:, 0:LP], 0.0, ALU.add, ALU.max), s)
            for n in range(NB):
                ts = slice(LP + n * NT, LP + (n + 1) * NT)
                st(dve.tensor_tensor_scan(m[:, ts], lf[:, ts], ig[:, ts], m0[:, n:n + 1], ALU.add, ALU.max), s)
            st(dve.memset(mp[:, 0:1], 0.0), s)
            st(dve.tensor_copy(mp[:, NC:NC + NB], m0[:]), s)
            st.sync()
            st(dve.tensor_tensor(rr[:], cum[:], m[:], ALU.subtract), s)
            st(dve.tensor_tensor(cc[:], ig, cum[:], ALU.subtract), s)
            st(dve.tensor_copy(mp[:, 1:NC], m[:, P - 1:LP - P:P]), s)
            st.sync()
            st(dve.tensor_tensor(wi[:, LP:T].rearrange("p (n t) -> p n t", n=NB), rr[:, LP:T].rearrange("p (n t) -> p n t", n=NB),
                                 mp[:, NC:NC + NB].unsqueeze(2).broadcast_to([MH, NB, NT]), ALU.add), s)
            st.sync()
            dve.tensor_tensor(wi[:, 0:LP].rearrange("p (n t) -> p n t", n=NC), rr[:, 0:LP].rearrange("p (n t) -> p n t", n=NC),
                              mp[:, 0:NC].unsqueeze(2).broadcast_to([MH, NC, P]), ALU.add).then_inc(S["gates"], 1)
            dve.wait_ge(S["ct_pe"], 1)
            dve.tensor_copy(ct[:].rearrange("p i h -> p (i h)"), ps[:, 2, 0:(NC + 1) * MH]).then_inc(S["ct"], 1)

            def first(h):
                j, two = h // 2, h % 2
                if two == 0:
                    dve.wait_ge(S["win"], j + 1)
                    if j >= 2:
                        dve.wait_ge(S["nd"], 2 * (h - 2))
                    dve.tensor_copy(dec[:, j, :], ps[:, 7, P - 1:LP:P]).then_inc(S["qw"], 1)
                    dve.tensor_tensor(qw[j % 2][:], ps[:, 7, :], proj[:, j, 0:LP], ALU.mult).then_inc(S["qw"], 1)
                dve.wait_ge(S["w"], h + 1)
                dve.wait_ge(S["s"], h + 1)
                if h >= 2:
                    dve.wait_ge(S["nd"], 2 * (h - 1))
                    dve.wait_ge(S["dc"], h - 1)
                dve.tensor_tensor(at[two][:], ps[:, 1, :], wt[two][:], ALU.mult).then_inc(S["at"], 1)
                dve.wait_ge(S["knat"], j + 1)
                dve.tensor_tensor(ksc[two][:], k_nat[j % 2][:, :, rows(h)],
                                  wt[two][:, P - 1:LP:P].unsqueeze(2).broadcast_to([P, NC, DK]), ALU.mult).then_inc(S["ksc"], 1)
                dve.wait_ge(S["dc"], h + 1)
                dve.wait_ge(S["qw"], 2 * j + 2)
                for i in range(NC):
                    c = (i % 2) * 2 * P
                    src = ps[rows(h), 3 + i // 2, c:c + 2 * P]
                    dst = cn[rows(h), i, :] if i < NC - 1 else cfin[rows(h), j, :]
                    if i == 0:
                        dve.tensor_copy(dst, src).then_inc(S["cn"], 1)
                    else:
                        dve.wait_ge(S["cn"], NC * h + i)
                        dve.scalar_tensor_tensor(dst, cn[rows(h), i - 1, :], dec[rows(h), j, i:i + 1], src, ALU.mult, ALU.add)\
                            .then_inc(S["cn"], 1)

            def second(h):
                dve.wait_ge(S["em"], h + 1)
                dve.wait_ge(S["d2"], h + 1)
                dve.scalar_tensor_tensor(em[:], sqd[:], TINY, em[:], ALU.max, ALU.max).then_inc(S["d"], 1)
                dve.wait_ge(S["d"], h + 1)
                dve.wait_ge(S["msq"], h + 1)
                dve.scalar_tensor_tensor(em[:], ps[:, 6, :], 1.0 / DV, em[:], ALU.mult, ALU.add).then_inc(S["var"], 1)
                dve.wait_ge(S["var"], h + 1)
                dve.reciprocal(em[:], em[:]).then_inc(S["inv"], 1)

            def out(h):
                dve.wait_ge(S["og"], h + 1)
                if h >= 2:
                    dve.wait_ge(S["hi"], h - 1)
                    dve.wait_ge(S["lo"], h - 1)
                dve.scalar_tensor_tensor(mo[h % 2][:], ps[:, 5, :], gain[:, h:h + 1], og[:], ALU.mult, ALU.mult)\
                    .then_inc(S["out"], 1)
            first(0)
            for h in range(MH):
                if h + 1 < MH:
                    first(h + 1)
                if h:
                    out(h - 1)
                second(h)
            out(MH - 1)

        @block.gpsimd
        def _(pool):
            for h in range(MH):
                pool.wait_ge(S["rs"], h + 1)
                pool.wait_ge(S["sig"], h + 1)
                pool.tensor_tensor(og[:], og[:], proj[:, 16 + h, 0:LP], ALU.mult).then_inc(S["og"], 1)
                pool.wait_ge(S["hi"], h + 1)
                pool.tensor_tensor(K.xl[:, h, 0:LP], mo[h % 2][:], K.xh[:, h, 0:LP].bitcast(F32), ALU.subtract)\
                    .then_inc(S["lo"], 1)

    a = Region(nc, K.panels_at)
    wt_s, at_s, tl = (a(f"mls_{x}", [LS, MH, LS]) for x in ("wt", "at", "last"))
    wk = a("mls_wk", [LS, MH])
    k_s, ksc_s = a("mls_k", [LS, 4, 2, DK]), a("mls_ksc", [LS, 2, 4, DK])
    v_s = a("mls_v", [LS, MH, DV])
    vm = [a(f"mls_vm{x}", [LS, NB, DV]) for x in range(2)]
    qw_s, qwn = a("mls_qw", [P, 4, NB, NT]), a("mls_qwn", [P, 4, NB, NT])
    n0 = a("mls_n0", [P, NB, 4])
    nf = a("mls_nf", [P, NB, 4])
    np_ = a("mls_np", [P, 4])
    dec_s = a("mls_dec", [P, 4, NB])
    num, den, ems, sqs, ogs, os_ = (a(f"mls_{x}", [P, MH, LS]) for x in ("num", "den", "em", "sq", "og", "out"))
    nout, npout = a("mls_nout", [LS, P]), a("mls_npout", [4, P])
    assert a.at <= K.scratch_at, (a.at, K.scratch_at)
    R = {n: sem("mls_" + n) for n in ("b7", "b6", "st", "tr", "n0t", "act", "w_pre", "last_w", "ksc", "vm", "num", "nd", "sq",
                                      "msq", "dc", "dn", "norm", "n_den", "c_decayed", "c_new", "n_new", "nt", "nout", "hi")}

    def by_parity(t, lo, hi):
        return t.rearrange("p (j two) x -> p two j x", two=2)[:, :, :, lo:hi]

    def c_view(h):
        return c0[rows(h)].rearrange("p (n j) v -> p n j v", n=NB)[:, :, h // 2, :]

    def order(h):
        return (h % 2) * 4 + h // 2

    with nc.Block() as block:
        @block.tensor
        def _(pe):
            for j in range(4):
                pe.matmul(ps[:, 7, j * LS:(j + 1) * LS], sel[:, 2 * j * P + DK:2 * j * P + DK + P], wi[:, LP:T],
                          start=True, stop=True)
            for h in range(MH):
                o = P + order(h) * LS
                ins = pe.matmul(ps[:, 7, o:o + LS], sel_of(h), m[:, LP:T], start=True, stop=True)
            ins.then_inc(R["b7"], 1)
            for h in range(MH):
                o = order(h) * LS
                ins = pe.matmul(ps[0:LS, 6, o:o + LS], sel_of(h, LS), rr[:, LP:T], start=True, stop=True)
            ins.then_inc(R["b6"], 1)
            for h in range(MH):
                j = h // 2
                ins = pe.matmul(ps[0:LS, h % 2, j * LS:(j + 1) * LS], proj[rows(h), 4 + j, LP:T], proj[rows(h), j, LP:T],
                                start=True, stop=True)
            ins.then_inc(R["st"], 1)
            for j in range(4):
                pe.transpose(ps[0:LS, 2, j * P:(j + 1) * P], proj[:, 4 + j, LP:T], K.ident)
            for h in range(MH):
                ins = pe.transpose(ps[0:LS, 3 + h // 4, (h % 4) * P:(h % 4 + 1) * P], proj[:, 8 + h, LP:T], K.ident)
            ins.then_inc(R["tr"], 1)
            pe.transpose(ps[:, 5, 0:LS], n0_nat[:], K.ident[0:LS, 0:LS]).then_inc(R["n0t"], 1)
            pe.wait_ge(R["num"], 4)
            pe.wait_ge(R["act"], 5)
            for h in range(MH):
                j = h // 2
                for n in range(NB):
                    pe.matmul(ps[:, h % 2, j * LS + n * NT:j * LS + (n + 1) * NT], c_view(h)[:, n, :],
                              qw_s[rows(h), j, n, :], start=True, stop=True)
            for two in range(2):
                ins = pe.matmul(ps[:, two, 2 * P:3 * P], K.ones[rows(two), :],
                                qwn[rows(two)].rearrange("p j n t -> p (j n t)"), start=True, stop=True)
            ins.then_inc(R["nd"], 1)
            for h in range(MH):
                o = order(h)
                pe.matmul(ps[:, 6, o * LS:(o + 1) * LS], v_s[:, h, :], at_s[:, o, :], start=True, stop=True)
            pe.matmul(ps[:, 6, 2 * P:4 * P], K.ones[0:LS, :], at_s[:].rearrange("p h t -> p (h t)"), start=True, stop=True)\
                .then_inc(R["nd"], 1)
            pe.wait_ge(R["ksc"], 1)
            for h in range(MH):
                j = h // 2
                ins = pe.matmul(ps[rows(h), 7, 3 * P + j * NB:3 * P + (j + 1) * NB], ksc_s[:, h % 2, j, :], in_batch[:],
                                start=True, stop=True)
            ins.then_inc(R["dn"], 1)
            pe.wait_ge(R["n_new"], 1)
            pe.wait_ge(R["hi"], 1)
            pe.transpose(ps[0:LS, 0, 0:P], nf[:].rearrange("p n j -> p (n j)"), K.ident)
            pe.transpose(ps[0:4, 0, P:2 * P], np_[:], K.ident).then_inc(R["nt"], 1)
            pe.wait_ge(R["sq"], 1)
            pe.matmul(ps[:, 1, 0:2 * P], K.ones[:], sqs[:].rearrange("p h t -> p (h t)"), start=True, stop=True)\
                .then_inc(R["msq"], 1)
            for h in range(MH):
                pe.wait_ge(R["vm"], h + 1)
                if h >= 2:
                    pe.wait_ge(R["c_new"], h - 1)
                for half in range(2):
                    ins = pe.matmul(ps[rows(h), 2 + 2 * (h % 2) + half, :], ksc_s[:, h % 2, h // 2, :],
                                    vm[h % 2][:, 4 * half:4 * half + 4, :].rearrange("p n v -> p (n v)"), start=True, stop=True)
                ins.then_inc(R["dc"], 1)

        @block.scalar
        def _(act):
            act.wait_ge(R["num"], 2)
            act.activation(ems[:].rearrange("p h t -> p (h t)"), ps[:, 7, P:3 * P], ACT.Exp, scale=-2.0,
                           bias=ln_eps[:]).then_inc(R["act"], 1)
            act.wait_ge(R["tr"], 1)
            act.copy(k_s[:].rearrange("p j two d -> p (j two d)"), ps[0:LS, 2, :]).then_inc(R["act"], 1)
            act.copy(v_s[:].rearrange("p (a h) d -> p a (h d)", a=2), ps[0:LS, 3:5, :]).then_inc(R["act"], 1)
            act.wait_ge(R["n0t"], 1)
            act.copy(n0[:].rearrange("p n j -> p (n j)"), ps[:, 5, 0:LS]).then_inc(R["act"], 1)
            act.wait_ge(R["w_pre"], 3)
            act.activation(wt_s[:], wt_s[:], ACT.Exp).then_inc(R["act"], 1)
            act.wait_ge(R["nd"], 1)
            v = lambda t: t.rearrange("p (two j) x -> p two (j x)", two=2)
            act.copy(v(num[:]), ps[:, 0:2, 0:P]).then_inc(R["act"], 1)
            act.copy(v(den[:]), ps[:, 0:2, 2 * P:3 * P]).then_inc(R["act"], 1)
            act.wait_ge(R["act"], 7)
            act.copy(np_[:], cfin[:, :, P]).then_inc(R["hi"], 1)
            act.wait_ge(R["norm"], 1)
            act.activation(sqs[:], num[:], ACT.Square).then_inc(R["sq"], 1)
            act.wait_ge(R["norm"], 2)
            act.activation(den[:], den[:], ACT.Square, scale=EPS ** 0.5).then_inc(R["act"], 1)
            act.wait_ge(R["norm"], 4)
            act.activation(ems[:], ems[:], ACT.Sqrt).then_inc(R["act"], 1)
            act.wait_ge(R["norm"], 7)
            for two in range(2):
                ins = act.copy(by_parity(K.xh, LP, T)[:, two], os_[:, 4 * two:4 * two + 4, :])
            ins.then_inc(R["hi"], 1)

        @block.vector
        def _(dve):
            dve.wait_ge(R["b7"], 1)
            dve.tensor_copy(dec_s[:], ps[:, 7, 0:P].rearrange("p (j n t) -> p j n t", n=NB, t=NT)[:, :, :, NT - 1])\
                .then_inc(R["num"], 1)
            dve.tensor_tensor(qw_s[:].rearrange("p j n t -> p j (n t)"), ps[:, 7, 0:P].rearrange("p (j t) -> p j t", j=4),
                              proj[:, 0:4, LP:T], ALU.mult).then_inc(R["num"], 1)
            dve.wait_ge(R["b6"], 1)
            o4 = ct[0:LS, NC, :].rearrange("p (j two) -> p two j", two=2)
            for two in range(2):
                dve.tensor_tensor(wt_s[:, 4 * two:4 * two + 4, :], ps[0:LS, 6, two * P:(two + 1) * P].rearrange("p (j t) -> p j t", j=4),
                                  o4[:, two, :].unsqueeze(2).broadcast_to([LS, 4, LS]), ALU.add).then_inc(R["w_pre"], 1)
            dve.wait_ge(R["w_pre"], 2)
            dve.tensor_tensor(wt_s[:], wt_s[:], s_causal[:].unsqueeze(1).broadcast_to([LS, MH, LS]), ALU.add)\
                .then_inc(R["w_pre"], 1)
            dve.wait_ge(R["act"], 5)
            dve.wait_ge(R["num"], 2)
            for j in range(4):
                ins = dve.tensor_tensor(qwn[:, j], qw_s[:, j], n0[:, :, j].unsqueeze(2).broadcast_to([P, NB, NT]), ALU.mult)
            ins.then_inc(R["num"], 1)
            dve.wait_ge(R["st"], 1)
            for two in range(2):
                ins = dve.tensor_tensor(at_s[:, 4 * two:4 * two + 4, :], ps[0:LS, two, 0:P].rearrange("p (j t) -> p j t", j=4),
                                        wt_s[:, 4 * two:4 * two + 4, :], ALU.mult)
            ins.then_inc(R["num"], 1)
            dve.wait_ge(R["act"], 5)
            dve.tensor_tensor(tl[:], wt_s[:], s_last[:].unsqueeze(1).broadcast_to([LS, MH, LS]), ALU.mult).then_inc(R["last_w"], 1)
            dve.wait_ge(R["last_w"], 1)
            dve.tensor_reduce(wk[:], tl[:], AX.X, ALU.add).then_inc(R["last_w"], 1)
            dve.wait_ge(R["last_w"], 2)
            for two in range(2):
                ins = dve.tensor_tensor(ksc_s[:, two], k_s[:, :, two, :],
                                        wk[:, 4 * two:4 * two + 4].unsqueeze(2).broadcast_to([LS, 4, DK]), ALU.mult)
            ins.then_inc(R["ksc"], 1)
            dve.wait_ge(R["nd"], 2)
            dve.wait_ge(R["act"], 7)
            f = lambda t: t[:].rearrange("p h t -> p (h t)")
            dve.tensor_tensor(f(num), ps[:, 6, 0:2 * P], f(num), ALU.add).then_inc(R["norm"], 1)
            dve.tensor_tensor(f(den), ps[:, 6, 2 * P:4 * P], f(den), ALU.add).then_inc(R["norm"], 1)
            dve.wait_ge(R["dn"], 1)
            t = nf[:].rearrange("p n j -> p j n")
            dve.tensor_tensor(t, n0[:].rearrange("p n j -> p j n"), dec_s[:], ALU.mult).then_inc(R["n_den"], 1)
            dve.wait_ge(R["n_den"], 1)
            dve.tensor_tensor(t, ps[:, 7, 3 * P:3 * P + 4 * NB].rearrange("p (j n) -> p j n", j=4), t, ALU.add).then_inc(R["n_new"], 1)
            dve.wait_ge(R["act"], 8)
            dve.scalar_tensor_tensor(f(ems), f(den), TINY, f(ems), ALU.max, ALU.max).then_inc(R["n_den"], 1)
            dve.wait_ge(R["msq"], 1)
            dve.wait_ge(R["n_den"], 2)
            dve.scalar_tensor_tensor(f(ems), ps[:, 1, 0:2 * P], 1.0 / DV, f(ems), ALU.mult, ALU.add).then_inc(R["norm"], 1)
            dve.wait_ge(R["norm"], 3)
            dve.reciprocal(ems[:], ems[:]).then_inc(R["norm"], 1)
            dve.wait_ge(R["act"], 9)
            sg = by_parity(proj[:, 16:24, :], LP, T)
            gv = gain[:].rearrange("p (j two) -> p two j", two=2)
            for two in range(2):
                ins = dve.tensor_tensor(ogs[:, 4 * two:4 * two + 4, :], sg[:, two], gv[:, two, :].unsqueeze(2).broadcast_to([P, 4, LS]),
                                        ALU.mult)
            ins.then_inc(R["norm"], 1)
            dve.tensor_tensor(os_[:], num[:], ems[:], ALU.mult).then_inc(R["norm"], 1)
            dve.wait_ge(R["norm"], 6)
            dve.tensor_tensor(os_[:], os_[:], ogs[:], ALU.mult).then_inc(R["norm"], 1)
            dve.wait_ge(R["hi"], 2)
            for two in range(2):
                ins = dve.tensor_tensor(by_parity(K.xl, LP, T)[:, two], os_[:, 4 * two:4 * two + 4, :],
                                        by_parity(K.xh, LP, T)[:, two].bitcast(F32), ALU.subtract)
            dve.wait_ge(R["nt"], 1)
            dve.tensor_copy(nout[:], ps[0:LS, 0, 0:P])
            dve.tensor_copy(npout[:], ps[0:4, 0, P:2 * P]).then_inc(R["nout"], 1)
            for h in range(MH):
                dve.wait_ge(R["dc"], h + 1)
                dve.wait_ge(R["c_decayed"], h + 1)
                for half in range(2):
                    v = c_view(h)[:, 4 * half:4 * half + 4, :]
                    ins = dve.tensor_tensor(v, ps[rows(h), 2 + 2 * (h % 2) + half, :].rearrange("p (n v) -> p n v", n=4), v, ALU.add)
                ins.then_inc(R["c_new"], 1)

        @block.gpsimd
        def _(pool):
            def vmask(h):
                if h >= 2:
                    pool.wait_ge(R["dc"], h - 1)
                pool.tensor_tensor(vm[h % 2][:], v_s[:, h, :].unsqueeze(1).broadcast_to([LS, NB, DV]),
                                   in_batch[:].unsqueeze(2).broadcast_to([LS, NB, DV]), ALU.mult).then_inc(R["vm"], 1)
            pool.wait_ge(R["act"], 3)
            vmask(0)
            vmask(1)
            pool.wait_ge(R["nd"], 1)
            for h in range(MH):
                pool.tensor_tensor(c_view(h), c_view(h), dec_s[rows(h), h // 2, :].unsqueeze(2).broadcast_to([DK, NB, DV]),
                                   ALU.mult).then_inc(R["c_decayed"], 1)
                if h + 2 < MH:
                    vmask(h + 2)

        @block.sync
        def _(sp):
            sp.wait_ge(R["nout"], 1)
            sp.dma_start(O[14][0].rearrange("b (j two) d -> (b j) (two d)", two=2), nout[:]).then_inc(S["out_c"], 16)
            sp.dma_start(O[7][0, 0].rearrange("(j two) d -> j (two d)", two=2), npout[:]).then_inc(S["out_c"], 16)
            sp.wait_ge(R["c_new"], MH)
            sp.dma_start(O[13][0].rearrange("b (j two) d v -> (two d) (b j) v", two=2), c0[:]).then_inc(S["out_c"], 16)
            sp.wait_ge(S["out_c"], 16 * (MH + 5))


_OUTS = [(1, LP, D), (NB, NT, D),
         (1, 1, WIN, KVH, HD), (1, 1, WIN, KVH, HD), (1, 1, S5G, S5P), (1, 1, S5G, S5P),
         (1, 1, MH, DK, DV), (1, 1, MH, DK), (1, 1, MH),
         (1, NB, WIN, KVH, HD), (1, NB, WIN, KVH, HD), (1, NB, S5G, S5P), (1, NB, S5G, S5P),
         (1, NB, MH, DK, DV), (1, NB, MH, DK), (1, NB, MH)]


def hybrid_step(nc, ins, outs):
    K = Core(nc, ins, outs)
    phase_load(K)
    phase_even_in(K)
    phase_s5(K)
    phase_attention(K)
    phase_out_ffn(K, (even_out_dmas(K), 3), 0)
    phase_odd_in(K)
    phase_mlstm(K)
    phase_out_ffn(K, (plain_dmas(K, ins["w_out_odd"][0], DC), 2), 1)
    phase_store(K)


def kernel(**inputs):
    import concourse.bacc as bacc
    from concourse.bass_utils import run_bass_kernel_spmd

    nc = bacc.Bacc("TRN2", target_bir_lowering=False, num_devices=1)
    arrays = {f"in_{k}": np.ascontiguousarray(v) for k, v in inputs.items()}
    arrays["in_tables"] = np.concatenate(list(constant_tables().values()), axis=1)
    ins = {k[3:]: nc.dram_tensor(k, v.shape, F32, kind="ExternalInput").ap() for k, v in arrays.items()}
    outs = [nc.dram_tensor(f"out_{i}", s, F32, kind="ExternalOutput").ap() for i, s in enumerate(_OUTS)]
    hybrid_step(nc, ins, outs)
    r = run_bass_kernel_spmd(nc, [arrays], core_ids=[0])
    return tuple(r.results[0][f"out_{i}"] for i in range(len(_OUTS)))
```

```python
import numpy as np
import concourse.bass as bass
from concourse import mybir
from concourse.alu_op_type import AluOpType as ALU

F32 = mybir.dt.float32
F32R = mybir.dt.float32r
ACT = mybir.ActivationFunctionType
AX = mybir.AxisListType

P = 128
D = 1024
DC = D // P
LP = 512
NB, NT = 8, 4
LS = NB * NT
T = LP + LS
HT = T // 2
WIN = 128
PAST = 2048
HD = 64
QH, KVH = 8, 2
QG = QH // KVH
NH = QH + KVH
EVEN_IN = 1280
S5G, S5H, S5P = 32, 16, 64
NPAIR = S5G // 2
SUB = 8
NSUB = LP // SUB
MH, DK, DV = 8, 64, 128
ODD_IN = 3088
FF = 2816
FC = FF // P
FH = FC // 2
EPS = 1e-6
NEG = -1e30
TINY = 1e-37
TWO_PI = 2 * np.pi
ROUND = float(1.5 * 2 ** 23)


def constant_tables():
    f = np.float32
    t = {}
    t["ident"] = np.eye(P, dtype=f)
    cols = np.zeros((P, 2 * NH - 2), f)
    cols[:HD, NH - 2] = 1
    cols[HD:, NH - 1] = 1
    t["head_cols"] = cols
    back = np.zeros((P, NH // 2 * P), f)
    for h in range(NH):
        back[h, h * HD:(h + 1) * HD] = 1
    t["head_back"] = back
    half = HD // 8
    swap = np.zeros((P, P), f)
    for h in range(2):
        for d in range(half):
            swap[h * HD + half + d, h * HD + d] = -1
            swap[h * HD + d, h * HD + half + d] = 1
    t["rope_swap"] = swap
    inv = np.power(f(500000.0), -np.arange(half, dtype=f) / f(half)).astype(f)
    pos = np.concatenate([np.arange(LP), np.tile(PAST + np.arange(NT), NB)]).astype(f)
    ang = (pos[:, None] * inv[None, :]).astype(f)
    c = np.ones((P, T), f)
    s = np.zeros((P, T), f)
    for h in range(2):
        for part in range(2):
            at = h * HD + part * half
            c[at:at + half] = np.cos(ang).T
            s[at:at + half] = np.sin(ang).T
    t["rope_cos"], t["rope_sin"] = c, s
    q = np.arange(P)[:, None]
    j = np.arange(2 * P)[None, :]
    t["band"] = np.where((j >= q) & (j <= q + WIN), 0, NEG).astype(f)
    qb = (np.arange(P) % LS // NT)[:, None]
    qt = (np.arange(P) % NT)[:, None]
    old = np.arange(NB * WIN)[None, :]
    new = np.arange(LS)[None, :]
    m_old = (old // WIN == qb) & (old % WIN >= qt)
    m_new = (new // NT == qb) & (new % NT <= qt)
    t["sample_band"] = np.where(np.concatenate([m_old, m_new], 1), 0, NEG).astype(f)
    tt = np.arange(P)
    t["causal"] = np.where(tt[:, None] <= tt[None, :], 0, NEG).astype(f)
    st = np.arange(LS)
    same = st[:, None] // NT == st[None, :] // NT
    cs = np.full((P, LS), NEG, f)
    cs[:LS] = np.where(same & (st[:, None] <= st[None, :]), 0, NEG)
    t["sample_causal"] = cs
    last = np.zeros((P, LS), f)
    last[:LS] = same & (st[None, :] % NT == NT - 1)
    t["sample_last"] = last
    inb = np.zeros((P, NB), f)
    inb[:LS] = st[:, None] // NT == np.arange(NB)[None, :]
    t["in_batch"] = inb
    sel = np.zeros((P, MH * P), f)
    for h in range(MH):
        sel[h, h * P:(h + 1) * P] = 1
    t["head_sel"] = sel
    keep = np.ones((P, T), f)
    keep[:, 0:LP:P] = 0
    keep[:, LP::NT] = 0
    t["keep"] = keep
    return t


def table_places():
    at, out = 0, {}
    for name, a in constant_tables().items():
        out[name] = (at, at + a.shape[1])
        at += a.shape[1]
    return out, at


class Steps:

    def __init__(self, eng):
        self.eng, self.count, self.open = eng, {}, {}

    def __call__(self, ins, sem):
        ins.then_inc(sem, 1)
        self.count[sem.name] = self.count.get(sem.name, 0) + 1
        self.open[sem.name] = sem
        return ins

    def sync(self):
        for name, sem in self.open.items():
            self.eng.wait_ge(sem, self.count[name])
        self.open = {}


class Region:

    def __init__(self, nc, at):
        self.nc, self.at = nc, at

    def __call__(self, name, shape, dt=F32):
        n = int(np.prod(shape[1:])) * 4
        t = self.nc.alloc_sbuf_tensor_at(name, list(shape), dt, offset=self.at)
        self.at += -(-n // 64) * 64
        return t


class Core:

    def __init__(self, nc, ins, outs):
        self.nc, self.I, self.O, self.sems = nc, ins, outs, {}
        self.places, _ = table_places()
        self.ps = nc.alloc_psum_tensor("ps", [P, 8, 512], F32)
        r = Region(nc, 16512)
        self.cst = r("cst", [P, self.places["band"][0]])
        self.gains = r("gains", [P, 4, DC])
        self.rstd = r("rstd", [P, T])
        self.ssum = r("ssum", [P, T])
        self.sq = r("sq", [P, T])
        self.ones = r("ones", [P, P])
        self.resid = r("resid", [P, DC, T])
        self.xh = r("xh", [P, DC, T], F32R)
        self.xl = r("xl", [P, DC, T], F32R)
        self.panels_at = r.at
        self.xl_at, self.xh_at = r.at - DC * T * 4, r.at - 2 * DC * T * 4
        self.wraw = [r(f"wraw{s}", [P, FH, P]) for s in range(2)]
        self.whi = [r(f"whi{s}", [P, FH, P], F32R) for s in range(2)]
        self.wlo = [r(f"wlo{s}", [P, FH, P], F32R) for s in range(2)]
        self.scratch_at = r.at
        self.rot_at = r.at - 3 * NPAIR * NSUB * 4
        self.top_at = 178560
        self.n, self.raw = [0, 0], [0, 0]
        self.ident = self.table("ident")
        self.raw_ready = [self.sem(f"raw_ready{s}") for s in range(2)]
        self.hi_ready = [self.sem(f"hi_ready{s}") for s in range(2)]
        self.lo_ready = [self.sem(f"lo_ready{s}") for s in range(2)]
        self.panel_done = [self.sem(f"panel_done{s}") for s in range(2)]
        self.acc_free = [self.sem(f"acc_free{s}") for s in range(2)]
        self.acc = [self.ps[:, 2 * s:2 * s + 2, 0:HT] for s in range(2)]

    def sem(self, name):
        if name not in self.sems:
            self.sems[name] = self.nc.alloc_semaphore(name)
        return self.sems[name]

    def clear_sems(self, prefixes):
        done = [s for n, s in self.sems.items() if n.startswith(prefixes)]
        self.sems = {n: s for n, s in self.sems.items() if not n.startswith(prefixes)}
        with self.nc.Block() as block:
            @block.gpsimd
            def _(pool):
                self.nc.clear_and_free_semaphores(done)

    def table(self, name):
        a, b = self.places[name]
        return self.cst[:, a:b]

    def table_dram(self, name, rows=P):
        a, b = self.places[name]
        return self.I["tables"][0:rows, a:b]

    def product(self, pairs, kc, nd, slots=(0, 1)):
        g = Product()
        g.n, g.raw, g.pairs, g.kc, g.nd, g.slots = list(self.n), list(self.raw), pairs, kc, nd, slots
        for s in slots:
            self.n[s] += pairs
            self.raw[s] += 16 * nd * pairs
        return g


class Product:
    pass


def chunk(t, m, cols=slice(None)):
    if isinstance(m, int):
        return t[:, m, cols]
    return t[:, bass.ds(m, 1), cols].rearrange("p a t -> p (a t)")


def halves(ap):
    return ap.rearrange("p (a t) -> p a t", a=2)


def loop(eng, start, end, body):
    if end == start + 1:
        body(start)
    elif end > start:
        with eng.Fori(start, end) as i:
            body(i)


def load_panels(K, sp, g, dmas, start=0, end=None):
    def body(i):
        for s in g.slots:
            if not (isinstance(i, int) and g.n[s] + i == 0):
                sp.wait_ge(K.lo_ready[s], g.n[s] + i)
            for dst, src in dmas(s, i):
                sp.dma_start(dst, src).then_inc(K.raw_ready[s], 16)
    if g.n[0] == 0 and start == 0:
        body(0)
        start = 1
    loop(sp, start, g.pairs if end is None else end, body)


def split_hi(K, act, g, s, i):
    act.wait_ge(K.raw_ready[s], g.raw[s] + (i + 1) * (16 * g.nd))
    if not (isinstance(i, int) and g.n[s] + i == 0):
        act.wait_ge(K.panel_done[s], g.n[s] + i)
    act.copy(K.whi[s][:, 0:g.kc, :], K.wraw[s][:, 0:g.kc, :]).then_inc(K.hi_ready[s], 1)


def split_lo(K, dve, g, s, i):
    dve.wait_ge(K.hi_ready[s], g.n[s] + i + 1)
    dve.tensor_tensor(K.wlo[s][:, 0:g.kc, :], K.wraw[s][:, 0:g.kc, :], K.whi[s][:, 0:g.kc, :].bitcast(F32),
                      ALU.subtract).then_inc(K.lo_ready[s], 1)


def split_and_take(K, eng, g, split, evac=None, after=None, primed=False, peeled=0):
    if not primed:
        for s in g.slots:
            split(K, eng, g, s, 0)

    def body(i):
        for s in g.slots:
            if evac is not None:
                evac(s, i)
            split(K, eng, g, s, i + 1)
    for i in range(peeled):
        body(i)
    loop(eng, peeled, g.pairs - 1, body)
    for s in g.slots:
        if evac is not None:
            evac(s, g.pairs - 1)
        if after is not None and s in after.slots:
            split(K, eng, after, s, 0)


def multiply_panels(K, pe, g, ah, al, before_chunk=None, midway=None):
    def body(i):
        for s in g.slots:
            pe.wait_ge(K.lo_ready[s], g.n[s] + i + 1)
            if not (isinstance(i, int) and g.n[s] + i == 0):
                pe.wait_ge(K.acc_free[s], g.n[s] + i)
            for k in range(g.kc):
                if before_chunk is not None and s == 0 and isinstance(i, int) and i == 0:
                    before_chunk(k)
                for w, a, start, stop in ((K.whi, ah, k == 0, False), (K.whi, al, False, False),
                                          (K.wlo, ah, False, k == g.kc - 1)):
                    for h in range(2):
                        ins = pe.matmul(K.ps[:, 2 * s + h, 0:HT], w[s][:, k, :],
                                        a[:, k, h * HT:(h + 1) * HT], start=start, stop=stop)
            ins.then_inc(K.panel_done[s], 1)
            if midway is not None and s == 0 and isinstance(i, int) and i == 0:
                midway()
    first = 1 if g.n[0] == 0 or before_chunk is not None else 0
    if first:
        body(0)
    loop(pe, first, g.pairs, body)


def take(K, eng, g, s, i):
    eng.wait_ge(K.panel_done[s], g.n[s] + i + 1)


def plain_dmas(K, w, kc, m_of=lambda s, i: i * 2 + s):
    v = w.rearrange("(k p) (m c) -> m p k c", p=P, c=P)
    cut = kc // 2

    def dmas(s, i):
        m = m_of(s, i)
        src = v[m] if isinstance(m, int) else v[bass.ds(m, 1)].rearrange("a p k c -> p (a k) c")
        return [(K.wraw[s][:, 0:cut, :], src[:, 0:cut, :]), (K.wraw[s][:, cut:kc, :], src[:, cut:kc, :])]
    return dmas


def square_chunk(K, pool, m, before):
    if not (isinstance(before, int) and before == 0):
        pool.wait_ge(K.sem("summed"), before)
    pool.tensor_tensor(K.sq[:], chunk(K.resid, m), chunk(K.resid, m), ALU.mult).then_inc(K.sem("squared"), 1)
    pool.wait_ge(K.sem("squared"), before + 1)
    pool.tensor_tensor(K.ssum[:], K.ssum[:], K.sq[:], ALU.add).then_inc(K.sem("summed"), 1)


def clear_squares(K, pool, norm):
    if norm:
        pool.wait_ge(K.sem("rms_sum"), norm)
    pool.memset(K.ssum[:], 0.0).then_inc(K.sem("squares_cleared"), 1)
    pool.wait_ge(K.sem("squares_cleared"), norm + 1)


def rms_pe(K, pe, norm):
    pe.wait_ge(K.sem("summed"), DC * (norm + 1))
    for h in range(2):
        ins = pe.matmul(K.ps[:, 6 + h, 0:HT], K.ones[:], K.ssum[:, h * HT:(h + 1) * HT], start=True, stop=True)
    ins.then_inc(K.sem("rms_sum"), 1)


def rms_dve(K, dve, norm):
    dve.wait_ge(K.sem("rms_sum"), norm + 1)
    dve.tensor_scalar(halves(K.rstd[:]), K.ps[:, 6:8, 0:HT], 1.0 / D, EPS, ALU.mult, ALU.add)\
        .then_inc(K.sem("rms_taken"), 1)
    dve.wait_ge(K.sem("rms_taken"), norm + 1)
    dve.reciprocal(K.rstd[:], K.rstd[:]).then_inc(K.sem("rms_inverse"), 1)


def rms_act(K, act, norm):
    act.wait_ge(K.sem("rms_inverse"), norm + 1)
    act.activation(K.rstd[:], K.rstd[:], ACT.Sqrt).then_inc(K.sem("rms_ready"), 1)


def split_x_hi(K, act, norm, chunks=range(DC)):
    for m in chunks:
        act.activation(K.xh[:, m, :], K.resid[:, m, :], ACT.Copy, scale=K.gains[:, norm, m:m + 1])\
            .then_inc(K.sem("x_hi"), 1)


def split_x_lo(K, dve, norm, chunks=range(DC)):
    for m in chunks:
        dve.wait_ge(K.sem("x_hi"), DC * norm + m + 1)
        dve.scalar_tensor_tensor(K.xl[:, m, :], K.resid[:, m, :], K.gains[:, norm, m:m + 1],
                                 K.xh[:, m, :].bitcast(F32), ALU.mult, ALU.subtract).then_inc(K.sem("x_lo"), 1)


def wait_x(K, pe, norm):
    return lambda k: pe.wait_ge(K.sem("x_lo"), DC * norm + k + 1)


def phase_load(K):
    nc, I = K.nc, K.I
    sem = K.sem
    xs = Region(nc, K.scratch_at)("xs", [P, 5, D])
    x_in, consts_in, x_t = sem("x_in"), sem("consts_in"), sem("x_transposed")
    res_act, res_dve, s5_in = sem("resid_prompt"), sem("resid_sample"), sem("s5_in")
    K.even_scratch = K.scratch_at + EVEN_IN // P * T * 4
    r = Region(nc, K.even_scratch)
    par_in = K.s5_par_in = r("s5_par_in", [P, P])
    b_in = K.s5_b_in = [r(f"s5_b_{x}", [P, NPAIR, S5H]) for x in "ri"]
    c_in = K.s5_c_in = [r(f"s5_c_{x}", [P, 4, 2, S5P]) for x in "ri"]
    K.s5_tmp_at = r.at
    d_in = K.s5_d_in = Region(nc, K.top_at - 128)("s5_d_in", [S5H, S5G])
    K.g_even = K.product(5, DC, 2)
    vq = I["w_in_even"][0][:, 0:512].rearrange("(k p) (two h d) -> h two p k d", p=P, two=2, d=HD)

    def q_dmas(s, i):
        return [(K.wraw[s][:, 0:DC, two * HD:(two + 1) * HD], vq[2 * i + s][two]) for two in range(2)]
    K.q_dmas = q_dmas

    with nc.Block() as block:
        @block.sync
        def _(sp):
            sp.dma_start(xs[:, 0:4, :], I["x_prompt"][0].rearrange("(n p) d -> p n d", p=P)).then_inc(x_in, 16)
            sp.dma_start(xs[0:LS, 4, :], I["x_sample"].rearrange("b t d -> (b t) d")).then_inc(x_in, 16)
            load_panels(K, sp, K.g_even, q_dmas, 0, 1)
            for n, x in enumerate(("s5_a_re", "s5_a_im", "s5_log_dt")):
                sp.dma_start(par_in[16 * n:16 * n + 16, :], I[x][0].rearrange("(j two) p -> j (two p)", two=2))\
                    .then_inc(s5_in, 16)
            for x, nm in enumerate(("re", "im")):
                sp.dma_start(b_in[x][:], I["s5_b_" + nm][0].rearrange("(j two) p h -> (two p) j h", two=2)).then_inc(s5_in, 16)
                cv = I["s5_c_" + nm][0].rearrange("g h p -> (g h) p").rearrange("(m q) p -> q m p", q=P)
                for two in range(2):
                    sp.dma_start(c_in[x][:, :, two, :], cv).then_inc(s5_in, 16)
            sp.dma_start(d_in[:], I["s5_d"][0].rearrange("g h -> h g"), allow_slow_non_contiguous=True).then_inc(s5_in, 16)
            sp.dma_start(K.cst[:, P:], I["tables"][:, P:K.places["band"][0]]).then_inc(sem("tables_in"), 16)

        @block.scalar
        def _(act):
            act.dma_start(K.ident, I["tables"][:, 0:P]).then_inc(consts_in, 16)
            for n, g in enumerate(("norm_mix", "norm_ffn")):
                for l in range(2):
                    act.dma_start(K.gains[:, 2 * l + n, :], I[g][l].rearrange("(c p) -> p c", p=P),
                                  allow_slow_non_contiguous=True).then_inc(consts_in, 16)
            act.wait_ge(consts_in, 80)

            def high(m):
                act.wait_ge(res_act, m + 1)
                act.wait_ge(res_dve, m + 1)
                split_x_hi(K, act, 0, [m])
            for m in range(DC):
                act.wait_ge(x_t, m + 1)
                act.copy(K.resid[:, m, 0:LP], K.ps[:, 2 * (m % 2), :]).then_inc(res_act, 1)
                if m:
                    high(m - 1)
            high(DC - 1)
            for s in range(2):
                split_hi(K, act, K.g_even, s, 0)

        @block.vector
        def _(dve):
            dve.memset(K.ones[:], 1.0).then_inc(sem("ones_ready"), 1)
            dve.wait_ge(consts_in, 80)

            def low(m):
                dve.wait_ge(res_dve, m + 1)
                dve.wait_ge(res_act, m + 1)
                split_x_lo(K, dve, 0, [m])
            for m in range(DC):
                dve.wait_ge(x_t, m + 1)
                dve.tensor_copy(K.resid[:, m, LP:T], K.ps[:, 2 * (m % 2) + 1, 0:LS]).then_inc(res_dve, 1)
                if m:
                    low(m - 1)
            low(DC - 1)
            for s in range(2):
                split_lo(K, dve, K.g_even, s, 0)
            dve.wait_ge(sem("tables_in"), 16)

        @block.gpsimd
        def _(pool):
            clear_squares(K, pool, 0)
            for m in range(DC // 2):
                pool.wait_ge(res_act, m + 1)
                pool.wait_ge(res_dve, m + 1)
                square_chunk(K, pool, m, m)

        @block.tensor
        def _(pe):
            pe.wait_ge(consts_in, 80)
            pe.wait_ge(x_in, 32)
            for m in range(DC):
                if m >= 2:
                    pe.wait_ge(res_act, m - 1)
                    pe.wait_ge(res_dve, m - 1)
                for n in range(4):
                    pe.transpose(K.ps[:, 2 * (m % 2), n * P:(n + 1) * P], xs[:, n, m * P:(m + 1) * P], K.ident)
                pe.transpose(K.ps[:, 2 * (m % 2) + 1, 0:LS], xs[0:LS, 4, m * P:(m + 1) * P],
                             K.cst[0:LS, 0:LS]).then_inc(x_t, 1)


def phase_out_ffn(K, dmas_out, layer):
    nc, I, sem = K.nc, K.I, K.sem
    r = Region(nc, K.scratch_at)
    hh, hl = r(f"hh{layer}", [P, FH, T], F32R), r(f"hl{layer}", [P, FH, T], F32R)
    gate, up, act_gate = (r(f"{x}{layer}", [P, T]) for x in ("gate", "up", "act_gate"))
    norm = 2 * layer + 1
    squares = DC * norm
    w_gate, w_up, w_down = I["w_gate"][layer], I["w_up"][layer], I["w_down"][layer]
    g_out = K.g_out
    g_up, g_down = [], []
    for half in range(2):
        g_up.append(K.product(FH, DC, 2))
        g_down.append(K.product(DC // 2, FH, 2))
    K.g_odd = g_next = K.product(12, DC, 2) if layer == 0 else None
    gated, hid, hid_hi, hid_lo = (sem(x) for x in ("gated", "hidden", "hidden_hi", "hidden_lo"))
    turns = [FH * (2 * layer + half) for half in range(2)]

    def two_loads(half):
        vs = [w.rearrange("(k p) (m c) -> m p k c", p=P, c=P) for w in (w_gate, w_up)]

        def dmas(s, i):
            m = i + FH * half
            src = vs[s][m] if isinstance(m, int) else vs[s][bass.ds(m, 1)].rearrange("a p k c -> p (a k) c")
            return [(K.wraw[s][:, 0:4, :], src[:, 0:4, :]), (K.wraw[s][:, 4:8, :], src[:, 4:8, :])]
        return dmas

    def add_resid(dve, g):
        def evac(s, i):
            take(K, dve, g, s, i)
            m = i * 2 + s
            x = chunk(K.resid, m)
            dve.tensor_tensor(halves(x), K.acc[s], halves(x), ALU.add).then_inc(K.acc_free[s], 1)
        return evac

    with nc.Block() as block:
        @block.sync
        def _(sp):
            load_panels(K, sp, g_out, dmas_out, 1)
            for half in range(2):
                load_panels(K, sp, g_up[half], two_loads(half))
                load_panels(K, sp, g_down[half], plain_dmas(K, w_down[half * FH * P:(half + 1) * FH * P], FH))
            if g_next is not None:
                load_panels(K, sp, g_next, plain_dmas(K, I["w_in_odd"][0][:, 0:3072], DC), 0, 1)

        @block.tensor
        def _(pe):
            multiply_panels(K, pe, g_out, K.xh, K.xl)
            for half in range(2):
                if half == 0:
                    multiply_first = wait_x(K, pe, norm)
                    rms_pe(K, pe, norm)
                    multiply_panels(K, pe, g_up[0], K.xh, K.xl, multiply_first)
                else:
                    multiply_panels(K, pe, g_up[1], K.xh, K.xl)
                multiply_panels(K, pe, g_down[half], hh, hl,
                                lambda k: pe.wait_ge(hid_lo, turns[half] + k + 1))

        @block.vector
        def _(dve):
            split_and_take(K, dve, g_out, split_lo, add_resid(dve, g_out), g_up[0])
            split_x_lo(K, dve, norm)
            rms_dve(K, dve, norm)
            for half in range(2):
                n = turns[half]

                def evac(s, i):
                    take(K, dve, g_up[half], s, i)
                    if s == 0:
                        if half == 0 and isinstance(i, int):
                            dve.wait_ge(sem("rms_ready"), norm + 1)
                        if not (isinstance(i, int) and n + i == 0):
                            dve.wait_ge(gated, n + i)
                        dve.tensor_tensor(halves(gate[:]), K.acc[0], halves(K.rstd[:]), ALU.mult)\
                            .then_inc(K.acc_free[0], 1)
                    else:
                        if not (isinstance(i, int) and n + i == 0):
                            dve.wait_ge(hid_lo, n + i)
                        dve.tensor_tensor(halves(up[:]), K.acc[1], halves(K.rstd[:]), ALU.mult)\
                            .then_inc(K.acc_free[1], 1)
                        dve.wait_ge(K.acc_free[1], g_up[half].n[1] + i + 1)
                        dve.wait_ge(gated, n + i + 1)
                        dve.tensor_tensor(up[:], up[:], act_gate[:], ALU.mult).then_inc(hid, 1)
                        dve.wait_ge(hid_hi, n + i + 1)
                        dve.tensor_tensor(chunk(hl, i), up[:], chunk(hh, i).bitcast(F32), ALU.subtract)\
                            .then_inc(hid_lo, 1)
                if half == 0:
                    dve.wait_ge(sem("rms_ready"), norm + 1)
                split_and_take(K, dve, g_up[half], split_lo, evac, g_down[half], True, int(n == 0))
                split_and_take(K, dve, g_down[half], split_lo, add_resid(dve, g_down[half]),
                               g_up[1] if half == 0 else g_next, True)

        @block.scalar
        def _(act):
            split_and_take(K, act, g_out, split_hi, after=g_up[0])
            act.wait_ge(K.acc_free[0], g_out.n[0] + g_out.pairs)
            act.wait_ge(K.acc_free[1], g_out.n[1] + g_out.pairs)
            split_x_hi(K, act, norm)
            rms_act(K, act, norm)
            for half in range(2):
                n = turns[half]

                def evac(s, i):
                    if s == 0:
                        act.wait_ge(K.acc_free[0], g_up[half].n[0] + i + 1)
                        if not (isinstance(i, int) and n + i == 0):
                            act.wait_ge(hid, n + i)
                        act.activation(act_gate[:], gate[:], ACT.Silu).then_inc(gated, 1)
                    else:
                        act.wait_ge(hid, n + i + 1)
                        act.copy(chunk(hh, i), up[:]).then_inc(hid_hi, 1)
                split_and_take(K, act, g_up[half], split_hi, evac, g_down[half], True, int(n == 0))
                split_and_take(K, act, g_down[half], split_hi, after=g_up[1] if half == 0 else g_next, primed=True)

        @block.gpsimd
        def _(pool):
            def squares_of(g, at):
                def body(i):
                    for s in (0, 1):
                        pool.wait_ge(K.acc_free[s], g.n[s] + i + 1)
                        square_chunk(K, pool, i * 2 + s, i * 2 + (s + at))
                loop(pool, 0, g.pairs, body)
            clear_squares(K, pool, norm)
            squares_of(g_out, squares)
            if layer == 0:
                clear_squares(K, pool, norm + 1)
                squares_of(g_down[1], squares + DC)


def phase_store(K):
    nc, sem = K.nc, K.sem
    ys = Region(nc, K.scratch_at)("ys", [P, 5, D])
    y_t, y_a, y_d, y_out = sem("y_transposed"), sem("y_taken_act"), sem("y_taken_dve"), sem("y_out")
    with nc.Block() as block:
        @block.tensor
        def _(pe):
            for n in range(5):
                rows = P if n < 4 else LS
                for q in range(2):
                    j = 2 * n + q
                    if j >= 4:
                        pe.wait_ge(y_a, j // 2 - 1)
                        pe.wait_ge(y_d, j // 2 - 1)
                    for m in range(4):
                        ins = pe.transpose(K.ps[0:rows, j % 4, m * P:(m + 1) * P],
                                           K.resid[:, 4 * q + m, n * P:n * P + rows], K.ident)
                    ins.then_inc(y_t, 1)

        @block.scalar
        def _(act):
            for n in range(5):
                rows = P if n < 4 else LS
                act.wait_ge(y_t, 2 * n + 1)
                act.copy(ys[0:rows, n, 0:512], K.ps[0:rows, (2 * n) % 4, :]).then_inc(y_a, 1)

        @block.vector
        def _(dve):
            for n in range(5):
                rows = P if n < 4 else LS
                dve.wait_ge(y_t, 2 * n + 2)
                dve.tensor_copy(ys[0:rows, n, 512:D], K.ps[0:rows, (2 * n + 1) % 4, :]).then_inc(y_d, 1)

        @block.sync
        def _(sp):
            for n in range(5):
                sp.wait_ge(y_a, n + 1)
                sp.wait_ge(y_d, n + 1)
                if n < 4:
                    sp.dma_start(K.O[0][0, n * P:(n + 1) * P, :], ys[:, n, :]).then_inc(y_out, 16)
                else:
                    sp.dma_start(K.O[1].rearrange("b t d -> (b t) d"), ys[0:LS, 4, :]).then_inc(y_out, 16)
            sp.wait_ge(y_out, 80)


def cmul(st, eng, s, out_r, out_i, ar, ai, br, bi, tmp):
    st(eng.tensor_tensor(out_r, ar, br, ALU.mult), s)
    st(eng.tensor_tensor(tmp, ai, bi, ALU.mult), s)
    st(eng.tensor_tensor(out_i, ar, bi, ALU.mult), s)
    st.sync()
    st(eng.tensor_tensor(out_r, out_r, tmp, ALU.subtract), s)
    st.sync()
    st(eng.tensor_tensor(tmp, ai, br, ALU.mult), s)
    st.sync()
    st(eng.tensor_tensor(out_i, out_i, tmp, ALU.add), s)
    st.sync()


ROW = {n: k for k, n in enumerate("dt ard aid mag k r carg wi wr lr li den lm cr ci t1 t2 m8".split())}


def small_rows(small):
    return lambda name: small[:, ROW[name], :]


def phase_even_in(K):
    nc, I, sem = K.nc, K.I, K.sem
    proj = K.proj = Region(nc, K.scratch_at)("proj", [P, EVEN_IN // P, T])
    par_in, b_in, c_in = K.s5_par_in, K.s5_b_in, K.s5_c_in
    w_in = I["w_in_even"][0]
    top = Region(nc, K.top_at)
    F = K.s5_f = [top(f"s5_f_{x}", [P, NPAIR, SUB + 1, S5H]) for x in "ri"]
    G = K.s5_g = top("s5_g", [P, S5G, P])
    pw = K.s5_pw = [top(f"s5_pw_{x}", [P, NPAIR, SUB + 1]) for x in "ri"]
    bb = K.s5_bb = [top(f"s5_bb_{x}", [P, NPAIR, S5H]) for x in "ri"]
    small = K.s5_small = top("s5_small", [P, 18, NPAIR])
    par = top("s5_par", [P, 3 * NPAIR])
    ct = [top(f"s5_ct_{x}", [P, NPAIR, S5H]) for x in "ri"]
    K.s5_u = top("s5_u", [P, S5G, NSUB])
    K.s5_us = top("s5_us", [P, S5G, NB])
    assert top.at <= 229368, top.at
    lo = Region(nc, K.rot_at)
    K.s5_rot = [lo(f"s5_rot_{x}", [P, NPAIR, NSUB]) for x in "ri"]
    K.s5_decay = lo("s5_decay", [P, NPAIR, NSUB])
    assert lo.at <= K.scratch_at
    tmp = Region(nc, K.s5_tmp_at)("s5_tmp", [P, NPAIR, SUB, S5H])
    K.s5_eb = [G[:, 0:NPAIR, :], G[:, NPAIR:2 * NPAIR, :]]
    eb = [G[:, 0:NPAIR, :], G[:, NPAIR:2 * NPAIR, :]]
    g = K.g_even
    s5_in, s5_small, s5_act = sem("s5_in"), sem("s5_small"), sem("s5_act")
    par_t, c_t, c_taken = sem("s5_par_t"), sem("s5_c_t"), sem("s5_c_taken")
    s5_pool, coef_ready = sem("s5_pool"), sem("s5_coef")
    sm = small_rows(small)
    with nc.Block() as block:
        @block.sync
        def _(sp):
            load_panels(K, sp, g, K.q_dmas, 1, 2)
            load_panels(K, sp, g, plain_dmas(K, w_in, DC), 2)
        @block.tensor
        def _(pe):
            pe.wait_ge(s5_in, 160)
            pe.transpose(K.ps[:, 3, 0:48], par_in[0:48, :], K.cst[0:48, 0:48]).then_inc(par_t, 1)
            for x in range(2):
                for m in range(4):
                    ins = pe.transpose(K.ps[:, 4 + x, m * P:(m + 1) * P],
                                       c_in[x][:, m, :, :].rearrange("p a b -> p (a b)"), K.ident)
            ins.then_inc(c_t, 1)
            pe.wait_ge(s5_small, 1)
            multiply_panels(K, pe, g, K.xh, K.xl, wait_x(K, pe, 0), lambda: rms_pe(K, pe, 0))
        @block.scalar
        def _(act):
            act.wait_ge(s5_small, 1)
            act.activation(sm("dt"), par[:, 32:48], ACT.Exp).then_inc(s5_act, 1)
            act.wait_ge(c_t, 1)
            for x in range(2):
                cp = K.ps[:, 4 + x, :].rearrange("p (j two h) -> p j two h", two=2, h=S5H)
                for two in range(2):
                    hp = slice(two * S5P, (two + 1) * S5P)
                    ins = act.copy(ct[x][hp, :, :], cp[hp, :, two, :])
                    ins.then_inc(c_taken, 1)
            act.wait_ge(s5_small, 3)
            act.activation(sm("mag"), sm("ard"), ACT.Exp).then_inc(s5_act, 1)
            rms_act(K, act, 0)
            act.wait_ge(s5_small, 12)
            act.activation(sm("wi"), sm("r"), ACT.Sin).then_inc(s5_act, 1)
            act.activation(sm("wr"), sm("carg"), ACT.Sin).then_inc(s5_act, 1)
            split_and_take(K, act, g, split_hi, primed=True)

        @block.vector
        def _(dve):
            st = Steps(dve)
            s = s5_small
            dve.wait_ge(par_t, 1)
            st(dve.tensor_copy(par[:], K.ps[:, 3, 0:48]), s)
            ar, ai = par[:, 0:16], par[:, 16:32]
            st.sync()
            dve.wait_ge(s5_act, 1)
            st(dve.tensor_tensor(sm("aid"), ai, sm("dt"), ALU.mult), s)
            st(dve.tensor_tensor(sm("ard"), ar, sm("dt"), ALU.mult), s)
            st.sync()
            st(dve.tensor_scalar(sm("k"), sm("aid"), 1 / TWO_PI, ROUND, ALU.mult, ALU.add), s)
            st.sync()
            st(dve.tensor_scalar(sm("k"), sm("k"), ROUND, None, ALU.subtract), s)
            st.sync()
            c1 = 6.28125
            c2 = round((TWO_PI - c1) * 2 ** 20) / 2 ** 20
            c3 = TWO_PI - c1 - c2
            src = "aid"
            for c in (c1, c2, c3):
                st(dve.scalar_tensor_tensor(sm("r"), sm("k"), -c, sm(src), ALU.mult, ALU.add), s)
                st.sync()
                src = "r"
            st(dve.tensor_scalar(sm("r"), sm("r"), 3.1415925, -3.1415925, ALU.min, ALU.max), s)
            st.sync()
            st(dve.tensor_scalar(sm("carg"), sm("r"), -1.0, None, ALU.mult), s)
            st.sync()
            st(dve.tensor_tensor(sm("carg"), sm("carg"), sm("r"), ALU.min), s)
            st.sync()
            st(dve.tensor_scalar(sm("carg"), sm("carg"), np.pi / 2, None, ALU.add), s)
            rms_dve(K, dve, 0)
            dve.wait_ge(s5_act, 4)
            st(dve.tensor_tensor(sm("lr"), sm("mag"), sm("wr"), ALU.mult), s)
            st(dve.tensor_tensor(sm("li"), sm("mag"), sm("wi"), ALU.mult), s)
            st(dve.tensor_tensor(sm("den"), ar, ar, ALU.mult), s)
            st(dve.tensor_tensor(sm("t1"), ai, ai, ALU.mult), s)
            st(dve.tensor_tensor(sm("m8"), sm("mag"), sm("mag"), ALU.mult), s)
            st.sync()
            st(dve.tensor_tensor(sm("den"), sm("den"), sm("t1"), ALU.add), s)
            st(dve.tensor_scalar(sm("lm"), sm("lr"), -1.0, None, ALU.add), s)
            st(dve.tensor_tensor(sm("t2"), sm("m8"), sm("m8"), ALU.mult), s)
            st.sync()
            st(dve.reciprocal(sm("den"), sm("den")), s)
            st(dve.tensor_tensor(sm("m8"), sm("t2"), sm("t2"), ALU.mult), s)
            st.sync()
            st(dve.tensor_tensor(sm("cr"), sm("lm"), ar, ALU.mult), s)
            st(dve.tensor_tensor(sm("t1"), sm("li"), ai, ALU.mult), s)
            st(dve.tensor_tensor(sm("ci"), sm("li"), ar, ALU.mult), s)
            st(dve.tensor_tensor(sm("t2"), sm("lm"), ai, ALU.mult), s)
            st.sync()
            st(dve.tensor_tensor(sm("cr"), sm("cr"), sm("t1"), ALU.add), s)
            st(dve.tensor_tensor(sm("ci"), sm("ci"), sm("t2"), ALU.subtract), s)
            st.sync()
            st(dve.tensor_tensor(sm("cr"), sm("cr"), sm("den"), ALU.mult), s)
            st(dve.tensor_tensor(sm("ci"), sm("ci"), sm("den"), ALU.mult), s)
            st.sync()
            dve.memset(sm("t1"), 0.0).then_inc(coef_ready, 1)
            dve.wait_ge(sem("rms_ready"), 1)

            def evac(slot, i):
                take(K, dve, g, slot, i)
                dve.tensor_tensor(halves(chunk(proj, i * 2 + slot)), K.acc[slot], halves(K.rstd[:]), ALU.mult)\
                    .then_inc(K.acc_free[slot], 1)
            split_and_take(K, dve, g, split_lo, evac, primed=True)

        @block.gpsimd
        def _(pool):
            st = Steps(pool)
            s = s5_pool
            for m in range(DC // 2, DC):
                square_chunk(K, pool, m, m)
            pool.wait_ge(coef_ready, 1)

            def b3(name):
                return sm(name).unsqueeze(2).broadcast_to([P, NPAIR, S5H])
            t3 = tmp[:, :, 0, :]
            cmul(st, pool, s, bb[0][:], bb[1][:], b3("cr"), b3("ci"), b_in[0][:], b_in[1][:], t3)
            st(pool.memset(pw[0][:, :, 0:1], 1.0), s)
            st(pool.memset(pw[1][:, :, 0:1], 0.0), s)
            st(pool.tensor_copy(pw[0][:, :, 1:2], sm("lr").unsqueeze(2)), s)
            st(pool.tensor_copy(pw[1][:, :, 1:2], sm("li").unsqueeze(2)), s)
            st.sync()
            for n in (1, 2, 4):
                a = [pw[x][:, :, 1:n + 1] for x in range(2)]
                w = [pw[x][:, :, n:n + 1].broadcast_to([P, NPAIR, n]) for x in range(2)]
                cmul(st, pool, s, pw[0][:, :, n + 1:2 * n + 1], pw[1][:, :, n + 1:2 * n + 1], *a, *w, t3[:, :, 0:n])
            pool.wait_ge(c_taken, 4)
            for lo, hi in ((0, SUB), (SUB, SUB + 1)):
                n = hi - lo
                sh = [P, NPAIR, n, S5H]
                cb = [ct[x][:].unsqueeze(2).broadcast_to(sh) for x in range(2)]
                pb = [pw[x][:, :, lo:hi].unsqueeze(3).broadcast_to(sh) for x in range(2)]
                cmul(st, pool, s, F[0][:, :, lo:hi, :], F[1][:, :, lo:hi, :], *cb, *pb, tmp[:, :, 0:n, :])
                st(pool.tensor_scalar(F[1][:, :, lo:hi, :], F[1][:, :, lo:hi, :], -1.0, None, ALU.mult), s)
                st.sync()


def perm(ap, outer, inner):
    return ap.rearrange("p (c t) -> p t c", c=inner, t=outer)


def natural(ap, lo, hi, outer, inner):
    return ap[:, lo:hi].rearrange("p (t c) -> p t c", t=outer, c=inner)


def phase_s5(K):
    nc, I, O, sem = K.nc, K.I, K.O, K.sem
    proj, F, G, rot, decay, pw, bb, eb, d_in = K.proj, K.s5_f, K.s5_g, K.s5_rot, K.s5_decay, K.s5_pw, K.s5_bb, K.s5_eb, K.s5_d_in
    U, US = K.s5_u, K.s5_us
    K.g_out = K.product(DC // 2, DC, 3)
    e_t, e_act, e_dve, kt_t, kt_taken, g_in = (sem(x) for x in ("s5_e_t", "s5_e_act", "s5_e_dve", "s5_kt_t", "s5_kt_taken", "s5_g_in"))
    zeroed = sem("s5_zeroed")
    a = Region(nc, K.panels_at)
    kt = Region(nc, K.panels_at)("s5_kt", [S5H, S5G, P])
    X = [a(f"s5_x_{x}", [P, NPAIR, NSUB]) for x in "ri"]
    R = [a(f"s5_r_{x}", [P, NPAIR, NSUB]) for x in "ri"]
    tp = a("s5_tp", [P, NPAIR * NSUB])
    assert a.at <= K.rot_at
    b = Region(nc, K.even_scratch)
    E = [b(f"s5_e_{x}", [P, NPAIR, P]) for x in "ri"]
    h_nat = [b(f"s5_h_nat_{x}", [P, P]) for x in "ri"]
    H = [b(f"s5_h_{x}", [P, NPAIR, NSUB + 1]) for x in "ri"]
    up = b("s5_up", [P, 4, T])
    h0 = [b(f"s5_h0_{x}", [P, NPAIR, NB]) for x in "ri"]
    fin_s = [b(f"s5_fin_s_{x}", [P, NB, NPAIR]) for x in "ri"]
    fin_p = b("s5_fin_p", [P, 2, NPAIR])
    b_glu = b("s5_b_glu_t", [P, 4])
    YS = b("s5_ys", [P, S5G, NB])
    t8 = b("s5_t8", [P, NPAIR, NB])
    assert b.at <= K.top_at, b.at
    fin_pt = t8[0:32].rearrange("p j b -> p (j b)")
    Y = U
    yT = proj[:, 6:10, :]
    wg = Region(nc, K.panels_at + 2 * FH * P * 4)("s5_wg", [P, 4, 512])
    o_glu = [Region(nc, K.panels_at + 2 * FH * P * 4 + 8192 + 2176 * x)(f"s5_o{x}", [P, T]) for x in range(2)]
    sg = [Region(nc, K.panels_at + 2 * FH * P * 4 + 8192 + 4352 + 2176 * x)(f"s5_sg{x}", [P, T]) for x in range(2)]
    y_d = nc.dram_tensor("y_scratch", [512, T], F32, kind="Internal").ap()
    yd_v = y_d.rearrange("(g h) x -> h g x", h=S5H)
    S = {n: sem("s5a_" + n) for n in ("up", "ud", "u", "h_in", "h_t", "h0", "inc", "x_pe", "x_sb", "rot_r", "rot_i",
                                      "scan", "h", "y_pe", "y_sb", "ys_sb", "yd", "yt", "gelu", "glu", "sig", "o", "mh",
                                      "fin", "fin_t", "fin_sb", "st", "z_in", "small", "dve", "pool", "ml", "xfree")}
    def y_out(eng, half, tokens):
        gs = slice(half * S5G // 2, (half + 1) * S5G // 2)
        for t in tokens:
            eng.dma_start(yd_v[:, gs, t * NSUB:(t + 1) * NSUB], Y[t * S5H:(t + 1) * S5H, gs, :]).then_inc(S["yd"], 16)

    with nc.Block() as block:
        @block.sync
        def _(sp):
            for x, nm in enumerate(("re", "im")):
                sp.dma_start(h_nat[x][:], I["state_ssm_" + nm][0].rearrange("b (j two) p -> (b j) (two p)", two=2))\
                    .then_inc(S["h_in"], 16)
            sp.dma_start(b_glu[:], I["s5_b_glu"][0].rearrange("(m p) -> p m", p=P), allow_slow_non_contiguous=True)\
                .then_inc(S["z_in"], 16)
            sp.wait_ge(kt_taken, 10)
            sp.wait_ge(zeroed, 1)
            for row in range(SUB):
                s = SUB - 1 - row
                sp.dma_start(G[row * S5H:(row + 1) * S5H, :, s * S5H:P], kt[:, :, 0:P - s * S5H]).then_inc(g_in, 16)
            sp.wait_ge(S["xfree"], 1)
            sp.dma_start(wg[:], I["s5_w_glu"][0].rearrange("(k p) n -> p k n", p=P)).then_inc(S["z_in"], 16)
            load_panels(K, sp, K.g_out, even_out_dmas(K), 0, 1)
            sp.wait_ge(S["ys_sb"], 2)
            for t in range(NT):
                sp.dma_start(yd_v[:, :, LP + t * NB:LP + (t + 1) * NB], YS[t * S5H:(t + 1) * S5H, :, :]).then_inc(S["yd"], 16)
            for half in range(2):
                sp.wait_ge(S["y_sb"], 2 * half + 2)
                y_out(sp, half, range(0, SUB // 2))
            sp.wait_ge(S["yd"], 16 * (2 * SUB + NT))
            sp.dma_start(yT, y_d.rearrange("(m q) x -> q m x", q=P)).then_inc(S["yt"], 16)
            sp.wait_ge(S["fin_sb"], 3)
            for x in range(2):
                sp.dma_start(O[4 + x][0, 0].rearrange("(j two) p -> j (two p)", two=2), fin_pt[16 * x:16 * x + 16, :])\
                    .then_inc(S["st"], 16)
                sp.dma_start(O[11 + x][0].rearrange("b (j two) p -> (b j) (two p)", two=2),
                             h_nat[x][:]).then_inc(S["st"], 16)
            sp.wait_ge(S["st"], 64)

        @block.scalar
        def _(act):
            for k in range(0, 8, 2):
                act.wait_ge(e_t, k + 1)
                act.copy(E[k // 4][:, 4 * (k % 4):4 * (k % 4) + 4, :].rearrange("p a b -> p (a b)"),
                         K.ps[:, k % 4, :]).then_inc(e_act, 1)
            for x in range(2):
                act.wait_ge(S["h_t"], 1)
                act.copy(h0[x][:].rearrange("p j b -> p b j"),
                         K.ps[:, 7, x * P:(x + 1) * P].rearrange("p (b j) -> p b j", b=NB)).then_inc(S["h0"], 1)
            act.wait_ge(g_in, 16 * SUB)
            for x in range(2):
                act.wait_ge(S["x_pe"], x + 1)
                act.copy(X[x][:].rearrange("p j c -> p (j c)").rearrange("p (a q) -> p a q", a=2),
                         K.ps[:, 2 * x:2 * x + 2, :]).then_inc(S["x_sb"], 1)
            for m in range(4):
                act.wait_ge(S["y_pe"], m + 1)
                at = 8 * (m // 2)
                act.copy(Y[:].rearrange("p (j two) c -> p j two c", two=2)[:, at:at + 8, m % 2, :],
                         K.ps[:, m, :].rearrange("p (j c) -> p j c", c=NSUB)).then_inc(S["y_sb"], 1)
                if m % 2:
                    act.wait_ge(S["y_sb"], m + 1)
                    y_out(act, m // 2, range(SUB // 2, SUB))
            act.wait_ge(S["yt"], 16)
            for m in range(4):
                act.activation(up[:, m, :], yT[:, m, :], ACT.Gelu).then_inc(S["gelu"], 1)
            act.wait_ge(S["z_in"], 32)
            for m in range(4):
                act.wait_ge(S["glu"], m + 1)
                if m >= 2:
                    act.wait_ge(S["o"], m - 1)
                act.activation(halves(sg[m % 2][:]), K.ps[:, 2 * (m % 2):2 * (m % 2) + 2, 0:HT], ACT.Sigmoid,
                               bias=b_glu[:, m:m + 1]).then_inc(S["sig"], 1)
                act.wait_ge(S["o"], m + 1)
                act.copy(perm(K.xh[:, 4 + m, 0:LP], SUB, NSUB), natural(o_glu[m % 2], 0, LP, SUB, NSUB))
                act.copy(perm(K.xh[:, 4 + m, LP:T], NT, NB), natural(o_glu[m % 2], LP, T, NT, NB)).then_inc(S["mh"], 1)

        @block.tensor
        def _(pe):
            pe.wait_ge(S["h_in"], 32)
            for x in range(2):
                ins = pe.transpose(K.ps[:, 7, x * P:(x + 1) * P], h_nat[x][:], K.ident)
            ins.then_inc(S["h_t"], 1)
            for x in range(2):
                for b in range(4):
                    k = 4 * x + b
                    if k >= 4:
                        pe.wait_ge(e_act if k % 2 == 0 else e_dve, (k - 4) // 2 + 1)
                    for m in range(4):
                        ins = pe.transpose(K.ps[:, k % 4, m * P:(m + 1) * P], eb[x][:, 4 * b + m, :], K.ident)
                    ins.then_inc(e_t, 1)
            for q in range(4):
                for two in range(2):
                    k = 2 * q + two
                    bank = k % 4
                    if k < 4:
                        pe.wait_ge(e_act if k % 2 == 0 else e_dve, (4 + k) // 2 + 1)
                    else:
                        pe.wait_ge(kt_taken, k - 3)
                    hp = slice(two * S5P, (two + 1) * S5P)
                    for jj in range(4):
                        j = 4 * q + jj
                        for x in range(2):
                            ins = pe.matmul(K.ps[0:S5H, bank, jj * P:(jj + 1) * P], bb[x][hp, j, :],
                                            F[x][hp, j, 0:SUB, :].rearrange("p a b -> p (a b)"), start=x == 0, stop=x == 1)
                    ins.then_inc(kt_t, 1)
            for x in range(2):
                for j in range(NPAIR):
                    for two in range(2):
                        hp = slice(two * S5P, (two + 1) * S5P)
                        c = x * P + j * NB
                        ins = pe.matmul(K.ps[hp, 4, c:c + NB], E[x][0:64, j, hp], US[0:64, 2 * j + two, :], start=True, stop=True)
            ins.then_inc(S["inc"], 1)
            pe.wait_ge(kt_taken, 8)
            for x in range(2):
                for j in range(NPAIR):
                    for two in range(2):
                        hp = slice(two * S5P, (two + 1) * S5P)
                        c = (j % 8) * NSUB
                        ins = pe.matmul(K.ps[hp, 2 * x + j // 8, c:c + NSUB], E[x][:, j, hp], U[:, 2 * j + two, :],
                                        start=True, stop=True)
                ins.then_inc(S["x_pe"], 1)
            pe.wait_ge(S["h0"], 2)
            pe.wait_ge(g_in, 16 * SUB)
            for gg in [*range(0, S5G, 2), *range(1, S5G, 2)]:
                j, two = gg // 2, gg % 2
                hp = slice(two * S5P, (two + 1) * S5P)
                out = K.ps[0:64, 5 + two, j * NB:(j + 1) * NB]
                pe.matmul(out, G[:, gg, 0:64], US[:, gg, :], start=True, stop=False)
                for x in range(2):
                    ins = pe.matmul(out, F[x][hp, j, 1:5, :].rearrange("p a b -> p (a b)"), h0[x][hp, j, :],
                                    start=False, stop=x == 1)
            ins.then_inc(S["small"], 1)
            pe.wait_ge(S["x_sb"], 2)
            pe.wait_ge(S["h"], 2)
            for m in range(4):
                two, at = m % 2, 8 * (m // 2)
                hp = slice(two * S5P, (two + 1) * S5P)
                for k in range(8):
                    j = at + k
                    gg = 2 * j + two
                    out = K.ps[:, m, k * NSUB:(k + 1) * NSUB]
                    pe.matmul(out, G[:, gg, :], U[:, gg, :], start=True, stop=False)
                    for x in range(2):
                        ins = pe.matmul(out, F[x][hp, j, 1:SUB + 1, :].rearrange("p a b -> p (a b)"),
                                        H[x][hp, j, 0:NSUB], start=False, stop=x == 1)
                ins.then_inc(S["y_pe"], 1)
            pe.wait_ge(S["fin"], 3)
            pe.wait_ge(S["ys_sb"], 2)
            pe.transpose(K.ps[0:32, 6, 0:P], fin_p[:].rearrange("p x j -> p (x j)"), K.ident).then_inc(S["fin_t"], 1)
            for x in range(2):
                ins = pe.transpose(K.ps[:, 7, x * P:(x + 1) * P], fin_s[x][:].rearrange("p b j -> p (b j)"), K.ident)
            ins.then_inc(S["fin_t"], 1)
            pe.wait_ge(S["z_in"], 32)
            pe.wait_ge(S["gelu"], 4)
            pe.wait_ge(S["y_sb"], 4)
            for m in range(4):
                if m >= 2:
                    pe.wait_ge(S["sig"], m - 1)
                for k in range(4):
                    for h in range(2):
                        ins = pe.matmul(K.ps[:, 2 * (m % 2) + h, 0:HT], wg[:, k, m * P:(m + 1) * P],
                                        up[:, k, h * HT:(h + 1) * HT], start=k == 0, stop=k == 3)
                ins.then_inc(S["glu"], 1)

        @block.vector
        def _(dve):
            st = Steps(dve)
            s = S["dve"]
            st(dve.memset(H[0][:, :, 0:1], 0.0), s)
            st(dve.memset(H[1][:, :, 0:1], 0.0), s)
            for k in range(1, 8, 2):
                dve.wait_ge(e_t, k + 1)
                dve.tensor_copy(E[k // 4][:, 4 * (k % 4):4 * (k % 4) + 4, :].rearrange("p a b -> p (a b)"),
                                K.ps[:, k % 4, :]).then_inc(e_dve, 1)
            dve.wait_ge(e_act, 4)
            dve.memset(G[:], 0.0).then_inc(zeroed, 1)
            for q in range(4):
                for two in range(2):
                    k = 2 * q + two
                    dve.wait_ge(kt_t, k + 1)
                    v = kt[:, :, :].rearrange("h (j two) x -> h j two x", two=2)[:, 4 * q:4 * q + 4, two, :]
                    dve.tensor_copy(v, K.ps[0:S5H, k % 4, :].rearrange("h (j x) -> h j x", x=P)).then_inc(kt_taken, 1)
            dve.wait_ge(kt_taken, 8)
            dd = K.sq[0:S5H, 0:S5G * S5H].rearrange("p (g x) -> p g x", x=S5H)
            dve.tensor_tensor(dd, K.ident[0:S5H, 0:S5H].unsqueeze(1).broadcast_to([S5H, S5G, S5H]),
                              d_in[:].unsqueeze(2).broadcast_to([S5H, S5G, S5H]), ALU.mult).then_inc(kt_taken, 1)
            dve.wait_ge(kt_taken, 9)
            dve.tensor_tensor(kt[:, :, 0:S5H], kt[:, :, 0:S5H], dd, ALU.add).then_inc(kt_taken, 1)
            dve.wait_ge(S["inc"], 1)
            dve.wait_ge(S["h0"], 2)
            l4 = [pw[x][:, :, 4:5].broadcast_to([P, NPAIR, NB]) for x in range(2)]
            f = [fin_s[x][:].rearrange("p b j -> p j b") for x in range(2)]
            cmul(st, dve, s, *f, *l4, h0[0][:], h0[1][:], t8[:])
            for x in range(2):
                dve.tensor_tensor(f[x], K.ps[:, 4, x * P:(x + 1) * P].rearrange("p (j b) -> p j b", b=NB), f[x], ALU.add)\
                    .then_inc(S["fin"], 1)
            dve.wait_ge(S["x_sb"], 2)
            st(dve.tensor_tensor(R[0][:], X[0][:], rot[0][:], ALU.mult), s)
            t = H[1][:, :, 1:NSUB + 1]
            st(dve.tensor_tensor(t, X[1][:], rot[1][:], ALU.mult), s)
            st.sync()
            st(dve.tensor_tensor(R[0][:], R[0][:], t, ALU.add), s)
            st.sync()
            dve.wait_ge(S["rot_i"], 1)
            fl = lambda ap: ap.rearrange("p j c -> p (j c)")
            st(dve.tensor_tensor_scan(fl(X[0][:]), fl(decay[:]), fl(R[0][:]), 0.0, ALU.mult, ALU.add), s)
            st(dve.tensor_tensor_scan(fl(X[1][:]), fl(decay[:]), fl(R[1][:]), 0.0, ALU.mult, ALU.add), S["scan"])
            st.sync()
            h = H[0][:, :, 1:NSUB + 1]
            st(dve.tensor_tensor(h, X[0][:], rot[0][:], ALU.mult), s)
            st(dve.tensor_tensor(R[0][:], X[1][:], rot[1][:], ALU.mult), s)
            st.sync()
            dve.tensor_tensor(h, h, R[0][:], ALU.subtract).then_inc(S["h"], 1)
            dve.wait_ge(S["small"], 1)
            for two in range(2):
                dve.tensor_copy(YS[0:64].rearrange("p (j two) b -> p j two b", two=2)[:, :, two, :],
                                K.ps[0:64, 5 + two, 0:NPAIR * NB].rearrange("p (j b) -> p j b", b=NB)).then_inc(S["ys_sb"], 1)
            dve.wait_ge(S["h"], 2)
            st(dve.tensor_copy(fin_p[:, 0, :].unsqueeze(2), H[0][:, :, NSUB:NSUB + 1]), s)
            st.sync()
            dve.tensor_copy(fin_p[:, 1, :].unsqueeze(2), H[1][:, :, NSUB:NSUB + 1]).then_inc(S["fin"], 1)
            dve.wait_ge(S["fin"], 3)
            dve.memset(t8[:, 0:1, 0:1], 0.0).then_inc(S["xfree"], 1)
            dve.wait_ge(S["fin_t"], 1)
            dve.wait_ge(S["xfree"], 1)
            dve.tensor_copy(fin_pt, K.ps[0:32, 6, 0:P]).then_inc(S["fin_sb"], 1)
            dve.wait_ge(S["fin_t"], 2)
            for x in range(2):
                dve.tensor_copy(h_nat[x][:], K.ps[:, 7, x * P:(x + 1) * P]).then_inc(S["fin_sb"], 1)
            for m in range(4):
                dve.wait_ge(S["sig"], m + 1)
                if m >= 2:
                    dve.wait_ge(S["mh"], m - 1)
                    dve.wait_ge(S["ml"], m - 1)
                dve.tensor_tensor(o_glu[m % 2][:], up[:, m, :], sg[m % 2][:], ALU.mult).then_inc(S["o"], 1)
                dve.wait_ge(S["mh"], m + 1)
                dve.tensor_tensor(perm(K.xl[:, 4 + m, 0:LP], SUB, NSUB), natural(o_glu[m % 2], 0, LP, SUB, NSUB),
                                  perm(K.xh[:, 4 + m, 0:LP].bitcast(F32), SUB, NSUB), ALU.subtract)
                dve.tensor_tensor(perm(K.xl[:, 4 + m, LP:T], NT, NB), natural(o_glu[m % 2], LP, T, NT, NB),
                                  perm(K.xh[:, 4 + m, LP:T].bitcast(F32), NT, NB), ALU.subtract).then_inc(S["ml"], 1)

        @block.gpsimd
        def _(pool):
            st = Steps(pool)
            s = S["pool"]
            tv = tp[:].rearrange("p (j c) -> p j c", c=NSUB)
            pool.wait_ge(S["x_sb"], 2)
            st(pool.tensor_tensor(R[1][:], X[1][:], rot[0][:], ALU.mult), s)
            st(pool.tensor_tensor(tv, X[0][:], rot[1][:], ALU.mult), s)
            st.sync()
            st(pool.tensor_tensor(R[1][:], R[1][:], tv, ALU.subtract), S["rot_i"])
            pool.wait_ge(S["scan"], 1)
            h = H[1][:, :, 1:NSUB + 1]
            st.sync()
            st(pool.tensor_tensor(h, X[1][:], rot[0][:], ALU.mult), s)
            st(pool.tensor_tensor(tv, X[0][:], rot[1][:], ALU.mult), s)
            st.sync()
            pool.tensor_tensor(h, h, tv, ALU.add).then_inc(S["h"], 1)


def even_out_dmas(K):
    w = K.I["w_out_even"][0]
    va = w[0:512].rearrange("(two c d) (m x) -> m two d c x", two=2, d=HD, x=P)
    vs = w[512:D].rearrange("(k p) (m x) -> m p k x", p=P, x=P)

    def dmas(s, i):
        m = i * 2 + s
        out = []
        for two in range(2):
            src = va[m, two] if isinstance(m, int) else va[bass.ds(m, 1), two].rearrange("a d c x -> d (a c) x")
            out.append((K.wraw[s][two * HD:(two + 1) * HD, 0:4, :], src))
        src = vs[m] if isinstance(m, int) else vs[bass.ds(m, 1)].rearrange("a p k x -> p (a k) x")
        return out + [(K.wraw[s][:, 4:8, :], src)]
    return dmas


def phase_attention(K):
    nc, I, O, sem, ps = K.nc, K.I, K.O, K.sem, K.ps
    proj = K.proj
    a = Region(nc, K.panels_at)
    kc_in = a("kc_in", [P, NB, P])
    vc = a("vc", [P, NB, P])
    kc = a("kc", [P, NB, P])
    band = a("band", [P, 2 * P])
    sband = a("sband", [P, NB * WIN + LS])
    v_nat = a("v_nat", [P, 5, P])
    k_nat = a("k_nat", [P, 2, P])
    assert a.at <= K.rot_at
    r = Region(nc, K.even_scratch)
    g_qk = r("g_qk", [P, 2])
    qs = r("qs", [P, QG, LS])
    nsink = r("nsink", [P, QH])
    nsink_s = r("nsink_s", [P, KVH])
    UN = 10
    mx, nm, dk, es, den = (r("at_" + n, [P, UN, QG]) for n in ("mx", "nm", "dk", "es", "den"))
    early = Region(nc, r.at)
    sqb = [early(f"at_sq{x}", [P, T]) for x in range(5)]
    inv = early("at_inv", [NH, T])
    qn = [early(f"at_qn{x}", [P, T]) for x in range(2)]
    qc = [early(f"at_qc{x}", [P, T]) for x in range(2)]
    rs = [early(f"at_rs{x}", [P, T]) for x in range(2)]
    pm = [r(f"at_p{x}", [P, QG, 2 * P]) for x in range(2)]
    pt = [r(f"at_pt{x}", [P, 2, QG * P]) for x in range(2)]
    pms = [r(f"at_ps{x}", [P, NB * WIN + LS]) for x in range(2)]
    pts = [r(f"at_pts{x}", [P, NB, P]) for x in range(2)]
    ptn = [r(f"at_ptn{x}", [LS, P]) for x in range(2)]
    ub = Region(nc, K.xh_at + 4 * T * 4)("s5_ub", [P, 4, T])
    tmp = Region(nc, K.xl_at + 4 * T * 4)("s5_tmp2", [P, NPAIR, SUB, S5H])
    u_d = nc.dram_tensor("u_scratch", [512, T], F32, kind="Internal").ap()
    ud_v = u_d.rearrange("(g h) x -> h g x", h=S5H)
    s5_pool, u_up, u_out, u_in = sem("s5_pool_e"), sem("s5_u_up"), sem("s5_u_out"), sem("s5_u_in")
    U, US = K.s5_u, K.s5_us
    assert r.at <= K.top_at
    S = {n: sem("att_" + n) for n in ("in", "cache", "sq", "ssq", "var", "inv", "rt", "qn", "swap", "qc", "rs", "rope",
                                      "kt", "kc", "ktake", "spread", "s_pe", "mask", "mx", "nm", "dk", "exp", "es", "den", "rd", "p",
                                      "t_pe", "pt_a", "pt_d", "pv", "oh", "ol", "out", "sink", "qs")}
    cols, back, swap, cos, sin = (K.table(x) for x in ("head_cols", "head_back", "rope_swap", "rope_cos", "rope_sin"))

    units = [(i, kv) for i in range(4) for kv in range(KVH)]

    def rows(kv):
        return slice(kv * HD, (kv + 1) * HD)

    with nc.Block() as block:
        @block.sync
        def _(sp):
            for x, n in enumerate(("q_norm", "k_norm")):
                for two in range(2):
                    sp.dma_start(g_qk[rows(two), x:x + 1], I[n].rearrange("a d -> d a")).then_inc(S["in"], 16)
            sp.dma_start(nsink[:], I["attn_sinks"][0].partition_broadcast(P)).then_inc(S["in"], 16)
            sv = I["attn_sinks"].rearrange("a (kv c) -> a c kv", c=QG)
            for c in range(QG):
                sp.dma_start(nsink_s[c * LS:(c + 1) * LS, :], sv[0, c].partition_broadcast(LS),
                             allow_slow_non_contiguous=True).then_inc(S["in"], 16)
            sp.dma_start(band[:], K.table_dram("band")).then_inc(S["in"], 16)
            sp.dma_start(kc_in[:], I["cache_k"][0].rearrange("b w h d -> w b (h d)")).then_inc(S["cache"], 16)
            sp.dma_start(vc[:], I["cache_v"][0].rearrange("b w h d -> w b (h d)")).then_inc(S["cache"], 16)
            sp.dma_start(sband[:], K.table_dram("sample_band")).then_inc(S["cache"], 16)
            sp.wait_ge(u_up, 8)
            sp.dma_start(u_d.rearrange("(m q) x -> q m x", q=P), ub[:]).then_inc(u_out, 16)
            for o, x in ((9, "cache_k"), (10, "cache_v")):
                sp.dma_start(O[o][0, :, 0:WIN - NT], I[x][0, :, NT:WIN]).then_inc(S["out"], 16)
            sp.wait_ge(S["ktake"], 3)
            sp.dma_start(O[2][0, 0].rearrange("w h d -> w (h d)"), k_nat[:, 0, :]).then_inc(S["out"], 16)
            sp.dma_start(O[3][0, 0].rearrange("w h d -> w (h d)"), v_nat[:, 3, :]).then_inc(S["out"], 16)
            for b in range(NB):
                for o, t in ((9, k_nat[b * NT:(b + 1) * NT, 1, :]), (10, v_nat[b * NT:(b + 1) * NT, 4, :])):
                    sp.dma_start(O[o][0, b, WIN - NT:WIN].rearrange("w h d -> w (h d)"), t).then_inc(S["out"], 16)
            sp.wait_ge(u_out, 16)
            for row in range(SUB):
                t = SUB - 1 - row
                sp.dma_start(U[row * S5H:(row + 1) * S5H, :, :], ud_v[:, :, t * NSUB:(t + 1) * NSUB]).then_inc(u_in, 16)
            for t in range(NT):
                for row in (SUB - 1 - t, NT - 1 - t):
                    sp.dma_start(US[row * S5H:(row + 1) * S5H, :, :], ud_v[:, :, LP + t * NB:LP + (t + 1) * NB])\
                        .then_inc(u_in, 16)
            sp.wait_ge(u_in, 16 * (SUB + 2 * NT))
            sp.wait_ge(S["out"], 16 * 20)

        @block.tensor
        def _(pe):
            for c in range(5):
                pe.wait_ge(S["sq"], c + 1)
                for h in range(2):
                    ins = pe.matmul(ps[0:NH, h, 0:HT], cols[:, NH - 2 - 2 * c:2 * NH - 2 - 2 * c],
                                    sqb[c][:, h * HT:(h + 1) * HT], start=c == 0, stop=c == 4)
            ins.then_inc(S["ssq"], 1)
            for n in range(5):
                w = P if n < 4 else LS
                bank = 4 + n // 4
                ins = pe.transpose(ps[0:w, bank, (n % 4) * P:(n % 4 + 1) * P], proj[:, 5, n * P:n * P + w], K.ident)
            ins.then_inc(S["kt"], 1)
            pe.wait_ge(S["cache"], 48)
            for b in range(NB):
                ins = pe.transpose(ps[:, 6 + b // 4, (b % 4) * P:(b % 4 + 1) * P], kc_in[:, b, :], K.ident)
            ins.then_inc(S["kc"], 1)

            def spread(c):
                for h in range(2):
                    ins = pe.matmul(ps[:, 6 * (c % 2) + h, 0:HT], back[0:NH, c * P:(c + 1) * P],
                                    inv[:, h * HT:(h + 1) * HT], start=True, stop=True)
                ins.then_inc(S["spread"], 1)
            pe.wait_ge(S["rt"], 1)
            spread(0)
            pe.wait_ge(S["ktake"], 2)
            spread(1)
            for c in range(5):
                pe.wait_ge(S["qn"], c + 1)
                if c:
                    pe.wait_ge(S["rs"], c)
                for h in range(2):
                    ins = pe.matmul(ps[:, 2 + h, 0:HT], swap, qn[c % 2][:, h * HT:(h + 1) * HT], start=True, stop=True)
                ins.then_inc(S["swap"], 1)
                if c + 2 < 5:
                    spread(c + 2)
            pe.wait_ge(S["rope"], 5)
            pe.wait_ge(S["ktake"], 2)
            for n in range(2):
                w, at = (P, 3 * P) if n == 0 else (LS, LP)
                ins = pe.transpose(ps[0:w, 4, n * P:(n + 1) * P], proj[:, 4, at:at + w], K.ident)
            ins.then_inc(S["kt"], 1)

            def scores(u):
                i, kv = units[u]
                if u >= 2:
                    pe.wait_ge(S["mask"], u - 1)
                lo = (i - 1) * P if i else 0
                at = 0 if i else P
                for c in range(QG):
                    ins = pe.matmul(ps[:, 2 * kv + c // 2, (c % 2) * 2 * P + at:(c % 2 + 1) * 2 * P],
                                    proj[rows(kv), c, i * P:(i + 1) * P], proj[rows(kv), 4, lo:(i + 1) * P],
                                    start=True, stop=True)
                ins.then_inc(S["s_pe"], 1)

            def transposes(u):
                i, kv = units[u]
                pe.wait_ge(S["p"], u + 1)
                if u:
                    if u > 2:
                        pe.wait_ge(S["pt_a"], u - 2)
                    pe.wait_ge(S["pt_d"], u)
                else:
                    pe.wait_ge(S["ktake"], 3)
                for kb in ((0, 1) if i else (1,)):
                    for c in range(QG):
                        ins = pe.transpose(ps[:, 4 + kb, c * P:(c + 1) * P], pm[kv][:, c, kb * P:(kb + 1) * P], K.ident)
                ins.then_inc(S["t_pe"], 1)

            def values(u):
                i, kv = units[u]
                if u >= 2:
                    pe.wait_ge(S["pt_a"], u - 1)
                pe.wait_ge(S["pt_d"], u + 1)
                if u >= 2:
                    pe.wait_ge(S["ol"], u - 1)
                for kb in ((0, 1) if i else (1,)):
                    ins = pe.matmul(ps[rows(kv), 6 + kv, :], v_nat[:, i - 1 + kb, rows(kv)], pt[kv][:, kb, :],
                                    start=kb == 1 and not i or kb == 0, stop=kb == 1)
                ins.then_inc(S["pv"], 1)

            def sample_scores(kv):
                pe.wait_ge(S["mask"], 7 + kv)
                pe.wait_ge(S["ol"], 7 + kv)
                q = qs[rows(kv), :, :].rearrange("p c t -> p (c t)")
                for half in range(2):
                    pe.matmul(ps[:, 2 * kv + half, :], q, kc[rows(kv), 4 * half:4 * half + 4, :].rearrange("p b w -> p (b w)"),
                              start=True, stop=True)
                pe.matmul(ps[:, 6 + kv, 0:LS], q, proj[rows(kv), 4, LP:T], start=True, stop=True).then_inc(S["s_pe"], 1)
            pe.wait_ge(S["rs"], 5)
            scores(0)
            scores(1)
            for u in range(8):
                if u + 2 < 8:
                    scores(u + 2)
                transposes(u)
                values(u)
                if u == 6:
                    pe.wait_ge(S["qs"], 1)
                    sample_scores(0)
            sample_scores(1)
            for kv in range(KVH):
                u = 8 + kv
                pe.wait_ge(S["p"], u + 1)
                pe.wait_ge(S["pt_a"], u - 2)
                pe.wait_ge(S["pt_d"], u)
                for b in range(NB):
                    pe.transpose(ps[:, 4 + b // 4, (b % 4) * P:(b % 4 + 1) * P], pms[kv][:, b * P:(b + 1) * P], K.ident)
                pe.transpose(ps[0:LS, 2 * kv, 0:P], pms[kv][:, NB * P:], K.ident).then_inc(S["t_pe"], 1)
                pe.wait_ge(S["pt_a"], u - 1)
                pe.wait_ge(S["pt_d"], u + 1)
                out = ps[rows(kv), 6 + kv, P:2 * P]
                for b in range(NB):
                    pe.matmul(out, vc[:, b, rows(kv)], pts[kv][:, b, :], start=b == 0, stop=False)
                pe.matmul(out, v_nat[0:LS, 4, rows(kv)], ptn[kv][:], start=False, stop=True).then_inc(S["pv"], 1)

        @block.scalar
        def _(act):
            for c in range(5):
                act.activation(sqb[c][:], proj[:, c, :], ACT.Square).then_inc(S["sq"], 1)
            act.wait_ge(S["kt"], 1)
            act.copy(v_nat[:, 0:4, :].rearrange("p n x -> p (n x)"), ps[:, 4, :])
            act.copy(v_nat[0:LS, 4, :], ps[0:LS, 5, 0:P]).then_inc(S["ktake"], 1)
            act.wait_ge(S["kc"], 1)
            act.copy(kc[:].rearrange("p (a b) w -> p a (b w)", a=2), ps[:, 6:8, :]).then_inc(S["ktake"], 1)
            act.wait_ge(S["inv"], 1)
            act.activation(inv[:], inv[:], ACT.Sqrt).then_inc(S["rt"], 1)

            def exps(u):
                act.wait_ge(S["nm"], u + 1)
                if u < 8:
                    i, kv = units[u]
                    ks = slice(0, 2 * P) if i else slice(P, 2 * P)
                    for c in range(QG):
                        ins = act.activation(pm[kv][:, c, ks], pm[kv][:, c, ks], ACT.Exp, bias=nm[:, u, c:c + 1],
                                             accum_out=den[:, u, c:c + 1])
                else:
                    ins = act.activation(pms[u - 8][:], pms[u - 8][:], ACT.Exp, bias=nm[:, u, 0:1],
                                         accum_out=den[:, u, 0:1])
                ins.then_inc(S["exp"], 1)
                n = QG if u < 8 else 1
                act.wait_ge(S["dk"], u + 1)
                act.activation(es[:, u, 0:n], dk[:, u, 0:n], ACT.Exp).then_inc(S["es"], 1)

            def take_out(u):
                if u < 2:
                    return
                act.wait_ge(S["t_pe"], u + 1)
                if u >= 8:
                    kv = u - 8
                    act.copy(pts[kv][:, 0:4, :].rearrange("p b w -> p (b w)"), ps[:, 4, :])
                    act.copy(ptn[kv][:], ps[0:LS, 2 * kv, 0:P]).then_inc(S["pt_a"], 1)
                    return
                kv = units[u][1]
                act.copy(pt[kv][:, 0, :], ps[:, 4, :]).then_inc(S["pt_a"], 1)

            def high(u):
                act.wait_ge(S["pv"], u + 1)
                if u >= 8:
                    kv = u - 8
                    act.copy(K.xh[rows(kv), 0:QG, LP:T],
                             ps[rows(kv), 6 + kv, P:2 * P].rearrange("p (c t) -> p c t", c=QG)).then_inc(S["oh"], 1)
                    return
                i, kv = units[u]
                act.copy(K.xh[rows(kv), 0:QG, i * P:(i + 1) * P],
                         ps[rows(kv), 6 + kv, :].rearrange("p (c t) -> p c t", c=QG)).then_inc(S["oh"], 1)
            exps(0)
            for u in range(UN):
                if u in (7, 8):
                    high(u - 1)
                if u + 1 < UN:
                    exps(u + 1)
                if u and u not in (7, 8):
                    high(u - 1)
                take_out(u)
            high(UN - 1)

        @block.vector
        def _(dve):
            def norm(c):
                dve.wait_ge(S["spread"], c + 1)
                if c >= 2:
                    dve.wait_ge(S["swap"], c - 1)
                    dve.wait_ge(S["qc"], c - 1)
                g = g_qk[:, 0:1] if c < 4 else g_qk[:, 1:2]
                at = 6 * (c % 2)
                dve.scalar_tensor_tensor(halves(qn[c % 2][:]), halves(proj[:, c, :]), g, ps[:, at:at + 2, 0:HT],
                                         ALU.mult, ALU.mult).then_inc(S["qn"], 1)

            def rotate(c):
                dve.wait_ge(S["swap"], c + 1)
                if c >= 2:
                    dve.wait_ge(S["rope"], c - 1)
                dve.tensor_tensor(halves(rs[c % 2][:]), ps[:, 2:4, 0:HT], halves(sin), ALU.mult).then_inc(S["rs"], 1)
                dve.wait_ge(S["rs"], c + 1)
                dve.wait_ge(S["qc"], c + 1)
                dve.wait_ge(S["qn"], c + 1)
                dve.tensor_tensor(proj[:, c, :], qc[c % 2][:], rs[c % 2][:], ALU.add).then_inc(S["rope"], 1)
            dve.wait_ge(S["ssq"], 1)
            dve.tensor_scalar(halves(inv[:]), ps[0:NH, 0:2, 0:HT], 1.0 / HD, EPS, ALU.mult, ALU.add).then_inc(S["var"], 1)
            dve.wait_ge(S["var"], 1)
            dve.reciprocal(inv[:], inv[:]).then_inc(S["inv"], 1)
            dve.wait_ge(S["in"], 16 * 10)
            dve.tensor_scalar(nsink[:], nsink[:], -1.0, None, ALU.mult).then_inc(S["sink"], 1)
            dve.tensor_scalar(nsink_s[:], nsink_s[:], -1.0, None, ALU.mult).then_inc(S["sink"], 1)
            for c in range(5):
                norm(c)
                if c:
                    rotate(c - 1)
            rotate(4)
            dve.wait_ge(S["kt"], 2)
            dve.tensor_copy(k_nat[:, 0, :], ps[:, 4, 0:P])
            dve.tensor_copy(k_nat[0:LS, 1, :], ps[0:LS, 4, P:2 * P]).then_inc(S["ktake"], 1)
            dve.wait_ge(S["sink"], 2)

            def masked(u):
                dve.wait_ge(S["s_pe"], u + 1)
                if u >= 2:
                    dve.wait_ge(S["t_pe"], u - 1)
                if u < 8:
                    i, kv = units[u]
                    ks = slice(0, 2 * P) if i else slice(P, 2 * P)
                    for h in range(2):
                        sc = ps[:, 2 * kv + h, :].rearrange("p (c k) -> p c k", c=2)[:, :, ks]
                        ins = dve.scalar_tensor_tensor(pm[kv][:, 2 * h:2 * h + 2, ks], sc, HD ** -0.5,
                                                       band[:, ks].unsqueeze(1).broadcast_to([P, 2, ks.stop - ks.start]),
                                                       ALU.mult, ALU.add)
                    ins.then_inc(S["mask"], 1)
                    src, n, ns = pm[kv][:, :, ks], QG, nsink[:, kv * QG:(kv + 1) * QG]
                else:
                    kv = u - 8
                    for h in range(2):
                        dve.scalar_tensor_tensor(pms[kv][:, h * 512:(h + 1) * 512], ps[:, 2 * kv + h, :], HD ** -0.5,
                                                 sband[:, h * 512:(h + 1) * 512], ALU.mult, ALU.add)
                    dve.scalar_tensor_tensor(pms[kv][:, 1024:], ps[:, 6 + kv, 0:LS], HD ** -0.5,
                                             sband[:, 1024:], ALU.mult, ALU.add).then_inc(S["mask"], 1)
                    src, n, ns = pms[kv][:], 1, nsink_s[:, kv:kv + 1]
                dve.wait_ge(S["mask"], u + 1)
                dve.tensor_reduce(mx[:, u, 0:n], src, AX.X, ALU.max).then_inc(S["mx"], 1)
                dve.wait_ge(S["mx"], u + 1)
                dve.scalar_tensor_tensor(nm[:, u, 0:n], mx[:, u, 0:n], -1.0, ns, ALU.mult, ALU.min).then_inc(S["nm"], 1)
                dve.wait_ge(S["nm"], u + 1)
                dve.tensor_tensor(dk[:, u, 0:n], nm[:, u, 0:n], ns, ALU.subtract).then_inc(S["dk"], 1)

            def normed(u):
                dve.wait_ge(S["exp"], u + 1)
                dve.wait_ge(S["es"], u + 1)
                n = QG if u < 8 else 1
                dve.tensor_tensor(den[:, u, 0:n], den[:, u, 0:n], es[:, u, 0:n], ALU.add).then_inc(S["den"], 1)
                dve.wait_ge(S["den"], u + 1)
                dve.reciprocal(den[:, u, 0:n], den[:, u, 0:n]).then_inc(S["rd"], 1)
                dve.wait_ge(S["rd"], u + 1)
                if u < 8:
                    i, kv = units[u]
                    ks = slice(0, 2 * P) if i else slice(P, 2 * P)
                    v = pm[kv][:, :, ks]
                    dve.tensor_tensor(v, v, den[:, u, :].unsqueeze(2).broadcast_to([P, QG, ks.stop - ks.start]), ALU.mult)\
                        .then_inc(S["p"], 1)
                else:
                    v = pms[u - 8][:]
                    dve.tensor_scalar(v, v, den[:, u, 0:1], None, ALU.mult).then_inc(S["p"], 1)

            def take_out(u):
                dve.wait_ge(S["t_pe"], u + 1)
                if u < 8:
                    i, kv = units[u]
                    dve.tensor_copy(pt[kv][:, 1, :], ps[:, 5, :]).then_inc(S["pt_d"], 1)
                else:
                    kv = u - 8
                    dve.tensor_copy(pts[kv][:, 4:8, :].rearrange("p b w -> p (b w)"), ps[:, 5, :]).then_inc(S["pt_d"], 1)

            def low(u):
                if u < 8:
                    i, kv = units[u]
                    cols, src = slice(i * P, (i + 1) * P), ps[rows(kv), 6 + kv, :]
                else:
                    kv = u - 8
                    cols, src = slice(LP, T), ps[rows(kv), 6 + kv, P:2 * P]
                dve.wait_ge(S["oh"], u + 1)
                dve.tensor_tensor(K.xl[rows(kv), 0:QG, cols], src.rearrange("p (c t) -> p c t", c=QG),
                                  K.xh[rows(kv), 0:QG, cols].bitcast(F32), ALU.subtract).then_inc(S["ol"], 1)
            masked(0)
            for u in range(UN):
                if u in (7, 8):
                    low(u - 1)
                if u + 1 < UN:
                    masked(u + 1)
                normed(u)
                if u and u not in (7, 8):
                    low(u - 1)
                take_out(u)
            low(UN - 1)

        @block.gpsimd
        def _(pool):
            st = Steps(pool)
            s = s5_pool
            sm, pw, bb, eb, rot, decay = small_rows(K.s5_small), K.s5_pw, K.s5_bb, K.s5_eb, K.s5_rot, K.s5_decay
            for c in range(5):
                pool.wait_ge(S["qn"], c + 1)
                if c >= 2:
                    pool.wait_ge(S["rope"], c - 1)
                pool.tensor_tensor(qc[c % 2][:], qn[c % 2][:], cos, ALU.mult).then_inc(S["qc"], 1)
            for m in range(4):
                pool.tensor_copy(natural(ub[:, m, :], 0, LP, SUB, NSUB), perm(proj[:, 6 + m, 0:LP], SUB, NSUB)).then_inc(u_up, 1)
                pool.tensor_copy(natural(ub[:, m, :], LP, T, NT, NB), perm(proj[:, 6 + m, LP:T], NT, NB)).then_inc(u_up, 1)
            pool.wait_ge(S["rope"], 5)
            pool.tensor_copy(qs[:], proj[:, 0:QG, LP:T]).then_inc(S["qs"], 1)
            sh = [P, NPAIR, SUB, S5H]
            ev = [eb[x].rearrange("p j (s h) -> p j s h", h=S5H) for x in range(2)]
            cmul(st, pool, s, ev[0], ev[1], *[pw[x][:, :, 0:SUB].unsqueeze(3).broadcast_to(sh) for x in range(2)],
                 *[bb[x][:].unsqueeze(2).broadcast_to(sh) for x in range(2)], tmp[:])
            w = [tmp[:, :, 0, x:x + 1] for x in range(2)]
            v = [tmp[:, :, 1, x:x + 1] for x in range(2)]
            tq = tmp[:, :, 2, 0:1]
            st(pool.tensor_copy(w[0], sm("wr").unsqueeze(2)), s)
            st(pool.tensor_copy(w[1], sm("wi").unsqueeze(2)), s)
            st.sync()
            for k in range(3):
                cmul(st, pool, s, *v, *w, *w, tq)
                w, v = v, w
            st(pool.memset(rot[0][:, :, 0:1], 1.0), s)
            st(pool.memset(rot[1][:, :, 0:1], 0.0), s)
            st(pool.tensor_copy(rot[0][:, :, 1:2], w[0]), s)
            st(pool.tensor_copy(rot[1][:, :, 1:2], w[1]), s)
            st.sync()
            n = 1
            while n < NSUB - 1:
                k = min(n, NSUB - 1 - n)
                a = [rot[x][:, :, 1:k + 1] for x in range(2)]
                wb = [rot[x][:, :, n:n + 1].broadcast_to([P, NPAIR, k]) for x in range(2)]
                tt = tmp[:].rearrange("p j a b -> p j (a b)")[:, :, 0:k]
                cmul(st, pool, s, rot[0][:, :, n + 1:n + 1 + k], rot[1][:, :, n + 1:n + 1 + k], *a, *wb, tt)
                n += k
            st(pool.memset(decay[:, :, 0:1], 0.0), s)
            st(pool.tensor_copy(decay[:, :, 1:NSUB], sm("m8").unsqueeze(2).broadcast_to([P, NPAIR, NSUB - 1])), s)
            st.sync()


def phase_odd_in(K):
    nc, I, sem = K.nc, K.I, K.sem
    K.clear_sems(("s5", "att_"))
    r = Region(nc, K.scratch_at)
    proj = K.projo = r("projo", [P, 24, T])
    gates = K.gates = r("gates", [MH, 2, T])
    K.odd_scratch = r.at
    b = r
    s_causal, s_last = b("ml_s_causal", [LS, LS]), b("ml_s_last", [LS, LS])
    in_batch = b("ml_in_batch", [LS, NB])
    keep = b("ml_keep", [MH, T])
    bias = b("ml_bias", [MH, 2])
    m0 = b("ml_m0", [MH, NB])
    selr = b("ml_selr", [MH, MH * P], F32R)
    causalr, identr = b("ml_causalr", [P, P], F32R), b("ml_identr", [P, P], F32R)
    raw = Region(nc, 224640)
    sel, causal = raw("ml_sel", [MH, MH * P]), raw("ml_causal", [P, P])
    gain = b("ml_gain", [P, MH])
    n0_nat = b("ml_n0_nat", [LS, P])
    c0 = b("ml_c0", [P, NB * 4, DV])
    K.ml_in = causal, s_causal, s_last, in_batch, sel, keep, bias, m0, selr, causalr, identr, gain, n0_nat, c0
    K.odd_free = b.at
    S = {n: sem("ml_" + n) for n in ("in", "c_in")}
    w_in = I["w_in_odd"][0]
    g = K.g_odd
    g_gate = K.product(1, DC, 2, slots=(0,))
    w_gate = w_in[:, 3072:ODD_IN].rearrange("(k p) (two c) -> two p k c", p=P, two=2)
    k_scaled = sem("k_scaled")

    def gate_dmas(s, i):
        return [(K.wraw[0][:, 0:DC, 32 * two:32 * two + MH], w_gate[two]) for two in range(2)]

    with nc.Block() as block:
        @block.sync
        def _(sp):
            load_panels(K, sp, g, plain_dmas(K, w_in[:, 0:3072], DC), 1)
            for t, nm in ((causal, "causal"), (s_causal, "sample_causal"), (s_last, "sample_last"),
                          (in_batch, "in_batch"), (sel, "head_sel"), (keep, "keep")):
                sp.dma_start(t[:], K.table_dram(nm, t.shape[0])).then_inc(S["in"], 16)
            for n, nm in enumerate(("ml_b_i", "ml_b_f")):
                sp.dma_start(bias[:, n:n + 1], I[nm][0].unsqueeze(1)).then_inc(S["in"], 16)
            sp.dma_start(m0[:], I["state_mlstm_m"][0].rearrange("b h -> h b"), allow_slow_non_contiguous=True)\
                .then_inc(S["in"], 16)
            sp.dma_start(gain[:], I["ml_out_norm"][0].rearrange("(h p) -> p h", p=P), allow_slow_non_contiguous=True)\
                .then_inc(S["in"], 16)
            sp.dma_start(n0_nat[:], I["state_mlstm_n"][0].rearrange("b (j two) d -> (b j) (two d)", two=2))\
                .then_inc(S["c_in"], 16)
            sp.dma_start(c0[:], I["state_mlstm_c"][0].rearrange("b (j two) d v -> (two d) (b j) v", two=2))\
                .then_inc(S["c_in"], 16)
            load_panels(K, sp, g_gate, gate_dmas)
            sp.wait_ge(S["in"], 160)
            sp.wait_ge(S["c_in"], 32)

        @block.tensor
        def _(pe):
            rms_pe(K, pe, 2)
            multiply_panels(K, pe, g, K.xh, K.xl, wait_x(K, pe, 2))
            multiply_panels(K, pe, g_gate, K.xh, K.xl)

        @block.vector
        def _(dve):
            split_x_lo(K, dve, 2)
            rms_dve(K, dve, 2)
            dve.wait_ge(sem("rms_ready"), 3)

            def evac(s, i):
                take(K, dve, g, s, i)
                dve.tensor_tensor(halves(chunk(proj, i * 2 + s)), K.acc[s], halves(K.rstd[:]), ALU.mult)\
                    .then_inc(K.acc_free[s], 1)
            split_and_take(K, dve, g, split_lo, evac, g_gate, True)

            def evac_gates(s, i):
                take(K, dve, g_gate, s, i)
                dve.tensor_tensor(halves(gates[:, 0, :]), K.ps[0:MH, 0:2, 0:HT], halves(K.rstd[0:MH, :]), ALU.mult)
                dve.tensor_tensor(halves(gates[:, 1, :]), K.ps[32:32 + MH, 0:2, 0:HT], halves(K.rstd[32:32 + MH, :]),
                                  ALU.mult).then_inc(K.acc_free[0], 1)
            split_and_take(K, dve, g_gate, split_lo, evac_gates, primed=True)

        @block.scalar
        def _(act):
            split_x_hi(K, act, 2)
            rms_act(K, act, 2)
            split_and_take(K, act, g, split_hi, after=g_gate, primed=True)
            split_and_take(K, act, g_gate, split_hi, primed=True)

        @block.gpsimd
        def _(pool):
            for s in range(2):
                pool.wait_ge(K.acc_free[s], g.n[s] + 4)
            pool.tensor_scalar(proj[:, 4:8, :], proj[:, 4:8, :], DK ** -0.5, None, ALU.mult).then_inc(k_scaled, 1)


def phase_mlstm(K):
    nc, I, O, sem, ps, proj, gates = K.nc, K.I, K.O, K.sem, K.ps, K.projo, K.gates
    a = Region(nc, K.panels_at)
    b = Region(nc, K.odd_free)
    causal, s_causal, s_last, in_batch, sel, keep, bias, m0, selr, causalr, identr, gain, n0_nat, c0 = K.ml_in
    K.g_out = K.product(DC // 2, DC, 2)
    NC = LP // P
    gate_at = b.at
    e, lf, cum, m, rr, cc, wi = (b(f"ml_g_{x}", [MH, T]) for x in "elbmrcw")
    rh, rl, mh, ml = (Region(nc, at_)(f"ml_g_{x}", [MH, LP], F32R)
                      for x, at_ in (("rh", gate_at), ("rl", gate_at + T * 4), ("mh", gate_at + 2 * T * 4),
                                     ("ml", K.odd_scratch - T * 4)))
    mp = b("ml_mp", [MH, NC + NB])
    ct = b("ml_ct", [P, NC + 1, MH])
    ln_eps = b("ml_ln_eps", [P, 1])
    cfin = b("ml_cfin", [P, 4, 2 * P])
    dec = b("ml_dec", [P, 4, NC])
    wt = [a(f"ml_wt{x}", [P, LP]) for x in range(2)]
    at = [a(f"ml_at{x}", [P, LP]) for x in range(2)]
    v_nat = [a(f"ml_v_nat{x}", [P, NC, P]) for x in range(2)]
    k_nat = [a(f"ml_k_nat{x}", [P, NC, P]) for x in range(2)]
    ksc = [a(f"ml_ksc{x}", [P, NC, DK]) for x in range(2)]
    mo = [a(f"ml_mo{x}", [P, LP]) for x in range(2)]
    sqn = [a(f"ml_sqn{x}", [P, LP]) for x in range(2)]
    assert a.at <= K.scratch_at, (a.at, K.scratch_at)
    qw_at = b.at
    qw = [b(f"ml_qw{x}", [P, LP]) for x in range(2)]
    cn = b("ml_cn", [P, NC - 1, 2 * P])
    em = a("ml_em", [P, LP])
    sqd = a("ml_sqd", [P, LP])
    og = a("ml_og", [P, LP])
    assert b.at <= 229368, b.at
    S = {n: sem("ml_" + n) for n in ("in", "c_in", "parts", "gd", "ga", "gates", "ct_pe", "ct", "sig", "win", "qw", "kt", "knat", "wpre",
                                     "w", "s", "at", "vt", "vnat", "ksc", "dc", "cn", "nd", "mb", "em", "sqn",
                                     "d", "d2", "msq", "var", "inv", "rs", "og", "out", "hi", "lo", "out_c")}

    def rows(h):
        return slice((h % 2) * DK, (h % 2 + 1) * DK)

    def sel_of(h, n=P):
        return selr[:, h * P:h * P + n].bitcast(F32)

    with nc.Block() as block:
        @block.sync
        def _(sp):
            for h in range(MH):
                sp.wait_ge(S["cn"], NC * (h + 1))
                sp.dma_start(O[6][0, 0, h], cfin[rows(h), h // 2, 0:P]).then_inc(S["out_c"], 16)
            sp.wait_ge(S["gates"], 1)
            sp.dma_start(O[8][0, 0].unsqueeze(1), m[:, LP - 1:LP]).then_inc(S["out_c"], 16)
            sp.dma_start(O[15][0].rearrange("b h -> h b"), m[:, LP + NT - 1:T:NT], allow_slow_non_contiguous=True)\
                .then_inc(S["out_c"], 16)
            sp.wait_ge(S["out_c"], 16 * (MH + 2))

        @block.tensor
        def _(pe):
            def k_by_token(h):
                for i in range(NC):
                    ins = pe.transpose(ps[:, 3, i * P:(i + 1) * P], proj[:, 4 + h // 2, i * P:(i + 1) * P], K.ident)
                ins.then_inc(S["kt"], 1)

            def scores(h):
                j = h // 2
                for i in range(NC):
                    ts = slice(i * P, (i + 1) * P)
                    ins = pe.matmul(ps[:, 1, ts], proj[rows(h), 4 + j, ts], proj[rows(h), j, ts], start=True, stop=True)
                ins.then_inc(S["s"], 1)
                for i in range(NC):
                    ins = pe.transpose(ps[:, 2, i * P:(i + 1) * P], proj[:, 8 + h, i * P:(i + 1) * P], K.ident)
                ins.then_inc(S["vt"], 1)
            k_by_token(0)
            scores(0)
            pe.wait_ge(S["in"], 161)
            pe.wait_ge(S["gates"], 1)
            for i in range(NC + 1):
                w = P if i < NC else LS
                ins = pe.transpose(ps[0:w, 4, i * MH:(i + 1) * MH], cc[:, i * P:i * P + w], K.ident[0:MH, 0:MH])
            ins.then_inc(S["ct_pe"], 1)
            pe.wait_ge(S["gates"], 2)

            def first(h):
                j, two = h // 2, h % 2
                if two == 0:
                    if h:
                        pe.wait_ge(S["em"], h - 1)
                        pe.wait_ge(S["cn"], NC * h)
                    if h == 0:
                        pe.wait_ge(S["parts"], 7)
                    pe.matmul(ps[:, 7, :], selr[:, h * P + DK:h * P + DK + P].bitcast(F32), wi[:, 0:LP], start=True, stop=True)\
                        .then_inc(S["win"], 1)
                    if h:
                        k_by_token(h)
                if h:
                    pe.wait_ge(S["w"], h)
                    pe.wait_ge(S["at"], h)
                    pe.wait_ge(S["vnat"], h)
                else:
                    pe.wait_ge(S["ct"], 1)
                    pe.wait_ge(S["parts"], 7)
                out = ps[:, 0, :].rearrange("p (i t) -> p i t", i=NC)
                pe.matmul(ps[:, 0, :], selr[:, h * P:(h + 1) * P], rh[:], start=True, stop=False)
                pe.matmul(ps[:, 0, :], selr[:, h * P:(h + 1) * P], rl[:], start=False, stop=False)
                pe.matmul(out, identr[:], causalr[:].unsqueeze(1).broadcast_to([P, NC, P]), start=False, stop=True)\
                    .then_inc(S["wpre"], 1)
                if h:
                    scores(h)

            def states(h):
                two = h % 2
                pe.wait_ge(S["ksc"], h + 1)
                pe.wait_ge(S["vnat"], h + 1)
                if h:
                    pe.wait_ge(S["cn"], NC * h)
                for i in range(NC):
                    c = (i % 2) * 2 * P
                    pe.matmul(ps[rows(h), 3 + i // 2, c:c + P], ksc[two][:, i, :], v_nat[two][:, i, :], start=True, stop=True)
                    ins = pe.matmul(ps[rows(h), 3 + i // 2, c + P:c + 2 * P], ksc[two][:, i, :], K.ones[:], start=True, stop=True)
                ins.then_inc(S["dc"], 1)

            def second(h):
                j, two = h // 2, h % 2
                pe.wait_ge(S["at"], h + 1)
                pe.wait_ge(S["cn"], NC * h + NC - 1)
                pe.wait_ge(S["qw"], 2 * min(4, (h + 1) // 2 + 1))
                if h:
                    pe.wait_ge(S["em"], h)
                    pe.wait_ge(S["var"], h)
                pe.matmul(ps[:, 7, :], selr[:, h * P:(h + 1) * P], mh[:], start=True, stop=False)
                pe.matmul(ps[:, 7, :], selr[:, h * P:(h + 1) * P], ml[:], start=False, stop=True).then_inc(S["mb"], 1)
                pe.matmul(ps[:, 6, :], K.ones[:], at[two][:], start=True, stop=False)
                for i in range(1, NC):
                    ts = slice(i * P, (i + 1) * P)
                    ins = pe.matmul(ps[:, 6, ts], cn[rows(h), i - 1, P:2 * P], qw[j % 2][rows(h), ts], start=False, stop=i == NC - 1)
                ins.then_inc(S["nd"], 1)
                if h:
                    pe.wait_ge(S["out"], h)
                    pe.wait_ge(S["sqn"], h)
                for i in range(NC):
                    ts = slice(i * P, (i + 1) * P)
                    ins = pe.matmul(ps[:, 5, ts], v_nat[two][:, i, :], at[two][:, ts], start=True, stop=i == 0)
                    if i:
                        ins = pe.matmul(ps[:, 5, ts], cn[rows(h), i - 1, 0:P], qw[j % 2][rows(h), ts], start=False, stop=True)
                ins.then_inc(S["nd"], 1)

            def squares(h):
                two = h % 2
                pe.wait_ge(S["sqn"], h + 1)
                pe.wait_ge(S["d2"], h + 1)
                pe.matmul(ps[:, 6, :], K.ones[:], sqn[two][:], start=True, stop=True).then_inc(S["msq"], 1)
            first(0)
            states(0)
            for h in range(MH):
                if h + 1 < MH:
                    first(h + 1)
                second(h)
                if h + 1 < MH:
                    states(h + 1)
                squares(h)

        @block.scalar
        def _(act):
            act.wait_ge(S["in"], 161)
            act.copy(selr[:], sel[:]).then_inc(S["parts"], 1)
            act.copy(causalr[:], causal[:]).then_inc(S["parts"], 1)
            act.copy(identr[:], K.ident).then_inc(S["parts"], 1)
            act.wait_ge(S["gd"], 2)
            act.activation(e[:], e[:], ACT.Exp).then_inc(S["ga"], 1)
            act.wait_ge(S["ga"], 1)
            act.activation(e[:], e[:], ACT.Ln, bias=K.ones[0:MH, 0:1]).then_inc(S["ga"], 1)
            act.wait_ge(S["gates"], 1)
            act.activation(wi[:], wi[:], ACT.Exp).then_inc(S["gates"], 1)
            act.copy(rh[:], rr[:, 0:LP]).then_inc(S["parts"], 1)
            act.copy(mh[:], m[:, 0:LP]).then_inc(S["parts"], 1)
            for h in range(MH):
                act.activation(proj[:, 16 + h, :], proj[:, 16 + h, :], ACT.Sigmoid).then_inc(S["sig"], 1)

            def first(h):
                j, two = h // 2, h % 2
                if two == 0:
                    act.wait_ge(S["kt"], j + 1)
                    if j >= 2:
                        act.wait_ge(S["ksc"], h - 2)
                    act.copy(k_nat[j % 2][:].rearrange("p i x -> p (i x)"), ps[:, 3, :]).then_inc(S["knat"], 1)
                act.wait_ge(S["wpre"], h + 1)
                if h >= 2:
                    act.wait_ge(S["at"], h - 1)
                    act.wait_ge(S["ksc"], h - 1)
                else:
                    act.wait_ge(S["ct"], 1)
                for i in range(NC):
                    ts = slice(i * P, (i + 1) * P)
                    ins = act.activation(wt[two][:, ts], ps[:, 0, ts], ACT.Exp, bias=ct[:, i, h:h + 1])
                ins.then_inc(S["w"], 1)
                act.wait_ge(S["vt"], h + 1)
                if h >= 2:
                    act.wait_ge(S["nd"], 2 * (h - 1))
                act.copy(v_nat[two][:].rearrange("p i x -> p (i x)"), ps[:, 2, :]).then_inc(S["vnat"], 1)

            def high(h):
                act.wait_ge(S["out"], h + 1)
                act.copy(K.xh[:, h, 0:LP], mo[h % 2][:]).then_inc(S["hi"], 1)

            def second(h):
                act.wait_ge(S["mb"], h + 1)
                if h:
                    act.wait_ge(S["d"], h)
                    act.wait_ge(S["rs"], h)
                act.activation(em[:], ps[:, 7, :], ACT.Exp, scale=-2.0, bias=ln_eps[:]).then_inc(S["em"], 1)
                act.wait_ge(S["nd"], 2 * h + 1)
                act.activation(sqd[:], ps[:, 6, :], ACT.Square, scale=EPS ** 0.5).then_inc(S["d2"], 1)
                act.wait_ge(S["nd"], 2 * h + 2)
                if h >= 2:
                    act.wait_ge(S["msq"], h - 1)
                act.activation(sqn[h % 2][:], ps[:, 5, :], ACT.Square).then_inc(S["sqn"], 1)
                act.wait_ge(S["var"], h + 1)
                act.activation(em[:], em[:], ACT.Ln).then_inc(S["inv"], 1)
                act.wait_ge(S["inv"], h + 1)
                act.activation(og[:], em[:], ACT.Exp, scale=-0.5).then_inc(S["rs"], 1)
            first(0)
            for h in range(MH):
                if h + 1 < MH:
                    first(h + 1)
                if h:
                    high(h - 1)
                second(h)
            high(MH - 1)

        @block.vector
        def _(dve):
            s = S["gd"]
            st = Steps(dve)
            dve.memset(ln_eps[:], float(np.log(EPS))).then_inc(S["in"], 1)
            dve.wait_ge(S["in"], 161)
            ig, f = gates[:, 0, :], gates[:, 1, :]
            st(dve.tensor_scalar(f, f, bias[:, 1:2], None, ALU.add), s)
            st.sync()
            st(dve.scalar_tensor_tensor(e[:], f, -1.0, f, ALU.mult, ALU.min), s)
            st(dve.tensor_scalar(ig, ig, bias[:, 0:1], None, ALU.add), s)
            dve.wait_ge(S["ga"], 2)
            st.sync()
            st(dve.scalar_tensor_tensor(lf[:], f, 0.0, e[:], ALU.min, ALU.subtract), s)
            st.sync()
            st(dve.tensor_tensor_scan(cum[:], keep[:], lf[:], 0.0, ALU.mult, ALU.add), s)
            st(dve.tensor_tensor_scan(m[:, 0:LP], lf[:, 0:LP], ig[:, 0:LP], 0.0, ALU.add, ALU.max), s)
            for n in range(NB):
                ts = slice(LP + n * NT, LP + (n + 1) * NT)
                st(dve.tensor_tensor_scan(m[:, ts], lf[:, ts], ig[:, ts], m0[:, n:n + 1], ALU.add, ALU.max), s)
            st(dve.memset(mp[:, 0:1], 0.0), s)
            st(dve.tensor_copy(mp[:, NC:NC + NB], m0[:]), s)
            st.sync()
            st(dve.tensor_tensor(rr[:], cum[:], m[:], ALU.subtract), s)
            st(dve.tensor_tensor(cc[:], ig, cum[:], ALU.subtract), s)
            st(dve.tensor_copy(mp[:, 1:NC], m[:, P - 1:LP - P:P]), s)
            st.sync()
            st(dve.tensor_tensor(wi[:, LP:T].rearrange("p (n t) -> p n t", n=NB), rr[:, LP:T].rearrange("p (n t) -> p n t", n=NB),
                                 mp[:, NC:NC + NB].unsqueeze(2).broadcast_to([MH, NB, NT]), ALU.add), s)
            st.sync()
            dve.tensor_tensor(wi[:, 0:LP].rearrange("p (n t) -> p n t", n=NC), rr[:, 0:LP].rearrange("p (n t) -> p n t", n=NC),
                              mp[:, 0:NC].unsqueeze(2).broadcast_to([MH, NC, P]), ALU.add).then_inc(S["gates"], 1)
            dve.wait_ge(S["parts"], 5)
            dve.tensor_tensor(rl[:], rr[:, 0:LP], rh[:].bitcast(F32), ALU.subtract).then_inc(S["parts"], 1)
            dve.tensor_tensor(ml[:], m[:, 0:LP], mh[:].bitcast(F32), ALU.subtract).then_inc(S["parts"], 1)
            dve.wait_ge(S["ct_pe"], 1)
            dve.tensor_copy(ct[:].rearrange("p i h -> p (i h)"), ps[:, 4, 0:(NC + 1) * MH]).then_inc(S["ct"], 1)

            def first(h):
                j, two = h // 2, h % 2
                if two == 0:
                    dve.wait_ge(S["win"], j + 1)
                    if j >= 2:
                        dve.wait_ge(S["nd"], 2 * (h - 2))
                    dve.tensor_copy(dec[:, j, :], ps[:, 7, P - 1:LP:P]).then_inc(S["qw"], 1)
                    dve.tensor_tensor(qw[j % 2][:], ps[:, 7, :], proj[:, j, 0:LP], ALU.mult).then_inc(S["qw"], 1)
                dve.wait_ge(S["w"], h + 1)
                dve.wait_ge(S["s"], h + 1)
                if h >= 2:
                    dve.wait_ge(S["nd"], 2 * (h - 1))
                    dve.wait_ge(S["dc"], h - 1)
                dve.tensor_tensor(at[two][:], ps[:, 1, :], wt[two][:], ALU.mult).then_inc(S["at"], 1)
                dve.wait_ge(S["knat"], j + 1)
                dve.tensor_tensor(ksc[two][:], k_nat[j % 2][:, :, rows(h)],
                                  wt[two][:, P - 1:LP:P].unsqueeze(2).broadcast_to([P, NC, DK]), ALU.mult).then_inc(S["ksc"], 1)

            def states(h):
                j = h // 2
                dve.wait_ge(S["dc"], h + 1)
                dve.wait_ge(S["qw"], 2 * j + 2)
                for i in range(NC):
                    c = (i % 2) * 2 * P
                    src = ps[rows(h), 3 + i // 2, c:c + 2 * P]
                    dst = cn[rows(h), i, :] if i < NC - 1 else cfin[rows(h), j, :]
                    if i == 0:
                        dve.tensor_copy(dst, src).then_inc(S["cn"], 1)
                    else:
                        dve.wait_ge(S["cn"], NC * h + i)
                        dve.scalar_tensor_tensor(dst, cn[rows(h), i - 1, :], dec[rows(h), j, i:i + 1], src, ALU.mult, ALU.add)\
                            .then_inc(S["cn"], 1)

            def second(h):
                dve.wait_ge(S["em"], h + 1)
                dve.wait_ge(S["d2"], h + 1)
                dve.scalar_tensor_tensor(em[:], sqd[:], TINY, em[:], ALU.max, ALU.max).then_inc(S["d"], 1)
                dve.wait_ge(S["d"], h + 1)
                dve.wait_ge(S["msq"], h + 1)
                dve.scalar_tensor_tensor(em[:], ps[:, 6, :], 1.0 / DV, em[:], ALU.mult, ALU.add).then_inc(S["var"], 1)

            def out(h):
                dve.wait_ge(S["og"], h + 1)
                if h >= 2:
                    dve.wait_ge(S["hi"], h - 1)
                    dve.wait_ge(S["lo"], h - 1)
                dve.scalar_tensor_tensor(mo[h % 2][:], ps[:, 5, :], gain[:, h:h + 1], og[:], ALU.mult, ALU.mult)\
                    .then_inc(S["out"], 1)
            first(0)
            states(0)
            for h in range(MH):
                if h + 1 < MH:
                    first(h + 1)
                if h:
                    out(h - 1)
                if h + 1 < MH:
                    states(h + 1)
                second(h)
            out(MH - 1)

        @block.gpsimd
        def _(pool):
            for h in range(MH):
                pool.wait_ge(S["rs"], h + 1)
                pool.wait_ge(S["sig"], h + 1)
                pool.tensor_tensor(og[:], og[:], proj[:, 16 + h, 0:LP], ALU.mult).then_inc(S["og"], 1)
                pool.wait_ge(S["hi"], h + 1)
                pool.tensor_tensor(K.xl[:, h, 0:LP], mo[h % 2][:], K.xh[:, h, 0:LP].bitcast(F32), ALU.subtract)\
                    .then_inc(S["lo"], 1)

    a = Region(nc, K.panels_at + 2 * FH * P * 4)
    wt_s, at_s, tl = (a(f"mls_{x}", [LS, MH, LS]) for x in ("wt", "at", "last"))
    wk = a("mls_wk", [LS, MH])
    k_s, ksc_s = a("mls_k", [LS, 4, 2, DK]), a("mls_ksc", [LS, 2, 4, DK])
    v_s = a("mls_v", [LS, MH, DV])
    vm = [Region(nc, at)(f"mls_vm{at}", [LS, NB, DV]) for at in (gate_at, qw_at)]
    qw_s, qwn = a("mls_qw", [P, 4, NB, NT]), a("mls_qwn", [P, 4, NB, NT])
    qb = [Region(nc, K.odd_scratch - (x + 1) * T * 4)(f"mls_qb{x}", [P, T]) for x in range(2)]
    io = a("mls_io", [2 * LS, 4, DV])
    n0 = a("mls_n0", [P, NB, 4])
    nf = a("mls_nf", [P, NB, 4])
    np_ = a("mls_np", [P, 4])
    dec_s = a("mls_dec", [P, 4, NB])
    num, den, ems, sqs, ogs, os_ = (a(f"mls_{x}", [P, MH, LS]) for x in ("num", "den", "em", "sq", "og", "out"))
    nout, npout = a("mls_nout", [LS, P]), a("mls_npout", [4, P])
    assert a.at <= K.scratch_at, (a.at, K.scratch_at)
    R = {n: sem("mls_" + n) for n in ("b7", "b6", "st", "tr", "n0t", "act", "w_pre", "last_w", "ksc", "vm", "num", "nd", "sq",
                                      "msq", "dc", "dn", "norm", "n_den", "vm_odd", "qb", "qb_zero", "inter", "io", "c_new", "n_new", "nt", "nout", "hi")}

    def by_parity(t, lo, hi):
        return t.rearrange("p (j two) x -> p two j x", two=2)[:, :, :, lo:hi]

    def c_view(h):
        return c0[rows(h)].rearrange("p (n j) v -> p n j v", n=NB)[:, :, h // 2, :]

    def order(h):
        return (h % 2) * 4 + h // 2

    def vmask(eng, two, j, done):
        if j:
            eng.wait_ge(R["dc"], j)
        eng.tensor_tensor(vm[two][:], v_s[:, 2 * j + two, :].unsqueeze(1).broadcast_to([LS, NB, DV]),
                          in_batch[:].unsqueeze(2).broadcast_to([LS, NB, DV]), ALU.mult).then_inc(R[done], 1)

    with nc.Block() as block:
        @block.tensor
        def _(pe):
            for j in range(4):
                pe.matmul(ps[:, 7, j * LS:(j + 1) * LS], selr[:, 2 * j * P + DK:2 * j * P + DK + P].bitcast(F32), wi[:, LP:T],
                          start=True, stop=True)
            for h in range(MH):
                o = P + order(h) * LS
                ins = pe.matmul(ps[:, 7, o:o + LS], sel_of(h), m[:, LP:T], start=True, stop=True)
            ins.then_inc(R["b7"], 1)
            for h in range(MH):
                o = order(h) * LS
                ins = pe.matmul(ps[0:LS, 6, o:o + LS], sel_of(h, LS), rr[:, LP:T], start=True, stop=True)
            ins.then_inc(R["b6"], 1)
            for h in range(MH):
                j = h // 2
                ins = pe.matmul(ps[0:LS, h % 2, j * LS:(j + 1) * LS], proj[rows(h), 4 + j, LP:T], proj[rows(h), j, LP:T],
                                start=True, stop=True)
            ins.then_inc(R["st"], 1)
            for j in range(4):
                pe.transpose(ps[0:LS, 2, j * P:(j + 1) * P], proj[:, 4 + j, LP:T], K.ident)
            for h in range(MH):
                ins = pe.transpose(ps[0:LS, 3 + h // 4, (h % 4) * P:(h % 4 + 1) * P], proj[:, 8 + h, LP:T], K.ident)
            ins.then_inc(R["tr"], 1)
            pe.transpose(ps[:, 5, 0:LS], n0_nat[:], K.ident[0:LS, 0:LS]).then_inc(R["n0t"], 1)
            pe.wait_ge(R["num"], 4)
            pe.wait_ge(R["act"], 5)
            for j in range(4):
                pe.wait_ge(R["qb"], j + 1)
                for n in range(NB):
                    ins = pe.matmul(ps[0:2 * LS, 1, j * DV:(j + 1) * DV], qb[j % 2][:, n * 2 * LS:(n + 1) * 2 * LS],
                                    c0[:, n * 4 + j, :], start=n == 0, stop=n == NB - 1)
                ins.then_inc(R["inter"], 1)
            pe.wait_ge(R["io"], 1)
            for j in range(4):
                pe.transpose(ps[:, 0, j * 2 * LS:(j + 1) * 2 * LS], io[:, j, :], K.ident[0:2 * LS, 0:2 * LS])
            for two in range(2):
                ins = pe.matmul(ps[:, two, 2 * P:3 * P], K.ones[rows(two), :],
                                qwn[rows(two)].rearrange("p j n t -> p (j n t)"), start=True, stop=True)
            ins.then_inc(R["nd"], 1)
            for h in range(MH):
                o = order(h)
                pe.matmul(ps[:, 6, o * LS:(o + 1) * LS], v_s[:, h, :], at_s[:, o, :], start=True, stop=True)
            pe.matmul(ps[:, 6, 2 * P:4 * P], K.ones[0:LS, :], at_s[:].rearrange("p h t -> p (h t)"), start=True, stop=True)\
                .then_inc(R["nd"], 1)
            pe.wait_ge(R["ksc"], 1)
            for h in range(MH):
                j = h // 2
                ins = pe.matmul(ps[rows(h), 7, 3 * P + j * NB:3 * P + (j + 1) * NB], ksc_s[:, h % 2, j, :], in_batch[:],
                                start=True, stop=True)
            ins.then_inc(R["dn"], 1)
            pe.wait_ge(R["n_new"], 1)
            pe.wait_ge(R["hi"], 1)
            pe.transpose(ps[0:LS, 0, 0:P], nf[:].rearrange("p n j -> p (n j)"), K.ident)
            pe.transpose(ps[0:4, 0, P:2 * P], np_[:], K.ident).then_inc(R["nt"], 1)
            pe.wait_ge(R["sq"], 1)
            pe.matmul(ps[:, 1, 0:2 * P], K.ones[:], sqs[:].rearrange("p h t -> p (h t)"), start=True, stop=True)\
                .then_inc(R["msq"], 1)
            for j in range(4):
                pe.wait_ge(R["vm"], j + 1)
                pe.wait_ge(R["vm_odd"], j + 1)
                if j >= 2:
                    pe.wait_ge(R["c_new"], j - 1)
                for two in range(2):
                    for half in range(2):
                        ins = pe.matmul(ps[two * DK:(two + 1) * DK, 2 + 2 * (j % 2) + half, :], ksc_s[:, two, j, :],
                                        vm[two][:, 4 * half:4 * half + 4, :].rearrange("p n v -> p (n v)"),
                                        start=True, stop=True)
                ins.then_inc(R["dc"], 1)

        @block.scalar
        def _(act):
            act.wait_ge(R["num"], 2)
            act.activation(ems[:].rearrange("p h t -> p (h t)"), ps[:, 7, P:3 * P], ACT.Exp, scale=-2.0,
                           bias=ln_eps[:]).then_inc(R["act"], 1)
            act.wait_ge(R["tr"], 1)
            act.copy(k_s[:].rearrange("p j two d -> p (j two d)"), ps[0:LS, 2, :]).then_inc(R["act"], 1)
            act.copy(v_s[:].rearrange("p (a h) d -> p a (h d)", a=2), ps[0:LS, 3:5, :]).then_inc(R["act"], 1)
            act.wait_ge(R["n0t"], 1)
            act.copy(n0[:].rearrange("p n j -> p (n j)"), ps[:, 5, 0:LS]).then_inc(R["act"], 1)
            act.wait_ge(R["w_pre"], 3)
            act.activation(wt_s[:], wt_s[:], ACT.Exp).then_inc(R["act"], 1)
            act.wait_ge(R["inter"], 4)
            act.copy(io[:].rearrange("p j v -> p (j v)"), ps[0:2 * LS, 1, :]).then_inc(R["io"], 1)
            act.wait_ge(R["nd"], 1)
            v = lambda t: t.rearrange("p (two j) x -> p two (j x)", two=2)
            act.copy(num[:].rearrange("p (two j) x -> p two j x", two=2),
                     ps[:, 0, 0:2 * P].rearrange("p (j two x) -> p two j x", j=4, two=2)).then_inc(R["act"], 1)
            act.copy(v(den[:]), ps[:, 0:2, 2 * P:3 * P]).then_inc(R["act"], 1)
            act.wait_ge(R["act"], 7)
            act.copy(np_[:], cfin[:, :, P]).then_inc(R["hi"], 1)
            act.wait_ge(R["norm"], 1)
            act.activation(sqs[:], num[:], ACT.Square).then_inc(R["sq"], 1)
            act.wait_ge(R["norm"], 2)
            act.activation(den[:], den[:], ACT.Square, scale=EPS ** 0.5).then_inc(R["act"], 1)
            act.wait_ge(R["norm"], 3)
            act.activation(ems[:], ems[:], ACT.Ln).then_inc(R["act"], 1)
            act.wait_ge(R["act"], 9)
            act.activation(ems[:], ems[:], ACT.Exp, scale=-0.5).then_inc(R["act"], 1)
            act.wait_ge(R["norm"], 6)
            for two in range(2):
                ins = act.copy(by_parity(K.xh, LP, T)[:, two], os_[:, 4 * two:4 * two + 4, :])
            ins.then_inc(R["hi"], 1)

        @block.vector
        def _(dve):
            dve.wait_ge(R["b7"], 1)
            dve.tensor_copy(dec_s[:], ps[:, 7, 0:P].rearrange("p (j n t) -> p j n t", n=NB, t=NT)[:, :, :, NT - 1])\
                .then_inc(R["num"], 1)
            dve.tensor_tensor(qw_s[:].rearrange("p j n t -> p j (n t)"), ps[:, 7, 0:P].rearrange("p (j t) -> p j t", j=4),
                              proj[:, 0:4, LP:T], ALU.mult).then_inc(R["num"], 1)
            dve.wait_ge(R["b6"], 1)
            o4 = ct[0:LS, NC, :].rearrange("p (j two) -> p two j", two=2)
            for two in range(2):
                dve.tensor_tensor(wt_s[:, 4 * two:4 * two + 4, :], ps[0:LS, 6, two * P:(two + 1) * P].rearrange("p (j t) -> p j t", j=4),
                                  o4[:, two, :].unsqueeze(2).broadcast_to([LS, 4, LS]), ALU.add).then_inc(R["w_pre"], 1)
            dve.wait_ge(R["w_pre"], 2)
            dve.tensor_tensor(wt_s[:], wt_s[:], s_causal[:].unsqueeze(1).broadcast_to([LS, MH, LS]), ALU.add)\
                .then_inc(R["w_pre"], 1)
            dve.wait_ge(R["act"], 5)
            dve.wait_ge(R["num"], 2)
            for j in range(4):
                ins = dve.tensor_tensor(qwn[:, j], qw_s[:, j], n0[:, :, j].unsqueeze(2).broadcast_to([P, NB, NT]), ALU.mult)
            ins.then_inc(R["num"], 1)
            dve.wait_ge(R["st"], 1)
            for two in range(2):
                ins = dve.tensor_tensor(at_s[:, 4 * two:4 * two + 4, :], ps[0:LS, two, 0:P].rearrange("p (j t) -> p j t", j=4),
                                        wt_s[:, 4 * two:4 * two + 4, :], ALU.mult)
            ins.then_inc(R["num"], 1)
            dve.wait_ge(R["act"], 5)
            for j in range(4):
                if j >= 2:
                    dve.wait_ge(R["inter"], j - 1)
                else:
                    dve.wait_ge(R["qb_zero"], j + 1)
                dve.wait_ge(R["num"], 2)
                for two in range(2):
                    q4 = qb[j % 2][rows(two)].rearrange("p (n x) -> p n x", n=NB)[:, :, two * LS:two * LS + NT]
                    ins = dve.tensor_copy(q4, qw_s[rows(two), j])
                ins.then_inc(R["qb"], 1)
            dve.tensor_tensor(tl[:], wt_s[:], s_last[:].unsqueeze(1).broadcast_to([LS, MH, LS]), ALU.mult).then_inc(R["last_w"], 1)
            dve.wait_ge(R["last_w"], 1)
            dve.tensor_reduce(wk[:], tl[:], AX.X, ALU.add).then_inc(R["last_w"], 1)
            dve.wait_ge(R["last_w"], 2)
            for two in range(2):
                ins = dve.tensor_tensor(ksc_s[:, two], k_s[:, :, two, :],
                                        wk[:, 4 * two:4 * two + 4].unsqueeze(2).broadcast_to([LS, 4, DK]), ALU.mult)
            ins.then_inc(R["ksc"], 1)
            vmask(dve, 1, 0, "vm_odd")
            dve.wait_ge(R["nd"], 2)
            dve.wait_ge(R["act"], 7)
            f = lambda t: t[:].rearrange("p h t -> p (h t)")
            dve.tensor_tensor(f(num), ps[:, 6, 0:2 * P], f(num), ALU.add).then_inc(R["norm"], 1)
            dve.tensor_tensor(f(den), ps[:, 6, 2 * P:4 * P], f(den), ALU.add).then_inc(R["norm"], 1)
            dve.wait_ge(R["dn"], 1)
            t = nf[:].rearrange("p n j -> p j n")
            dve.tensor_tensor(t, n0[:].rearrange("p n j -> p j n"), dec_s[:], ALU.mult).then_inc(R["n_den"], 1)
            dve.wait_ge(R["n_den"], 1)
            dve.tensor_tensor(t, ps[:, 7, 3 * P:3 * P + 4 * NB].rearrange("p (j n) -> p j n", j=4), t, ALU.add).then_inc(R["n_new"], 1)
            dve.wait_ge(R["act"], 8)
            dve.scalar_tensor_tensor(f(ems), f(den), TINY, f(ems), ALU.max, ALU.max).then_inc(R["n_den"], 1)
            dve.wait_ge(R["msq"], 1)
            dve.wait_ge(R["n_den"], 2)
            dve.scalar_tensor_tensor(f(ems), ps[:, 1, 0:2 * P], 1.0 / DV, f(ems), ALU.mult, ALU.add).then_inc(R["norm"], 1)
            sg = by_parity(proj[:, 16:24, :], LP, T)
            gv = gain[:].rearrange("p (j two) -> p two j", two=2)
            for two in range(2):
                ins = dve.tensor_tensor(ogs[:, 4 * two:4 * two + 4, :], sg[:, two], gv[:, two, :].unsqueeze(2).broadcast_to([P, 4, LS]),
                                        ALU.mult)
            ins.then_inc(R["norm"], 1)
            dve.wait_ge(R["act"], 10)
            dve.tensor_tensor(os_[:], num[:], ems[:], ALU.mult).then_inc(R["norm"], 1)
            dve.wait_ge(R["norm"], 5)
            dve.tensor_tensor(os_[:], os_[:], ogs[:], ALU.mult).then_inc(R["norm"], 1)
            dve.wait_ge(R["hi"], 2)
            for two in range(2):
                ins = dve.tensor_tensor(by_parity(K.xl, LP, T)[:, two], os_[:, 4 * two:4 * two + 4, :],
                                        by_parity(K.xh, LP, T)[:, two].bitcast(F32), ALU.subtract)
            dve.wait_ge(R["nt"], 1)
            dve.tensor_copy(nout[:], ps[0:LS, 0, 0:P])
            dve.tensor_copy(npout[:], ps[0:4, 0, P:2 * P]).then_inc(R["nout"], 1)
            vmask(dve, 1, 1, "vm_odd")
            for j in range(4):
                dve.wait_ge(R["dc"], j + 1)
                for n in range(NB):
                    c = c0[:, n * 4 + j, :]
                    ins = dve.scalar_tensor_tensor(c, c, dec_s[:, j, n:n + 1],
                                                   ps[:, 2 + 2 * (j % 2) + n // 4, (n % 4) * DV:(n % 4 + 1) * DV],
                                                   ALU.mult, ALU.add)
                ins.then_inc(R["c_new"], 1)
                if j + 2 < 4:
                    vmask(dve, 1, j + 2, "vm_odd")

        @block.gpsimd
        def _(pool):
            for x in range(2):
                pool.memset(qb[x][:], 0.0).then_inc(R["qb_zero"], 1)
            pool.wait_ge(R["act"], 3)
            for j in range(4):
                vmask(pool, 0, j, "vm")

        @block.sync
        def _(sp):
            load_panels(K, sp, K.g_out, plain_dmas(K, I["w_out_odd"][0], DC), 0, 1)
            sp.wait_ge(R["nout"], 1)
            sp.dma_start(O[14][0].rearrange("b (j two) d -> (b j) (two d)", two=2), nout[:]).then_inc(S["out_c"], 16)
            sp.dma_start(O[7][0, 0].rearrange("(j two) d -> j (two d)", two=2), npout[:]).then_inc(S["out_c"], 16)
            cv = O[13][0].rearrange("b (j two) d v -> j (two d) b v", two=2)
            for j in range(4):
                sp.wait_ge(R["c_new"], j + 1)
                sp.dma_start(cv[j], c0[:].rearrange("p (n j) v -> p j n v", j=4)[:, j]).then_inc(S["out_c"], 16)
            sp.wait_ge(S["out_c"], 16 * (MH + 8))


_OUTS = [(1, LP, D), (NB, NT, D),
         (1, 1, WIN, KVH, HD), (1, 1, WIN, KVH, HD), (1, 1, S5G, S5P), (1, 1, S5G, S5P),
         (1, 1, MH, DK, DV), (1, 1, MH, DK), (1, 1, MH),
         (1, NB, WIN, KVH, HD), (1, NB, WIN, KVH, HD), (1, NB, S5G, S5P), (1, NB, S5G, S5P),
         (1, NB, MH, DK, DV), (1, NB, MH, DK), (1, NB, MH)]


def hybrid_step(nc, ins, outs):
    K = Core(nc, ins, outs)
    phase_load(K)
    phase_even_in(K)
    phase_attention(K)
    phase_s5(K)
    phase_out_ffn(K, even_out_dmas(K), 0)
    phase_odd_in(K)
    phase_mlstm(K)
    phase_out_ffn(K, plain_dmas(K, ins["w_out_odd"][0], DC), 1)
    phase_store(K)


def kernel(**inputs):
    import concourse.bacc as bacc
    from concourse.bass_utils import run_bass_kernel_spmd

    nc = bacc.Bacc("TRN2", target_bir_lowering=False, num_devices=1)
    arrays = {f"in_{k}": np.ascontiguousarray(v) for k, v in inputs.items()}
    arrays["in_tables"] = np.concatenate(list(constant_tables().values()), axis=1)
    ins = {k[3:]: nc.dram_tensor(k, v.shape, F32, kind="ExternalInput").ap() for k, v in arrays.items()}
    outs = [nc.dram_tensor(f"out_{i}", s, F32, kind="ExternalOutput").ap() for i, s in enumerate(_OUTS)]
    hybrid_step(nc, ins, outs)
    r = run_bass_kernel_spmd(nc, [arrays], core_ids=[0])
    return tuple(r.results[0][f"out_{i}"] for i in range(len(_OUTS)))
```
